# Optimizing a Trainium2 kernel written in Bass

```python
import math
import jax
import jax.numpy as jnp
from jax import lax
import numpy as np

D_MODEL = 1024
BATCH = 1
SEQ = 512
DEPTH = 2
DEC_BATCH = 8
DEC_SEQ = 8
PAST_LEN = 4096
PAGE_SIZE = 128

D_FF = 2816
EPS = 1e-6
CHUNK = 128
A_GROUPS = 4
A_WIDTH = 512
A_GW = A_WIDTH // A_GROUPS
POOL_WINDOWS = (2, 4, 8, 16)
B_GROUPS = 4
B_WIDTH = 512
B_GW = B_WIDTH // B_GROUPS
POOL_BUF = 15
C_HEADS = 4
C_DQK = 128
C_DV = 256
C_QK_WIDTH = C_HEADS * C_DQK
C_V_WIDTH = C_HEADS * C_DV
MLSTM_CHUNK = 128
N_BRANCH = 3
IN_SPLITS = (A_WIDTH, A_WIDTH, B_WIDTH, C_QK_WIDTH, C_QK_WIDTH, C_V_WIDTH, C_V_WIDTH, C_HEADS, C_HEADS, N_BRANCH * D_MODEL)
IN_COLS = 7688

kernel_name = 'hybrid_gmlp_pool_mlstm_decoder_step'

def rmsnorm(x, g):
    xf = x.astype(jnp.float32)
    y = xf * lax.rsqrt(jnp.mean(xf * xf, axis=-1, keepdims=True) + EPS)
    return (y * g.astype(jnp.float32)).astype(x.dtype)

def layernorm(x, g, b):
    xf = x.astype(jnp.float32)
    mu = jnp.mean(xf, axis=-1, keepdims=True)
    xc = xf - mu
    var = jnp.mean(xc * xc, axis=-1, keepdims=True)
    y = xc * lax.rsqrt(var + EPS) * g.astype(jnp.float32) + b.astype(jnp.float32)
    return y.astype(x.dtype)

def swiglu(x, w_in, w_down):
    gate, up = jnp.split(x @ w_in, 2, axis=-1)
    return (jax.nn.silu(gate) * up) @ w_down

def chunk_mlp_mix(v, w_s, b_s):
    bsz, L, _ = v.shape
    if L <= CHUNK:
        T, n_chunks = L, 1
    else:
        T, n_chunks = CHUNK, -(-L // CHUNK)
    Lp = T * n_chunks
    ws = jnp.tril(w_s[:, :T, :T])
    vp = jnp.pad(v, ((0, 0), (0, Lp - L), (0, 0))).reshape(bsz, n_chunks, T, A_GROUPS, A_GW)
    bias = jnp.swapaxes(b_s[:, :T], 0, 1)[None, None, :, :, None]
    s = jnp.einsum('gts,bcsgd->bctgd', ws, vp) + bias
    return s.reshape(bsz, Lp, A_WIDTH)[:, :L]

def pool_mix(xb, prev, pool_w, pool_scale):
    bsz, L, _ = xb.shape
    if prev is None:
        xcat, n_prev, start = xb, 0, 0
    else:
        xcat = jnp.concatenate([prev.astype(xb.dtype), xb], axis=1)
        n_prev = prev.shape[1]
        start = PAST_LEN - n_prev
    Lc = xcat.shape[1]
    xf = xcat.astype(jnp.float32)
    pos = start + jnp.arange(Lc, dtype=jnp.int32)
    outs = []
    for g, w in enumerate(POOL_WINDOWS):
        xg = xf[..., g * B_GW:(g + 1) * B_GW]
        cs = jnp.cumsum(xg, axis=1)
        lower = jnp.pad(cs[:, :Lc - w], ((0, 0), (w, 0), (0, 0)))
        cnt = jnp.minimum(pos + 1, w).astype(jnp.float32)[None, :, None]
        outs.append((cs - lower) / cnt - xg)
    pooled = jnp.stack(outs, axis=2)[:, n_prev:]
    mixed = jnp.einsum('blgc,gcd->blgd', pooled, pool_w.astype(jnp.float32)).reshape(bsz, L, B_WIDTH)
    out = (mixed * pool_scale.astype(jnp.float32)).astype(xb.dtype)
    return out, xcat[:, Lc - POOL_BUF:]

def mlstm(q, k, v, ig, lf, c0, n0, m0):
    bsz, L = q.shape[0], q.shape[1]
    T = MLSTM_CHUNK if L % MLSTM_CHUNK == 0 else math.gcd(L, MLSTM_CHUNK)
    nc = L // T

    def to_chunks(a):
        return jnp.swapaxes(a.reshape((bsz, nc, T) + a.shape[2:]), 0, 1)

    causal = jnp.tril(jnp.ones((T, T), dtype=bool))

    def step(carry, xs):
        C, n, m = carry
        qc, kc, vc, ic, fc = xs
        b = jnp.cumsum(fc, axis=1)
        a = ic - b
        m_t = b + jnp.maximum(m[:, None], lax.cummax(a, axis=1))
        inter = jnp.exp(b + m[:, None] - m_t)
        bh = jnp.swapaxes(b - m_t, 1, 2)
        ah = jnp.swapaxes(a, 1, 2)
        log_d = bh[..., :, None] + ah[..., None, :]
        d = jnp.exp(jnp.where(causal, log_d, -jnp.inf))
        w = jnp.einsum('bthk,bshk->bhts', qc, kc) * d
        num = jnp.einsum('bhts,bshv->bthv', w, vc) + inter[..., None] * jnp.einsum('bhvk,bthk->bthv', C, qc)
        den = jnp.swapaxes(jnp.sum(w, axis=-1), 1, 2) + inter * jnp.einsum('bhk,bthk->bth', n, qc)
        h = num / jnp.maximum(jnp.abs(den), jnp.exp(-m_t))[..., None]
        m_end = m_t[:, -1]
        decay = jnp.exp(b[:, -1] + m - m_end)
        w_in = jnp.exp(a + (b[:, -1] - m_end)[:, None])
        C_new = decay[..., None, None] * C + jnp.einsum('bsh,bshv,bshk->bhvk', w_in, vc, kc)
        n_new = decay[..., None] * n + jnp.einsum('bsh,bshk->bhk', w_in, kc)
        return (C_new, n_new, m_end), h

    carry0 = (c0.astype(jnp.float32), n0.astype(jnp.float32), m0.astype(jnp.float32))
    xs = (to_chunks(q), to_chunks(k), to_chunks(v), to_chunks(ig), to_chunks(lf))
    (c_f, n_f, m_f), hs = lax.scan(step, carry0, xs)
    h = jnp.swapaxes(hs, 0, 1).reshape(bsz, L, C_HEADS, C_DV)
    return h, c_f, n_f, m_f

def trunk_layer(x, lp, pool_prev, c0, n0, m0):
    bsz, L, _ = x.shape
    f32 = jnp.float32
    x = x + 0.5 * rmsnorm(swiglu(rmsnorm(x, lp['ffn1_norm_pre']), lp['ffn1_w_in'], lp['ffn1_w_down']), lp['ffn1_norm_post'])
    h = rmsnorm(x, lp['mix_norm_pre'])
    z = h @ lp['w_in']
    split_at = [int(i) for i in np.cumsum(IN_SPLITS)[:-1]]
    a_u, a_v, b_in, c_q, c_k, c_v, c_o, c_i, c_f, g_all = jnp.split(z, split_at, axis=-1)
    v_n = layernorm(jax.nn.gelu(a_v), lp['gmlp_ln_g'], lp['gmlp_ln_b'])
    out_a = jax.nn.gelu(a_u) * chunk_mlp_mix(v_n, lp['gmlp_w_s'], lp['gmlp_b_s'])
    out_b, pool_buf = pool_mix(b_in, pool_prev, lp['pool_w'], lp['pool_scale'])
    q = c_q.reshape(bsz, L, C_HEADS, C_DQK).astype(f32)
    k = c_k.reshape(bsz, L, C_HEADS, C_DQK).astype(f32) * (C_DQK ** -0.5)
    v = c_v.reshape(bsz, L, C_HEADS, C_DV).astype(f32)
    ig = c_i.astype(f32) + lp['mlstm_i_bias'].astype(f32)
    lf = jax.nn.log_sigmoid(c_f.astype(f32) + lp['mlstm_f_bias'].astype(f32))
    hc, c_new, n_new, m_new = mlstm(q, k, v, ig, lf, c0, n0, m0)
    hc = hc * lax.rsqrt(jnp.mean(hc * hc, axis=-1, keepdims=True) + EPS) * lp['mlstm_norm_g'].astype(f32).reshape(C_HEADS, C_DV)
    out_c = jax.nn.sigmoid(c_o) * hc.reshape(bsz, L, C_V_WIDTH).astype(x.dtype)
    g_a, g_b, g_c = jnp.split(jax.nn.sigmoid(g_all), N_BRANCH, axis=-1)
    merged = g_a * (out_a @ lp['proj_a']) + g_b * (out_b @ lp['proj_b']) + g_c * (out_c @ lp['proj_c'])
    x = x + rmsnorm(merged @ lp['w_out'], lp['mix_norm_post'])
    x = x + 0.5 * rmsnorm(swiglu(rmsnorm(x, lp['ffn2_norm_pre']), lp['ffn2_w_in'], lp['ffn2_w_down']), lp['ffn2_norm_post'])
    return x, v_n, pool_buf, c_new, n_new, m_new

def setup_inputs(seed: int = 0) -> dict:
    key = jax.random.key(seed)
    keys = jax.random.split(key, 32)
    ks = [keys[i] for i in range(32)]

    def nrm(shape, scale):
        return jax.random.normal(ks.pop(), shape, jnp.float32) * scale

    def gain(shape):
        return 1.0 + nrm(shape, 0.05)

    inp = {}
    inp['x_prompt'] = nrm((BATCH, SEQ, D_MODEL), 1.0)
    inp['x_sample'] = nrm((DEC_BATCH, DEC_SEQ, D_MODEL), 1.0)
    inp['state_pool'] = nrm((DEPTH, DEC_BATCH, POOL_BUF, B_WIDTH), 1.0)
    inp['state_mlstm_C'] = nrm((DEPTH, DEC_BATCH, C_HEADS, C_DV, C_DQK), 0.1)
    inp['state_mlstm_n'] = nrm((DEPTH, DEC_BATCH, C_HEADS, C_DQK), 0.3)
    inp['state_mlstm_m'] = nrm((DEPTH, DEC_BATCH, C_HEADS), 0.5)
    inp['ffn1_norm_pre'] = gain((DEPTH, D_MODEL))
    inp['ffn1_w_in'] = nrm((DEPTH, D_MODEL, 2 * D_FF), D_MODEL ** -0.5)
    inp['ffn1_w_down'] = nrm((DEPTH, D_FF, D_MODEL), D_FF ** -0.5)
    inp['ffn1_norm_post'] = gain((DEPTH, D_MODEL))
    inp['mix_norm_pre'] = gain((DEPTH, D_MODEL))
    inp['w_in'] = nrm((DEPTH, D_MODEL, IN_COLS), D_MODEL ** -0.5)
    inp['gmlp_ln_g'] = gain((DEPTH, A_WIDTH))
    inp['gmlp_ln_b'] = nrm((DEPTH, A_WIDTH), 0.02)
    inp['gmlp_w_s'] = nrm((DEPTH, A_GROUPS, CHUNK, CHUNK), CHUNK ** -0.5)
    inp['gmlp_b_s'] = 1.0 + nrm((DEPTH, A_GROUPS, CHUNK), 0.1)
    inp['pool_w'] = nrm((DEPTH, B_GROUPS, B_GW, B_GW), B_GW ** -0.5)
    inp['pool_scale'] = gain((DEPTH, B_WIDTH))
    inp['mlstm_i_bias'] = nrm((DEPTH, C_HEADS), 0.1)
    inp['mlstm_f_bias'] = 3.0 + nrm((DEPTH, C_HEADS), 0.5)
    inp['mlstm_norm_g'] = gain((DEPTH, C_V_WIDTH))
    inp['proj_a'] = nrm((DEPTH, A_WIDTH, D_MODEL), A_WIDTH ** -0.5)
    inp['proj_b'] = nrm((DEPTH, B_WIDTH, D_MODEL), B_WIDTH ** -0.5)
    inp['proj_c'] = nrm((DEPTH, C_V_WIDTH, D_MODEL), C_V_WIDTH ** -0.5)
    inp['w_out'] = nrm((DEPTH, D_MODEL, D_MODEL), D_MODEL ** -0.5)
    inp['mix_norm_post'] = gain((DEPTH, D_MODEL))
    inp['ffn2_norm_pre'] = gain((DEPTH, D_MODEL))
    inp['ffn2_w_in'] = nrm((DEPTH, D_MODEL, 2 * D_FF), D_MODEL ** -0.5)
    inp['ffn2_w_down'] = nrm((DEPTH, D_FF, D_MODEL), D_FF ** -0.5)
    inp['ffn2_norm_post'] = gain((DEPTH, D_MODEL))
    return inp

def reference(x_prompt, x_sample, state_pool, state_mlstm_C, state_mlstm_n, state_mlstm_m,
              ffn1_norm_pre, ffn1_w_in, ffn1_w_down, ffn1_norm_post,
              mix_norm_pre, w_in, gmlp_ln_g, gmlp_ln_b, gmlp_w_s, gmlp_b_s,
              pool_w, pool_scale, mlstm_i_bias, mlstm_f_bias, mlstm_norm_g,
              proj_a, proj_b, proj_c, w_out, mix_norm_post,
              ffn2_norm_pre, ffn2_w_in, ffn2_w_down, ffn2_norm_post):
    yp, ys = x_prompt, x_sample
    bp = x_prompt.shape[0]
    pool_p, c_p, n_p, m_p = [], [], [], []
    pool_s, c_s, n_s, m_s, v_s = [], [], [], [], []
    for l in range(DEPTH):
        lp = dict(ffn1_norm_pre=ffn1_norm_pre[l], ffn1_w_in=ffn1_w_in[l], ffn1_w_down=ffn1_w_down[l],
                  ffn1_norm_post=ffn1_norm_post[l], mix_norm_pre=mix_norm_pre[l], w_in=w_in[l],
                  gmlp_ln_g=gmlp_ln_g[l], gmlp_ln_b=gmlp_ln_b[l], gmlp_w_s=gmlp_w_s[l], gmlp_b_s=gmlp_b_s[l],
                  pool_w=pool_w[l], pool_scale=pool_scale[l], mlstm_i_bias=mlstm_i_bias[l],
                  mlstm_f_bias=mlstm_f_bias[l], mlstm_norm_g=mlstm_norm_g[l], proj_a=proj_a[l],
                  proj_b=proj_b[l], proj_c=proj_c[l], w_out=w_out[l], mix_norm_post=mix_norm_post[l],
                  ffn2_norm_pre=ffn2_norm_pre[l], ffn2_w_in=ffn2_w_in[l], ffn2_w_down=ffn2_w_down[l],
                  ffn2_norm_post=ffn2_norm_post[l])
        c0 = jnp.zeros((bp, C_HEADS, C_DV, C_DQK), jnp.float32)
        n0 = jnp.zeros((bp, C_HEADS, C_DQK), jnp.float32)
        m0 = jnp.zeros((bp, C_HEADS), jnp.float32)
        yp, _, pb, cf, nf, mf = trunk_layer(yp, lp, None, c0, n0, m0)
        pool_p.append(pb); c_p.append(cf); n_p.append(nf); m_p.append(mf)
        ys, vn, pbs, cfs, nfs, mfs = trunk_layer(ys, lp, state_pool[l], state_mlstm_C[l], state_mlstm_n[l], state_mlstm_m[l])
        pool_s.append(pbs); c_s.append(cfs); n_s.append(nfs); m_s.append(mfs); v_s.append(vn)
    return (yp, ys,
            jnp.stack(pool_p), jnp.stack(c_p), jnp.stack(n_p), jnp.stack(m_p),
            jnp.stack(pool_s), jnp.stack(c_s), jnp.stack(n_s), jnp.stack(m_s), jnp.stack(v_s))


_drawn_inputs = setup_inputs


def setup_inputs(seed=0):
    import zlib

    import numpy as np

    out = dict(_drawn_inputs(seed))
    spreads = {}
    factors = {'gmlp_ln_b': 2.896}
    for name, (base, spread) in spreads.items():
        noise = np.random.default_rng([zlib.crc32(name.encode()), seed]).standard_normal(out[name].shape)
        drawn = base * np.exp(spread * noise) if base else spread * noise
        out[name] = jnp.asarray(drawn.astype(out[name].dtype))
    for name, factor in factors.items():
        out[name] = (out[name] * factor).astype(out[name].dtype)
    return out
```

```python
from contextlib import ExitStack

import concourse.bass as bass
from concourse import mybir

ALU = mybir.AluOpType
ACT = mybir.ActivationFunctionType
AX = mybir.AxisListType
F32 = mybir.dt.float32
F32R = mybir.dt.float32r
I32 = mybir.dt.int32

P = 128
EPS = 1e-6
NEG = -1e30
POOL_WINDOWS = (2, 4, 8, 16)


def trunk_program(nc, a, o):
    DEPTH, D, TWO_FF = a["ffn1_w_in"].shape
    SEQ = a["x_prompt"].shape[1]
    DB, DS = a["x_sample"].shape[0:2]
    NS = DB * DS
    T = SEQ + NS
    H = T // 2
    DF = TWO_FF // 2
    KD = D // P
    FT = DF // P
    AT = a["gmlp_ln_g"].shape[1] // P
    BT = a["pool_scale"].shape[1] // P
    HEADS, DV, DK = a["state_mlstm_C"].shape[2:5]
    CT_ = HEADS * DV // P
    VH = DV // P
    BUF = a["state_pool"].shape[2]
    NC = SEQ // P
    QK_SCALE = float(DK) ** -0.5
    assert D == 8 * P and DK == P and FT % 2 == 0 and AT == BT == HEADS == 4 and CT_ == 8 and NC == 4
    assert NS == 64 and DS == 8

    Z_U, Z_V, Z_B, Z_Q, Z_K, Z_VAL, Z_O = 0, 4, 8, 12, 16, 20, 28
    NZ = 36
    COL_I, COL_F, COL_G = NZ * P, NZ * P + HEADS, NZ * P + 2 * HEADS
    Z_RUNS = [(Z_Q, 16), (Z_V, 4), (Z_U, 4), (Z_B, 4), (Z_O, 8)]
    Z_ORDER = [t0 + i for t0, n in Z_RUNS for i in range(n)]
    HEAD_START = 16

    CHUNKS = [min(8, FT - c) for c in range(0, FT, 8)]
    NCH = len(CHUNKS)
    Q_FFN1 = 0
    Q_DOWN1 = Q_FFN1 + FT
    Q_MIX = Q_DOWN1 + KD * NCH // 2
    Q_GATE = Q_MIX + 1 + NZ // 2
    Q_OUT = Q_GATE + 3 * KD
    Q_FFN2 = Q_OUT + KD // 2
    Q_DOWN2 = Q_FFN2 + FT
    SLOT_USES = Q_DOWN2 + KD * NCH // 2
    PAIRS = 2 * FT + 3 * KD
    G_FFN = (0, FT + 3 * KD)
    G_MIX = FT

    DVE_STEPS = 105

    with ExitStack() as ctx:
        def sem(name):
            return ctx.enter_context(nc.semaphore(name))

        base = (nc.sbuf_base + 63) // 64 * 64
        top = nc.sbuf_usable_end

        def place(name, shape, dt, at):
            size = 4
            for s in shape[1:]:
                size *= s
            assert base <= at and at + size <= top, (name, at, size, top)
            return nc.alloc_sbuf_tensor_at(name, shape, dt, offset=at)

        TB = 4 * T
        X_AT = base
        H_AT = X_AT + KD * TB
        RING_AT = H_AT + 2 * KD * TB
        R_AT = RING_AT + 3 * 2 * KD * P * 4
        TAIL_AT = R_AT + NZ * TB
        R_END = R_AT + 2 * 22 * TB
        C_AT = R_END

        xT = place("xT", [P, KD, T], F32, X_AT)
        h_hi = place("h_hi", [P, KD, T], F32R, H_AT)
        h_lo = place("h_lo", [P, KD, T], F32R, H_AT + KD * TB)
        yT = place("yT", [P, KD, T], F32, H_AT + KD * TB)
        w_raw = place("w_raw", [P, 2, KD, P], F32, RING_AT)
        w_hi = place("w_hi", [P, 2, KD, P], F32R, RING_AT + 2 * KD * P * 4)
        w_lo = place("w_lo", [P, 2, KD, P], F32R, RING_AT + 4 * KD * P * 4)
        act_hi = place("act_hi", [P, FT, T], F32R, R_AT)
        act_lo = place("act_lo", [P, FT, T], F32R, R_AT + FT * TB)
        x_in = place("x_in", [P, NC + 1, D], F32, R_AT)
        z = place("z", [P, NZ, T], F32, R_AT)
        a_hi = place("a_hi", [P, AT, T], F32R, R_AT + Z_V * TB)
        a_lo = place("a_lo", [P, AT, T], F32R, TAIL_AT)
        b_hi = place("b_hi", [P, BT, T], F32R, TAIL_AT + AT * TB)
        b_lo = place("b_lo", [P, BT, T], F32R, R_AT + Z_U * TB)
        c_hi = place("c_hi", [P, CT_, T], F32R, R_AT + Z_Q * TB)
        c_lo = place("c_lo", [P, CT_, T], F32R, R_AT + Z_VAL * TB)
        merged_hi = place("merged_hi", [P, KD, T], F32R, R_AT + Z_O * TB)
        merged_lo0 = place("merged_lo0", [P, KD // 2, T], F32R, R_AT + Z_B * TB)
        rows = [place(n, [HEADS, T], F32, R_AT + (Z_O + i) * TB) for i, n in enumerate(
            ["row_i", "row_f", "row_softplus", "row_lf", "row_b", "row_reset", "row_lf2", "row_i2"])]
        row_i, row_f, row_softplus, row_lf, row_b, row_reset, row_lf2, row_i2 = rows
        row_m = place("row_m", [HEADS, T], F32, R_AT + (Z_O + 1) * TB)

        cursor = [C_AT]

        def small(name, shape, dt=F32):
            n = 4
            for s in shape[1:]:
                n *= s
            t = place(name, shape, dt, cursor[0])
            cursor[0] += (n + 31) // 32 * 32
            return t

        ident = small("ident", [P, P])
        ones = small("ones", [P, P])
        mask_p = small("mask_p", [P, P])
        mask_s = small("mask_s", [NS, NS])
        block01 = small("block01", [NS, DB])
        last01 = small("last01", [NS, DB])
        count_i = small("count_i", [P, 16], I32)
        recip16 = small("recip16", [P, BT, 16])
        rep8 = small("rep8", [DS, NS])
        NGAIN = 6 * KD + BT + CT_
        gains = small("gains", [P, DEPTH * NGAIN])
        gain = small("gain", [P, NGAIN])
        i_bias = small("i_bias", [HEADS, 1])
        f_bias = small("f_bias", [HEADS, 1])
        G_PRE = (0, 2 * KD, 4 * KD)
        G_POST = (KD, 3 * KD, 5 * KD)
        G_POOL, G_HEAD = 6 * KD, 6 * KD + BT
        TMP = cursor[0]

        gate_act = [place(f"gate_act{i}", [P, T], F32, TMP + i * TB) for i in range(2)]
        prod = [place(f"prod{i}", [P, T], F32, TMP + (2 + i) * TB) for i in range(2)]
        sq = [place(f"sq{i}", [P, T], F32, TMP + (4 + i) * TB) for i in range(2)]
        rstd = place("rstd", [P, T], F32, TMP + 6 * TB)
        ss_sum = place("ss_sum", [P, T], F32, TMP + 7 * TB)
        merged_lo1 = place("merged_lo1", [P, KD // 2, T], F32R, TMP + 8 * TB)
        gain_rows = place("gain_rows", [DEPTH * NGAIN, P], F32, TMP)

        cursor[0] = TMP
        VE = DV + 1
        vt = small("vt", [P, HEADS, VE])
        kw = small("kw", [P, HEADS, DK])
        dt_wt = small("dt_wt", [P, 2, HEADS, P])
        dt_, wt = dt_wt[:, 0], dt_wt[:, 1]
        squares = dt_wt.rearrange("p a h t -> p (a h t)").rearrange("p (h v) -> p h v", h=HEADS)
        num = small("num", [P, HEADS, VE])
        state = small("state", [P, HEADS, VE])
        tok_exp = small("tok_exp", [P, NC + 1, 96])
        tok_a = small("tok_a", [P, NC + 1, HEADS])
        decay = small("decay", [P, HEADS, NC + DB])
        row_bm = small("row_bm", [HEADS, T])
        m0 = small("m0", [HEADS, DB])
        m0t = small("m0t", [HEADS, DB])
        mprev = small("mprev", [HEADS, NC + DB])
        dlast = small("dlast", [HEADS, NC + DB])
        hden = small("hden", [P, HEADS])
        hrec = small("hrec", [P, HEADS])
        hss = small("hss", [P, HEADS])
        hvar = small("hvar", [P, HEADS])
        n0 = small("n0", [DB, HEADS * DK])
        n0T = small("n0T", [P, HEADS, DB])
        decay8 = small("decay8", [DB, HEADS])
        qm = small("qm", [P, DB, NS])
        nT_out = small("nT_out", [HEADS, DK])
        kwm = place("kwm", [NS, DB, DK], F32, TMP + ((4 * HEADS * VE + 31) // 32 * 32) * 2 + 3 * 2048)
        gate_q = place("gate_q", [P, T], F32, TMP + (4 * HEADS * VE + 31) // 32 * 32 + 3 * 2048)
        c0 = place("c0", [P, 2, DB, DK], F32, TAIL_AT)
        c0T = place("c0T", [P, DB, VE], F32, TAIL_AT + 2 * DB * DK * 4)
        c_out = place("c_out", [P, HEADS * VH, DK], F32, TAIL_AT)

        cursor[0] = TMP
        ln_gb = small("ln_gb", [P, 2, AT * P])
        ws_raw = small("ws_raw", [P, AT, P])
        wsT = small("wsT", [P, AT, P])
        ws_s = small("ws_s", [NS, AT, NS])
        bs_row = small("bs_row", [1, AT, P])
        vn = small("vn", [P, NC + 1, AT * P])
        ln_stats = small("ln_stats", [P, NC + 1, 6])
        ln_mv = small("ln_mv", [P, NC + 1, 2])
        ln_rstd = small("ln_rstd", [P, NC + 1])
        pool_rows_p = small("pool_rows_p", [BUF, BT * P])
        WID = BUF + SEQ + DB * (BUF + DS)
        cursor[0] = TAIL_AT
        seg = small("seg", [P, WID])
        win_a = small("win_a", [P, WID])
        win_b = small("win_b", [P, WID])
        prev_raw = small("prev_raw", [DB * BUF, BT * P])
        prevT = small("prevT", [P, BT, DB * BUF])
        pooled = small("pooled", [P, T])
        pool_rows_s = small("pool_rows_s", [NS, BT * P])
        pool_w = place("pool_w_sb", [P, BT, P], F32, TMP + 4096)

        ps = ctx.enter_context(nc.psum_tensor("ps", [P, 8, 512], F32))

        def pair(n):
            return ps[:, 2 * n:2 * n + 2, 0:H]

        def halves(t2):
            return t2.rearrange("p (b n) -> p b n", b=2)

        raw = [sem("raw0"), sem("raw1")]
        hi = [sem("hi0"), sem("hi1")]
        lo = [sem("lo0"), sem("lo1")]
        mm = [sem("mm0"), sem("mm1")]
        passed = sem("passed")
        s_const = sem("s_const")
        s_gain_in = sem("s_gain_in")
        s_gain_ps = sem("s_gain_ps")
        s_gains = sem("s_gains")
        s_gain = sem("s_gain")
        s_xin = sem("s_xin")
        s_x_ps = sem("s_x_ps")
        x_new_c = sem("x_chunk")
        s_dve0 = sem("s_dve0")
        st_zero = sem("st_zero")
        vt_ones = sem("vt_ones")
        merge1 = sem("merge1")
        x_new = sem("x_new")
        x_sq = sem("x_sq")
        x_ss = sem("x_ss")
        rs_var = sem("rs_var")
        rs_sqrt = sem("rs_sqrt")
        rs_inv = sem("rs_inv")
        h_f = sem("h_f")
        h_hi_s = sem("h_hi_s")
        h_lo_s = sem("h_lo_s")
        silu_s = sem("silu_s")
        gated = sem("gated")
        act_hi_s = sem("act_hi_s")
        act_lo_s = sem("act_lo_s")
        y_out = sem("y_out")
        ss_zero = sem("ss_zero")
        ss_add = sem("ss_add")
        ss_tot = sem("ss_tot")
        y_scaled = sem("y_scaled")
        z_out = sem("z_out")
        s_bias = sem("s_bias")
        s_m0 = sem("s_m0")
        row_in = sem("row_in")
        row_sp = sem("row_sp")
        row_done = sem("row_done")
        row_decay = sem("row_decay")
        decay_exp = sem("decay_exp")
        decay_ps = sem("decay_ps")
        decay_sb = sem("decay_sb")
        q_ps = sem("q_ps")
        tok_sb = sem("tok_sb")
        m_out = sem("m_out")
        link_a = sem("act_link")
        link_d = sem("dve_link")
        vk_ps = sem("vk_ps")
        vt_sb = sem("vt_sb")
        dt_sb = sem("dt_sb")
        kw_sb = sem("kw_sb")
        qk_ps = sem("qk_ps")
        wt_sb = sem("wt_sb")
        num_ps = sem("num_ps")
        num_sb = sem("num_sb")
        hss_s = sem("hss_s")
        hvar_s = sem("hvar_s")
        hstd_s = sem("hstd_s")
        hc_sb = sem("hc_sb")
        hct_ps = sem("hct_ps")
        hct_sb = sem("hct_sb")
        st_ps = sem("st_ps")
        st_sb = sem("st_sb")
        cT_ps = sem("cT_ps")
        cT_sb = sem("cT_sb")
        c_done = sem("c_done")
        n0_in = sem("n0_in")
        n0_ps = sem("n0_ps")
        qm_sb = sem("qm_sb")
        c0_in = [sem("c0_in0"), sem("c0_in1")]
        c0T_ps = sem("c0T_ps")
        c0T_sb = sem("c0T_sb")
        kwm_sb = sem("kwm_sb")
        cu_ps = sem("cu_ps")
        cu_sb = sem("cu_sb")
        c0_done = [sem("c0_done0"), sem("c0_done1")]
        nu_ps = sem("nu_ps")
        nu_sb = sem("nu_sb")
        n_done = sem("n_done")
        a_in = sem("a_in")
        ws_ps = sem("ws_ps")
        wsT_s = sem("wsT_s")
        wss_ps = sem("wss_ps")
        av_ps = sem("av_ps")
        av_sb = sem("av_sb")
        u_gelu = sem("u_gelu")
        ln_var = sem("ln_var")
        ln_std = sem("ln_std")
        vn_sb = sem("vn_sb")
        vn_done = sem("vn_done")
        mix_ps = sem("mix_ps")
        a_sb = sem("a_sb")
        prev_in = sem("prev_in")
        pw_in = sem("pw_in")
        prev_ps = sem("prev_ps")
        prev_sb = sem("prev_sb")
        prow_ps = sem("prow_ps")
        prow_sb = sem("prow_sb")
        prow_done = sem("prow_done")
        prev_done = sem("prev_done")
        seg_sb = sem("seg_sb")
        pooled_s = sem("pooled_s")
        pmix_ps = sem("pmix_ps")
        b_sb = sem("b_sb")
        a_hi_s = sem("a_hi_s")
        a_lo_s = sem("a_lo_s")
        b_hi_s = sem("b_hi_s")
        b_lo_s = sem("b_lo_s")
        o_sig = sem("o_sig")
        c_sb = sem("c_sb")
        c_hi_s = sem("c_hi_s")
        c_lo_s = sem("c_lo_s")
        sig_s = sem("sig_s")
        merged_s = sem("merged_s")
        merged_hi_s = sem("merged_hi_s")
        merged_lo_s = sem("merged_lo_s")
        xo_ps = sem("xo_ps")
        xo_sb = sem("xo_sb")
        xo_done = sem("xo_done")

        def cols(w, l, k0, kt, c0_, n=P):
            return w[bass.ds(l, 1), k0 * P:(k0 + kt) * P, bass.ds(c0_, n)].rearrange("a (k p) n -> p (a k) n", p=P)

        def tokens(ch):
            return (ch * P, P) if ch < NC else (SEQ, NS)

        bank = lambda i: ps[:, i, :]

        def apart(eng):
            eng.sem_inc(passed, 1)

        ctx.enter_context(nc.allow_non_contiguous_dma(reason="a few small transfers: gate biases, m, state rows"))
        block = ctx.enter_context(nc.Block())

        @block.sync
        def _(sp):
            def load(j, q, kt, src, n=P):
                sp.wait_ge(lo[j], q + 1)
                sp.dma_start(w_raw[:, j, 0:kt, 0:n], src).then_inc(raw[j], 16)

            def ffn(l, w_in, w_down, q0):
                with sp.Fori(0, FT) as m:
                    load(0, q0 + m, KD, cols(w_in, l, 0, KD, m * P))
                    load(1, q0 + m, KD, cols(w_in, l, 0, KD, DF + m * P))
                with sp.Fori(0, KD // 2) as i:
                    for n in range(2 * NCH):
                        m2, c = n // NCH, n % NCH
                        load(n % 2, q0 + FT + i * NCH + n // 2, CHUNKS[c],
                             cols(w_down, l, 8 * c, CHUNKS[c], i * 2 * P + m2 * P))

            with sp.Fori(0, DEPTH) as l:
                q0 = l * SLOT_USES
                ffn(l, a["ffn1_w_in"], a["ffn1_w_down"], q0 + Q_FFN1)
                load(0, q0 + Q_MIX, KD, cols(a["w_in"], l, 0, KD, COL_I, HEADS), HEADS)
                load(1, q0 + Q_MIX, KD, cols(a["w_in"], l, 0, KD, COL_F, HEADS), HEADS)
                n0_ = 0
                for t0, cnt in Z_RUNS:
                    with sp.Fori(0, cnt // 2) as i:
                        for j in range(2):
                            load(j, q0 + Q_MIX + 1 + n0_ // 2 + i, KD,
                                 cols(a["w_in"], l, 0, KD, (t0 + j) * P + i * 2 * P))
                    n0_ += cnt
                with sp.Fori(0, KD) as m:
                    for br, (w, kt) in enumerate((("proj_a", AT), ("proj_b", BT), ("proj_c", CT_))):
                        q = q0 + Q_GATE + 3 * m + br
                        load(0, q, KD, cols(a["w_in"], l, 0, KD, COL_G + br * D + m * P))
                        load(1, q, kt, cols(a[w], l, 0, kt, m * P))
                with sp.Fori(0, KD // 2) as i:
                    for j in range(2):
                        load(j, q0 + Q_OUT + i, KD, cols(a["w_out"], l, 0, KD, i * 2 * P + j * P))
                ffn(l, a["ffn2_w_in"], a["ffn2_w_down"], q0 + Q_FFN2)

        @block.gpsimd
        def _(pool):
            pool.memset(ident[:, :], 0.0).then_inc(s_const, 1)
            pool.memset(ones[:, :], 1.0).then_inc(s_const, 1)
            pool.memset(mask_p[:, :], 0.0).then_inc(s_const, 1)
            pool.memset(mask_s[:, :], 0.0).then_inc(s_const, 1)
            pool.memset(block01[:, :], 1.0).then_inc(s_const, 1)
            pool.memset(last01[:, :], 0.0).then_inc(s_const, 1)
            pool.memset(w_raw[:, 0, :, :], 0.0).then_inc(lo[0], 1)
            pool.memset(w_raw[:, 1, :, :], 0.0).then_inc(lo[1], 1)
            pool.memset(w_hi[:, 0, :, :].bitcast(F32), 0.0).then_inc(mm[0], 1)
            pool.memset(w_hi[:, 1, :, :].bitcast(F32), 0.0).then_inc(mm[1], 1)
            pool.memset(w_lo[:, :, :, :].bitcast(F32), 0.0).then_inc(s_const, 1)
            pool.iota(count_i[:, :], pattern=[[1, 16]], base=1, channel_multiplier=0).then_inc(s_const, 1)
            pool.wait_ge(s_const, 8)
            pool.affine_select(out=ident[:, :], in_=ident[:, :], compare_op=ALU.not_equal, fill=1.0, base=0,
                               pattern=[[-1, P]], channel_multiplier=1).then_inc(s_const, 1)
            pool.affine_select(out=mask_p[:, :], in_=mask_p[:, :], compare_op=ALU.is_ge, fill=NEG, base=0,
                               pattern=[[1, P]], channel_multiplier=-1).then_inc(s_const, 1)
            pool.affine_select(out=mask_s[:, :], in_=mask_s[:, :], compare_op=ALU.is_ge, fill=NEG, base=0,
                               pattern=[[1, NS]], channel_multiplier=-1).then_inc(s_const, 1)
            pool.affine_select(out=block01[:, :], in_=block01[:, :], compare_op=ALU.is_ge, fill=0.0, base=0,
                               pattern=[[-DS, DB]], channel_multiplier=1).then_inc(s_const, 1)
            pool.affine_select(out=last01[:, :], in_=last01[:, :], compare_op=ALU.not_equal, fill=1.0,
                               base=1 - DS, pattern=[[-DS, DB]], channel_multiplier=1).then_inc(s_const, 1)
            pool.wait_ge(s_const, 13)
            m3 = mask_s[:, :].rearrange("p (b t) -> p b t", b=DB)
            pool.affine_select(out=m3, in_=m3, compare_op=ALU.is_ge, fill=NEG, base=0,
                               pattern=[[-DS, DB], [0, DS]], channel_multiplier=1).then_inc(s_const, 1)
            pool.affine_select(out=block01[:, :], in_=block01[:, :], compare_op=ALU.is_ge, fill=0.0, base=DS - 1,
                               pattern=[[DS, DB]], channel_multiplier=-1).then_inc(s_const, 1)

            def lo_part(j, q, kt, n=P):
                pool.wait_ge(hi[j], q + 1)
                pool.tensor_tensor(w_lo[:, j, 0:kt, 0:n], w_raw[:, j, 0:kt, 0:n],
                                   w_hi[:, j, 0:kt, 0:n].bitcast(F32), ALU.subtract).then_inc(lo[j], 1)

            def ffn(q0):
                with pool.Fori(0, FT) as m:
                    lo_part(0, q0 + m, KD)
                    lo_part(1, q0 + m, KD)
                with pool.Fori(0, KD // 2) as i:
                    for n in range(2 * NCH):
                        lo_part(n % 2, q0 + FT + i * NCH + n // 2, CHUNKS[n % NCH])

            with pool.Fori(0, DEPTH) as l:
                q0 = l * SLOT_USES
                ffn(q0 + Q_FFN1)
                lo_part(0, q0 + Q_MIX, KD, HEADS)
                lo_part(1, q0 + Q_MIX, KD, HEADS)
                with pool.Fori(0, NZ // 2) as i:
                    for j in range(2):
                        lo_part(j, q0 + Q_MIX + 1 + i, KD)
                with pool.Fori(0, KD) as m:
                    for br, kt in enumerate((AT, BT, CT_)):
                        lo_part(0, q0 + Q_GATE + 3 * m + br, KD)
                        lo_part(1, q0 + Q_GATE + 3 * m + br, kt)
                with pool.Fori(0, KD // 2) as i:
                    for j in range(2):
                        lo_part(j, q0 + Q_OUT + i, KD)
                ffn(q0 + Q_FFN2)

        @block.tensor
        def _(pe):
            def transpose(out, in_, n):
                return pe.transpose(out, in_, ident[0:n, 0:n])

            def unit(j, q, kt, n_ps, rhs_hi, rhs_lo, k0=0, first=True, last=True):
                pe.wait_ge(lo[j], q + 2)
                for k in range(kt):
                    for part, (w, r) in enumerate(((w_hi, rhs_hi), (w_hi, rhs_lo), (w_lo, rhs_hi))):
                        for b in range(2):
                            ins = pe.matmul(ps[:, 2 * n_ps + b, 0:H], w[:, j, k, :],
                                            r(k0 + k)[:, b * H:(b + 1) * H],
                                            start=first and k == 0 and part == 0,
                                            stop=last and k == kt - 1 and part == 2)
                ins.then_inc(mm[j], 1)

            hh = lambda k: h_hi[:, k, :]
            hl = lambda k: h_lo[:, k, :]

            def sum_rows(n_ps, src, start, stop):
                for b in range(2):
                    ins = pe.matmul(ps[:, 2 * n_ps + b, 0:H], ones[:, :], src[:, b * H:(b + 1) * H],
                                    start=start, stop=stop)
                return ins

            def pre_norm(l, s):
                nb = l * 3 + s
                for k in range(KD):
                    pe.wait_ge(x_sq, nb * KD + k + 1)
                    sum_rows(3, sq[k % 2][:, :], k == 0, k == KD - 1).then_inc(x_ss, 1)

            def post_norm(l, s):
                pe.wait_ge(ss_add, (l * 3 + s) * KD + KD + 2)
                sum_rows(2, ss_sum[:, :], True, True).then_inc(ss_tot, 1)

            def out_tiles(l, s, q0, chunks, rhs_hi, rhs_lo):
                n_ch = len(chunks)
                with pe.Fori(0, KD // 2) as i:
                    for m2 in range(2):
                        pe.wait_ge(y_out, (l * 3 + s) * KD + 2 * i + m2 + 1)
                        for c in range(n_ch):
                            n = m2 * n_ch + c
                            unit(n % 2, q0 + i * n_ch + n // 2, chunks[c], m2, rhs_hi, rhs_lo, 8 * c,
                                 c == 0, c == n_ch - 1)

            def ffn(l, f, q0):
                s = 2 * f
                pe.wait_ge(h_lo_s, (l * 3 + s) * KD + KD)
                apart(pe)
                with pe.Fori(0, FT // 2) as i:
                    for m2 in range(2):
                        pe.wait_ge(gated, l * PAIRS + G_FFN[f] + 2 * i + m2 + 1)
                        for j in range(2):
                            unit(j, q0 + 2 * i + m2, KD, 2 * m2 + j, hh, hl)
                pe.wait_ge(act_lo_s, (l * 2 + f + 1) * FT)
                apart(pe)
                out_tiles(l, s, q0 + FT, CHUNKS, lambda k: act_hi[:, k, :], lambda k: act_lo[:, k, :])

            pe.wait_ge(s_const, 15)
            pe.wait_ge(s_gain_in, 16 * 8 * DEPTH)
            NG = DEPTH * NGAIN
            transpose(bank(7)[:, 0:NG], gain_rows[:, :], NG).then_inc(s_gain_ps, 1)
            for ch in range(NC + 1):
                _, n = tokens(ch)
                pe.wait_ge(s_xin, 16 * (NC + 1))
                for k in range(KD):
                    if ch >= 3:
                        pe.wait_ge(x_new_c, ch - 2)
                    ins = transpose(ps[:, 2 * (ch % 3) + k // 4, (k % 4) * P:(k % 4) * P + n],
                                    x_in[0:n, ch, k * P:(k + 1) * P], n)
                ins.then_inc(s_x_ps, 1)

            with pe.Fori(0, DEPTH) as l:
                q0 = l * SLOT_USES
                pre_norm(l, 0)
                ffn(l, 0, q0 + Q_FFN1)
                post_norm(l, 0)
                pre_norm(l, 1)

                pe.wait_ge(h_lo_s, (l * 3 + 1) * KD + KD)
                unit(0, q0 + Q_MIX, KD, 2, hh, hl)
                unit(1, q0 + Q_MIX, KD, 3, hh, hl)

                def z_tile(n, i=0):
                    pe.wait_ge(z_out, l * NZ + n + 2 * i + 1)
                    unit(n % 2, q0 + Q_MIX + 1 + n // 2 + i, KD, n % 2, hh, hl)

                with pe.Fori(0, HEAD_START // 4) as i:
                    z_tile(0, i)
                    z_tile(1, i)
                pe.wait_ge(decay_exp, l + 1)
                for h in range(HEADS):
                    ins = pe.matmul(ps[:, 6, h * (NC + DB):(h + 1) * (NC + DB)],
                                    ident[0:HEADS, h:h + 1].broadcast_to([HEADS, P]), dlast[:, :],
                                    start=h == 0, stop=h == HEADS - 1, skip_group_check=True)
                ins.then_inc(decay_ps, 1)
                pe.wait_ge(row_done, l + 1)
                for ch in range(NC + 1):
                    t0, n = tokens(ch)
                    ins = transpose(ps[0:n, 4 + ch // 4, (ch % 4) * P:(ch % 4 + 1) * P], gate_q[:, t0:t0 + n], P)
                ins.then_inc(q_ps, 1)
                with pe.Fori(HEAD_START // 4, HEAD_START // 2) as i:
                    z_tile(0, i)
                    z_tile(1, i)

                zn = HEAD_START
                for ch in range(NC + 1):
                    t0, n = tokens(ch)
                    cc = l * (NC + 1) + ch
                    sample = ch == NC
                    if ch == 0:
                        pe.wait_ge(z_out, l * NZ + HEAD_START + 2)
                        pe.wait_ge(tok_sb, l + 1)
                        pe.wait_ge(decay_sb, l + 1)
                    if ch > 0:
                        pe.wait_ge(hct_sb, cc)
                    apart(pe)
                    for i in range(CT_):
                        transpose(ps[0:n, 4 + i // 4, (i % 4) * P:(i % 4 + 1) * P], z[:, Z_VAL + i, t0:t0 + n], P)
                    for i in range(HEADS):
                        transpose(ps[0:n, 6, i * P:(i + 1) * P], z[:, Z_K + i, t0:t0 + n], P)
                    mask = mask_s if sample else mask_p
                    for h in range(HEADS):
                        pe.matmul(ps[0:n, 7, h * n:(h + 1) * n], ident[0:n, 0:n], mask[:, :], start=h == 0,
                                  stop=False, skip_group_check=True)
                    for h in range(HEADS):
                        ins = pe.matmul(ps[0:n, 7, h * n:(h + 1) * n],
                                        ident[0:HEADS, h:h + 1].broadcast_to([HEADS, n]), row_bm[:, t0:t0 + n],
                                        start=False, stop=h == HEADS - 1, skip_group_check=True)
                    ins.then_inc(vk_ps, 1)
                    if not sample:
                        z_tile(zn)
                        zn += 1
                    pe.wait_ge(vt_sb, cc + 1)
                    apart(pe)
                    for h in range(HEADS):
                        ins = pe.matmul(ps[0:n, 4, h * n:(h + 1) * n], z[:, Z_K + h, t0:t0 + n],
                                        z[:, Z_Q + h, t0:t0 + n], start=h == 0, stop=h == HEADS - 1,
                                        skip_group_check=True)
                    ins.then_inc(qk_ps, 1)
                    z_tile(zn)
                    zn += 1
                    pe.wait_ge(wt_sb, cc + 1)
                    pe.wait_ge(kw_sb, cc + 1)
                    pe.wait_ge(dt_sb, cc + 1)
                    if not sample:
                        if ch > 0:
                            pe.wait_ge(st_sb, l * NC + ch)
                        else:
                            pe.wait_ge(st_zero, l + 1)
                        for r in range(2):
                            if r:
                                pe.wait_ge(num_sb, l * (2 * NC + HEADS) + 2 * ch + 1)
                            for h2 in range(2):
                                h = 2 * r + h2
                                pe.matmul(ps[0:n, 4 + h2, 0:VE], wt[0:n, h, 0:n], vt[0:n, h, :], start=True, stop=True)
                                ins = pe.matmul(ps[0:n, 6 + h2, 0:VE], z[:, Z_Q + h, t0:t0 + n], state[:, h, :],
                                                start=True, stop=True)
                            ins.then_inc(num_ps, 1)
                        pe.wait_ge(num_sb, l * (2 * NC + HEADS) + 2 * ch + 2)
                        for h in range(HEADS):
                            ins = pe.matmul(ps[:, 4 + h, 0:VE], kw[:, h, :], vt[:, h, :], start=True, stop=True)
                        ins.then_inc(st_ps, 1)
                        z_tile(zn)
                        zn += 1
                        pe.wait_ge(st_sb, l * NC + ch + 1)
                    else:
                        for i in range(HEADS * VH):
                            h, vh = i // VH, i % VH
                            transpose(ps[:, 4 + i // 4, (i % 4) * P:(i % 4 + 1) * P],
                                      state[:, h, vh * P:(vh + 1) * P], P)
                        for_n = ps[0:HEADS, 6, 0:P]
                        transpose(for_n, state[:, :, DV:DV + 1].rearrange("p h o -> p (h o)"), P).then_inc(cT_ps, 1)
                        pe.wait_ge(cT_sb, l + 1)
                        pe.wait_ge(n0_in, 16 * (l + 1))
                        apart(pe)
                        for h in range(HEADS):
                            transpose(ps[:, 6, h * DB:(h + 1) * DB], n0[:, h * DK:(h + 1) * DK], DB)
                        pe.matmul(ps[0:DB, 5, 0:HEADS], last01[:, :], tok_exp[0:NS, NC, 0:HEADS], start=True, stop=True)
                        pe.matmul(ps[0:DB, 4, 0:HEADS * DK], block01[:, :], kw[0:NS, :, :], start=True, stop=True)\
                            .then_inc(n0_ps, 1)
                        pe.wait_ge(nu_sb, l + 1)
                        for h in range(HEADS):
                            hh_ = l * HEADS + h
                            for vh in range(VH):
                                u = hh_ * VH + vh
                                pe.wait_ge(c0_in[vh], 16 * (hh_ + 1))
                                if vh or h:
                                    pe.wait_ge(c0T_sb if vh else cu_sb, u)
                                for b in range(DB):
                                    ins = transpose(ps[:, 4 + b // 4, (b % 4) * P:(b % 4 + 1) * P], c0[:, vh, b, :], P)
                                ins.then_inc(c0T_ps, 1)
                            if h:
                                pe.wait_ge(num_sb, l * (2 * NC + HEADS) + 2 * NC + h)
                            apart(pe)
                            pe.matmul(ps[0:n, 6, 0:VE], wt[0:n, h, 0:n], vt[0:n, h, :], start=True, stop=True)
                            pe.wait_ge(c0T_sb, (hh_ + 1) * VH)
                            pe.wait_ge(qm_sb, hh_ + 1)
                            for b in range(DB):
                                ins = pe.matmul(ps[0:n, 7, 0:VE], qm[:, b, :], c0T[:, b, :], start=b == 0, stop=b == DB - 1)
                            ins.then_inc(num_ps, 1)
                            pe.wait_ge(kwm_sb, hh_ + 1)
                            for vh in range(VH):
                                u = hh_ * VH + vh
                                if vh:
                                    pe.wait_ge(cu_sb, u)
                                for b in range(2):
                                    ins = pe.matmul(ps[:, 4 + b, :], vt[0:n, h, vh * P:(vh + 1) * P],
                                                    kwm[:, b * (DB // 2):(b + 1) * (DB // 2), :], start=True, stop=True)
                                ins.then_inc(cu_ps, 1)
                        z_tile(zn)
                        zn += 1
                    pe.wait_ge(hc_sb, cc + 1)
                    if sample:
                        pe.wait_ge(cu_sb, (l + 1) * HEADS * VH)
                    apart(pe)
                    for i in range(CT_):
                        ins = transpose(ps[:, 4 + i // 4, (i % 4) * n:(i % 4 + 1) * n],
                                        num[0:n, i // VH, (i % VH) * P:(i % VH + 1) * P], n)
                    ins.then_inc(hct_ps, 1)

                pe.wait_ge(a_in, 16 * 4 * (l + 1))
                pe.wait_ge(hct_sb, (l + 1) * (NC + 1))
                for g in range(AT):
                    ins = transpose(ps[:, 6, g * P:(g + 1) * P], ws_raw[:, g, :], P)
                ins.then_inc(ws_ps, 1)
                for ch in range(NC + 1):
                    t0, n = tokens(ch)
                    bk = (4, 5, 4, 5, 7)[ch]
                    if ch in (2, 3):
                        pe.wait_ge(av_sb, l * (NC + 1) + ch - 1)
                    for g in range(AT):
                        ins = transpose(ps[0:n, bk, g * P:(g + 1) * P], z[:, Z_V + g, t0:t0 + n], P)
                    ins.then_inc(av_ps, 1)
                pe.wait_ge(wsT_s, l + 1)
                pe.matmul(ps[0:NS, 6, 0:AT * DS], rep8[:, :], wsT[0:DS, :, 0:DS], start=True, stop=True)\
                    .then_inc(wss_ps, 1)
                while zn < NZ:
                    z_tile(zn)
                    zn += 1
                for ch in range(NC + 1):
                    t0, n = tokens(ch)
                    cc = l * (NC + 1) + ch
                    bk = 4 + ch % 2
                    pe.wait_ge(vn_sb, cc + 1)
                    if ch >= 2:
                        pe.wait_ge(a_sb, cc - 1)
                    for g in range(AT):
                        out = ps[:, bk, g * n:(g + 1) * n]
                        if ch < NC:
                            bias, weights = bs_row[0:1, g, :], wsT[:, g, :]
                        else:
                            bias, weights = bs_row[0:1, g:g + 1, 0:DS].broadcast_to([1, DB, DS]), ws_s[:, g, :]
                            out_b = out.rearrange("p (b t) -> p b t", b=DB)
                        pe.matmul(out if ch < NC else out_b, ones[0:1, :], bias, start=g == 0, stop=False,
                                  skip_group_check=True)
                        ins = pe.matmul(out, vn[0:n, ch, g * P:(g + 1) * P], weights, start=False,
                                        stop=g == AT - 1, skip_group_check=True)
                    ins.then_inc(mix_ps, 1)

                pe.wait_ge(prev_in, 16 * (l + 1))
                apart(pe)
                NPREV = DB * BUF
                pe.wait_ge(z_out, l * NZ + NZ + 2)
                for g in range(BT):
                    transpose(ps[:, 6, g * NPREV:(g + 1) * NPREV], prev_raw[:, g * P:(g + 1) * P], NPREV)
                for g in range(BT):
                    transpose(ps[0:BUF, 7, g * P:(g + 1) * P], z[:, Z_B + g, SEQ - BUF:SEQ], P)
                for g in range(BT):
                    ins = transpose(ps[0:NS, 0, g * P:(g + 1) * P], z[:, Z_B + g, SEQ:T], P)
                ins.then_inc(prow_ps, 1)
                pe.wait_ge(pw_in, 16 * (l + 1))
                pe.wait_ge(prow_sb, l + 1)
                for g in range(BT):
                    gg = l * BT + g
                    pe.wait_ge(pooled_s, gg + 1)
                    for b in range(2):
                        ins = pe.matmul(ps[:, 6 + b, 0:H], pool_w[:, g, :], pooled[:, b * H:(b + 1) * H],
                                        start=True, stop=True)
                    ins.then_inc(pmix_ps, 1)
                    pe.wait_ge(b_sb, gg + 1)

                pe.wait_ge(a_lo_s, l + 1)
                pe.wait_ge(b_lo_s, l + 1)
                pe.wait_ge(c_lo_s, (l + 1) * CT_)
                apart(pe)
                branches = ((a_hi, a_lo, AT), (b_hi, b_lo, BT), (c_hi, c_lo, CT_))
                with pe.Fori(0, KD // 2) as i:
                    for m2 in range(2):
                        for br, (bh, bl, kt) in enumerate(branches):
                            n = 3 * m2 + br
                            pe.wait_ge(gated, l * PAIRS + G_MIX + 6 * i + n + 1)
                            q = q0 + Q_GATE + 6 * i + n
                            unit(0, q, KD, 2 * (n % 2), hh, hl)
                            unit(1, q, kt, 2 * (n % 2) + 1, lambda k: bh[:, k, :], lambda k: bl[:, k, :])
                pe.wait_ge(merged_lo_s, (l + 1) * KD)
                apart(pe)
                out_tiles(l, 1, q0 + Q_OUT, [KD], lambda k: merged_hi[:, k, :],
                          lambda k: (merged_lo0 if k < KD // 2 else merged_lo1)[:, k % (KD // 2), :])
                post_norm(l, 1)
                pre_norm(l, 2)
                ffn(l, 1, q0 + Q_FFN2)
                post_norm(l, 2)

            pe.wait_ge(x_new, (DEPTH * 3 + 1) * KD)
            for ch in range(NC + 1):
                t0, n = tokens(ch)
                if ch >= 3:
                    pe.wait_ge(xo_sb, ch - 2)
                for k in range(KD):
                    ins = transpose(ps[0:n, 2 * (ch % 3) + k // 4, (k % 4) * P:(k % 4 + 1) * P],
                                    xT[:, k, t0:t0 + n], P)
                ins.then_inc(xo_ps, 1)

        @block.scalar
        def _(act):
            act_steps = 2

            class Link:
                def __init__(self, l):
                    self.base, self.n = l * act_steps, 0

                def __call__(self, ins):
                    self.n += 1
                    ins.then_inc(link_a, 1)
                    act.wait_ge(link_a, self.base + self.n)

            def pre_norm(l, s):
                nb = l * 3 + s
                for k in range(KD):
                    act.wait_ge(x_new, nb * KD + k + 1)
                    if k >= 2:
                        act.wait_ge(x_ss, nb * KD + k - 1)
                    act.activation(sq[k % 2][:, :], xT[:, k, :], ACT.Square).then_inc(x_sq, 1)
                root(2 * nb)
                for k in range(KD):
                    act.wait_ge(h_f, nb * KD + k + 1)
                    act.activation(h_hi[:, k, :], prod[k % 2][:, :], ACT.Copy).then_inc(h_hi_s, 1)

            def hi_part(j, q):
                act.wait_ge(raw[j], (q + 1) * 16)
                act.wait_ge(mm[j], q + 1)
                act.activation(w_hi[:, j, :, :], w_raw[:, j, :, :], ACT.Copy).then_inc(hi[j], 1)

            def root(ri):
                act.wait_ge(rs_var, ri + 1)
                act.activation(rstd[:, :], rstd[:, :], ACT.Sqrt).then_inc(rs_sqrt, 1)

            def out_tiles(l, s, q0, n_ch):
                yb = (l * 3 + s) * KD

                def two_tiles(i, left):
                    for m2 in range(2):
                        for c in range(n_ch):
                            n = m2 * n_ch + c
                            if n < left:
                                hi_part(n % 2, q0 + i * n_ch + n // 2 + 1)
                        act.wait_ge(mm[n % 2], q0 + i * n_ch + n // 2 + 2)
                        act.activation(yT[:, bass.ds(2 * i + m2, 1), :].rearrange("p a (b n) -> p (a b) n", b=2),
                                       pair(m2), ACT.Copy)
                        act.wait_ge(ss_add, yb + 2 * i + m2 + 1)
                        act.activation(halves(sq[m2][:, :]), pair(m2), ACT.Square).then_inc(y_out, 1)

                whole = KD // 2 if s < 2 else KD // 2 - 1
                with act.Fori(0, whole) as i:
                    two_tiles(i, 2 * n_ch)
                if s == 2:
                    two_tiles(whole, 2 * n_ch - 2)

            def ffn(l, f, q0):
                with act.Fori(0, FT // 2) as i:
                    for m2 in range(2):
                        pg = l * PAIRS + G_FFN[f] + 2 * i + m2
                        hi_part(0, q0 + 2 * i + m2 + 1)
                        hi_part(1, q0 + 2 * i + m2 + 1)
                        act.wait_ge(gated, pg + 1)
                        act.activation(halves(gate_act[m2][:, :]), pair(2 * m2), ACT.Silu).then_inc(silu_s, 1)
                        act.wait_ge(gated, pg + 3)
                        act.activation(act_hi[:, bass.ds(2 * i + m2, 1), :].rearrange("p a n -> p (a n)"),
                                       prod[m2][:, :], ACT.Copy).then_inc(act_hi_s, 1)
                out_tiles(l, 2 * f, q0 + FT, NCH)

            for ch in range(NC + 1):
                t0, n = tokens(ch)
                src = a["x_prompt"][0, t0:t0 + n, :] if ch < NC else a["x_sample"].rearrange("b t d -> (b t) d")
                act.dma_start(x_in[0:n, ch, :], src).then_inc(s_xin, 16)
            kinds = ["ffn1_norm_pre", "ffn1_norm_post", "mix_norm_pre", "mix_norm_post", "ffn2_norm_pre",
                     "ffn2_norm_post", "pool_scale", "mlstm_norm_g"]
            for l0 in range(DEPTH):
                r0 = l0 * NGAIN
                for kind in kinds:
                    n = a[kind].shape[1] // P
                    act.dma_start(gain_rows[r0:r0 + n, :], a[kind][l0].rearrange("(k p) -> k p", p=P))\
                        .then_inc(s_gain_in, 16)
                    r0 += n
            act.wait_ge(s_gain_ps, 1)
            act.activation(gains[:, :], bank(7)[:, 0:DEPTH * NGAIN], ACT.Copy).then_inc(s_gains, 1)
            for ch in range(NC + 1):
                t0, n = tokens(ch)
                act.wait_ge(s_x_ps, ch + 1)
                for half in range(2):
                    src = ps[:, 2 * (ch % 3) + half, :].rearrange("p (k n) -> p k n", k=4)[:, :, 0:n]
                    ins = act.activation(xT[:, 4 * half:4 * half + 4, t0:t0 + n], src, ACT.Copy)
                ins.then_inc(x_new_c, 1)
            act.wait_ge(x_new_c, NC + 1)
            act.wait_ge(s_const, 15)
            for k in range(KD):
                act.activation(rstd[:, 16 + k:17 + k], ones[:, k:k + 1], ACT.Copy).then_inc(x_new, 1)

            with act.Fori(0, DEPTH) as l:
                link = Link(l)
                q0 = l * SLOT_USES
                hi_part(0, q0)
                hi_part(1, q0)
                pre_norm(l, 0)
                ffn(l, 0, q0 + Q_FFN1)
                root(2 * (l * 3) + 1)
                pre_norm(l, 1)

                lsl = bass.ds(l, 1)
                act.dma_start(i_bias[:, :], a["mlstm_i_bias"][lsl, :].rearrange("a h -> h a")).then_inc(s_bias, 16)
                act.dma_start(f_bias[:, :], a["mlstm_f_bias"][lsl, :].rearrange("a h -> h a")).then_inc(s_bias, 16)
                act.dma_start(m0[:, :], a["state_mlstm_m"][lsl, :, :].rearrange("a b h -> h (a b)")).then_inc(s_m0, 16)
                act.dma_start(n0[:, :], a["state_mlstm_n"][lsl].rearrange("a b h k -> (a b) (h k)")).then_inc(n0_in, 16)
                for j in range(2):
                    hi_part(j, q0 + Q_MIX + 1)
                act.wait_ge(row_in, l + 1)
                link(act.activation(row_softplus[:, :], row_f[:, :], ACT.Abs))
                link(act.activation(row_softplus[:, :], row_softplus[:, :], ACT.Exp, scale=-1.0))
                act.activation(row_softplus[:, :], row_softplus[:, :], ACT.Ln, bias=ones[0:HEADS, 0:1]).then_inc(row_sp, 1)

                def z_tile(n, t, i=0):
                    hi_part(n % 2, q0 + Q_MIX + 1 + n // 2 + i + 1)
                    dst = z[:, bass.ds(t + 2 * i, 1), :].rearrange("p a (b n) -> p (a b) n", b=2)
                    act.activation(dst, pair(n % 2), ACT.Copy).then_inc(z_out, 1)

                with act.Fori(0, HEAD_START // 4) as i:
                    z_tile(0, Z_Q, i)
                    z_tile(1, Z_Q + 1, i)
                act.wait_ge(row_decay, l + 1)
                act.activation(dlast[:, :], dlast[:, :], ACT.Exp).then_inc(decay_exp, 1)
                act.wait_ge(row_done, l + 1)
                act.dma_start(o["m_prompt"][lsl, 0, :].rearrange("a h -> h a"), row_m[:, SEQ - 1:SEQ]).then_inc(m_out, 16)
                act.dma_start(o["m_sample"][lsl, :, :].rearrange("a b h -> h (a b)"),
                              row_m[:, SEQ + DS - 1:T:DS]).then_inc(m_out, 16)
                act.wait_ge(q_ps, l + 1)
                tp = ps[:, 4, :].rearrange("p (c n) -> p c n", c=NC)
                act.activation(tok_exp[:, 0:NC, :], tp[:, :, 32:P], ACT.Exp)
                act.activation(tok_a[:, 0:NC, :], tp[:, :, 0:HEADS], ACT.Copy)
                act.activation(tok_exp[0:NS, NC, :], ps[0:NS, 5, 32:P], ACT.Exp)
                act.activation(tok_a[0:NS, NC, :], ps[0:NS, 5, 0:HEADS], ACT.Copy).then_inc(tok_sb, 1)
                with act.Fori(HEAD_START // 4, HEAD_START // 2) as i:
                    z_tile(0, Z_Q, i)
                    z_tile(1, Z_Q + 1, i)
                act.wait_ge(m_out, 32 * (l + 1))

                zn = HEAD_START
                for ch in range(NC + 1):
                    t0, n = tokens(ch)
                    cc = l * (NC + 1) + ch
                    sample = ch == NC
                    act.wait_ge(vk_ps, cc + 1)
                    if ch == 0:
                        act.wait_ge(vt_ones, l + 1)
                        act.wait_ge(tok_sb, l + 1)
                    else:
                        act.wait_ge(st_ps, l * NC + ch)
                    for i in range(2):
                        src = ps[0:n, 4 + i, :].rearrange("p (h v) -> p h v", h=2)
                        ins = act.activation(vt[0:n, 2 * i:2 * i + 2, 0:DV], src, ACT.Copy)
                    ins.then_inc(vt_sb, 1)
                    for h in range(HEADS):
                        ins = act.activation(dt_[0:n, h, 0:n], ps[0:n, 7, h * n:(h + 1) * n], ACT.Exp,
                                             bias=tok_a[0:n, ch, h:h + 1])
                    ins.then_inc(dt_sb, 1)
                    if not sample:
                        z_tile(zn, Z_ORDER[zn])
                        zn += 1
                    z_tile(zn, Z_ORDER[zn])
                    zn += 1
                    if sample:
                        act.wait_ge(cT_ps, l + 1)
                        act.activation(c_out[:, 0:4, :], ps[:, 4, :].rearrange("p (i k) -> p i k", i=4), ACT.Copy)
                        act.activation(c_out[:, 4:8, :], ps[:, 5, :].rearrange("p (i k) -> p i k", i=4), ACT.Copy)
                        act.activation(nT_out[:, :], ps[0:HEADS, 6, 0:P], ACT.Copy).then_inc(cT_sb, 1)
                        act.wait_ge(cT_sb, l + 1)
                        act.dma_start(o["C_prompt"][lsl, 0].rearrange("a h (w v) k -> v (a h w) k", v=P),
                                      c_out[:, :, :]).then_inc(c_done, 16)
                        act.dma_start(o["n_prompt"][lsl, 0].rearrange("a h k -> (a h) k"), nT_out[:, :]).then_inc(c_done, 16)
                        act.wait_ge(c_done, 32 * (l + 1))

                        def load_c0(h, vh):
                            src = a["state_mlstm_C"][lsl, :, h, vh * P:(vh + 1) * P, :]
                            act.dma_start(c0[:, vh, :, :], src.rearrange("a b v k -> v (a b) k")).then_inc(c0_in[vh], 16)

                        load_c0(0, 0)
                        load_c0(0, 1)
                        for h in range(HEADS):
                            hh_ = l * HEADS + h
                            for vh in range(VH):
                                u = hh_ * VH + vh
                                act.wait_ge(c0T_ps, u + 1)
                                if vh == 0:
                                    act.wait_ge(nu_sb, l + 1)
                                    if h:
                                        act.wait_ge(num_ps, l * (2 * NC + HEADS) + 2 * NC + h)
                                    act.activation(c0T[:, :, DV], n0T[:, h, :], ACT.Copy)
                                for b in range(2):
                                    ins = act.activation(c0T[:, 4 * b:4 * b + 4, vh * P:(vh + 1) * P],
                                                         ps[:, 4 + b, :].rearrange("p (b k) -> p b k", b=4), ACT.Copy)
                                ins.then_inc(c0T_sb, 1)
                            for vh in range(VH):
                                act.wait_ge(cu_sb, hh_ * VH + vh + 1)
                                dst = o["C_sample"][lsl, :, h, vh * P:(vh + 1) * P, :]
                                act.dma_start(dst.rearrange("a b v k -> v (a b) k"), c0[:, vh, :, :])\
                                    .then_inc(c0_done[vh], 16)
                            for vh in range(VH):
                                act.wait_ge(c0_done[vh], 16 * (hh_ + 1))
                                if h < HEADS - 1:
                                    load_c0(h + 1, vh)
                        act.wait_ge(nu_sb, l + 1)
                        act.dma_start(o["n_sample"][lsl].rearrange("a b h k -> (a b) (h k)"), n0[:, :]).then_inc(n_done, 16)
                        z_tile(zn, Z_ORDER[zn])
                        zn += 1
                    act.wait_ge(num_sb, l * (2 * NC + HEADS) + (2 * ch + 2 if not sample else 2 * NC + HEADS))
                    for h in range(HEADS):
                        ins = act.activation(squares[0:n, h, :], num[0:n, h, 0:DV], ACT.Square,
                                             accum_out=hss[0:n, h:h + 1])
                    ins.then_inc(hss_s, 1)
                    if not sample:
                        z_tile(zn, Z_ORDER[zn])
                        zn += 1
                    act.wait_ge(hvar_s, cc + 1)
                    act.activation(hvar[0:n, :], hvar[0:n, :], ACT.Sqrt).then_inc(hstd_s, 1)
                    act.wait_ge(hct_ps, cc + 1)
                    for i in range(2):
                        src = ps[:, 4 + i, 0:4 * n].rearrange("p (c n) -> p c n", c=4)
                        ins = act.activation(z[:, Z_VAL + 4 * i:Z_VAL + 4 * i + 4, t0:t0 + n], src, ACT.Copy)
                    ins.then_inc(hct_sb, 1)

                act.wait_ge(n_done, 16 * (l + 1))
                act.dma_start(ws_raw[:, :, :], a["gmlp_w_s"][lsl].rearrange("a g t s -> t (a g) s")).then_inc(a_in, 16)
                act.dma_start(bs_row[:, :, :], a["gmlp_b_s"][lsl]).then_inc(a_in, 16)
                act.dma_start(ln_gb[:, 0, :], a["gmlp_ln_g"][lsl, :].broadcast_to([P, AT * P])).then_inc(a_in, 16)
                act.dma_start(ln_gb[:, 1, :], a["gmlp_ln_b"][lsl, :].broadcast_to([P, AT * P])).then_inc(a_in, 16)
                act.dma_start(prev_raw[:, :], a["state_pool"][lsl].rearrange("a b r c -> (a b r) c")).then_inc(prev_in, 16)
                act.dma_start(o["pool_sample"][lsl, :, 0:BUF - DS, :], a["state_pool"][lsl, :, DS:BUF, :]).then_inc(prow_done, 16)
                for ch in range(NC + 1):
                    t0, n = tokens(ch)
                    bk = (4, 5, 4, 5, 7)[ch]
                    act.wait_ge(av_ps, l * (NC + 1) + ch + 1)
                    act.activation(vn[0:n, ch, :], ps[0:n, bk, :], ACT.Gelu_apprx_tanh).then_inc(av_sb, 1)
                act.activation(z[:, Z_U:Z_U + AT, :], z[:, Z_U:Z_U + AT, :], ACT.Gelu_apprx_tanh).then_inc(u_gelu, 1)
                act.wait_ge(ln_var, l + 1)
                act.activation(ln_rstd[:, :], ln_rstd[:, :], ACT.Sqrt).then_inc(ln_std, 1)
                while zn < NZ:
                    z_tile(zn, Z_ORDER[zn])
                    zn += 1
                act.wait_ge(vn_sb, (l + 1) * (NC + 1))
                act.dma_start(o["gmlp_v_sample"][lsl].rearrange("a b t c -> (a b t) c"), vn[0:NS, NC, :]).then_inc(vn_done, 16)
                act.wait_ge(wsT_s, l + 1)
                act.dma_start(pool_w[:, :, :], a["pool_w"][lsl].rearrange("a g c d -> c (a g) d")).then_inc(pw_in, 16)
                NPREV = DB * BUF
                act.wait_ge(prow_ps, l + 1)
                act.activation(prevT[:, :, :], ps[:, 6, 0:BT * NPREV].rearrange("p (g r) -> p g r", g=BT), ACT.Copy)
                act.activation(pool_rows_p[:, :], ps[0:BUF, 7, :], ACT.Copy)
                act.activation(pool_rows_s[:, :], ps[0:NS, 0, :], ACT.Copy).then_inc(prow_sb, 1)
                act.wait_ge(prow_sb, l + 1)
                act.dma_start(o["pool_prompt"][lsl, 0].rearrange("a r c -> (a r) c"), pool_rows_p[:, :]).then_inc(prow_done, 16)
                act.dma_start(o["pool_sample"][lsl, :, BUF - DS:BUF, :], pool_rows_s[:, :]).then_inc(prow_done, 16)
                act.activation(z[:, Z_O:Z_O + CT_, :], z[:, Z_O:Z_O + CT_, :], ACT.Sigmoid).then_inc(o_sig, 1)
                for g in range(BT):
                    gg = l * BT + g
                    if g:
                        act.wait_ge(pooled_s, gg)
                    act.activation(seg[:, BUF:BUF + SEQ], z[:, Z_B + g, 0:SEQ], ACT.Copy)
                    ss = seg[:, BUF + SEQ:WID].rearrange("p (b r) -> p b r", b=DB)
                    act.activation(ss[:, :, 0:BUF], prevT[:, g, :].rearrange("p (b r) -> p b r", b=DB), ACT.Copy)
                    act.activation(ss[:, :, BUF:BUF + DS], z[:, Z_B + g, SEQ:T].rearrange("p (b t) -> p b t", b=DB),
                                   ACT.Copy).then_inc(seg_sb, 1)
                act.wait_ge(a_sb, (l + 1) * (NC + 1))
                act.activation(a_hi[:, :, :], z[:, Z_U:Z_U + AT, :], ACT.Copy).then_inc(a_hi_s, 1)
                act.wait_ge(b_sb, (l + 1) * BT)
                act.wait_ge(prow_done, 48 * (l + 1))
                act.activation(b_hi[:, :, :], z[:, Z_B:Z_B + BT, :], ACT.Copy).then_inc(b_hi_s, 1)
                for t in range(CT_):
                    act.wait_ge(c_sb, l * CT_ + t + 1)
                    act.activation(c_hi[:, t, :], z[:, Z_O + t, :], ACT.Copy).then_inc(c_hi_s, 1)
                act.wait_ge(vn_done, 16 * (l + 1))
                for half in range(2):
                    with act.Fori(2 * half, 2 * half + 2) as i:
                        for m2 in range(2):
                            for br in range(3):
                                n = 3 * m2 + br
                                for j in range(2):
                                    hi_part(j, q0 + Q_GATE + 6 * i + n + 1)
                                act.wait_ge(gated, l * PAIRS + G_MIX + 6 * i + n + 1)
                                act.activation(halves(gate_act[n % 2][:, :]), pair(2 * (n % 2)), ACT.Sigmoid)\
                                    .then_inc(sig_s, 1)
                            act.wait_ge(merged_s, l * KD + 2 * i + m2 + 1)
                            act.activation(merged_hi[:, bass.ds(2 * i + m2, 1), :].rearrange("p a n -> p (a n)"),
                                           sq[m2][:, :], ACT.Copy).then_inc(merged_hi_s, 1)
                out_tiles(l, 1, q0 + Q_OUT, 1)
                root(2 * (l * 3 + 1) + 1)
                pre_norm(l, 2)
                ffn(l, 1, q0 + Q_FFN2)
                root(2 * (l * 3 + 2) + 1)

            for ch in range(NC + 1):
                t0, n = tokens(ch)
                act.wait_ge(xo_ps, ch + 1)
                act.activation(x_in[0:n, ch, 0:512], ps[0:n, 2 * (ch % 3), :], ACT.Copy)
                act.activation(x_in[0:n, ch, 512:1024], ps[0:n, 2 * (ch % 3) + 1, :], ACT.Copy).then_inc(xo_sb, 1)
                act.wait_ge(xo_sb, ch + 1)
                dst = o["y_prompt"][0, t0:t0 + n, :] if ch < NC else o["y_sample"].rearrange("b t d -> (b t) d")
                act.dma_start(dst, x_in[0:n, ch, :]).then_inc(xo_done, 16)
            act.wait_ge(xo_done, 16 * (NC + 1))
            act.wait_ge(m_out, 32 * DEPTH)
            act.wait_ge(c_done, 32 * DEPTH)
            act.wait_ge(n_done, 16 * DEPTH)
            act.wait_ge(vn_done, 16 * DEPTH)
            act.wait_ge(prow_done, 48 * DEPTH)
            for vh in range(VH):
                act.wait_ge(c0_done[vh], 16 * HEADS * DEPTH)

        @block.vector
        def _(dve):
            class Link:
                def __init__(self, l):
                    self.base, self.n = l * DVE_STEPS, 0

                def __call__(self, ins, alone=False):
                    self.n += 1
                    ins.then_inc(link_d, 1)
                    dve.wait_ge(link_d, self.base + self.n)
                    if alone:
                        apart(dve)

            def recip_root(n_ps, ri):
                dve.tensor_scalar(halves(rstd[:, :]), pair(n_ps), 1.0 / D, EPS, ALU.mult, ALU.add).then_inc(rs_var, 1)
                dve.wait_ge(rs_sqrt, ri + 1)
                dve.reciprocal(rstd[:, :], rstd[:, :]).then_inc(rs_inv, 1)
                dve.wait_ge(rs_inv, ri + 1)

            def pre_norm(l, s):
                nb = l * 3 + s
                dve.wait_ge(x_ss, nb * KD + KD)
                recip_root(3, 2 * nb)
                for k in range(KD + 1):
                    if k < KD:
                        if k >= 2:
                            dve.wait_ge(h_lo_s, nb * KD + k - 1)
                        g = G_PRE[s] + k
                        dve.scalar_tensor_tensor(out=prod[k % 2][:, :], in0=xT[:, k, :], scalar=gain[:, g:g + 1],
                                                 in1=rstd[:, :], op0=ALU.mult, op1=ALU.mult).then_inc(h_f, 1)
                    if k:
                        dve.wait_ge(h_hi_s, nb * KD + k)
                        dve.tensor_tensor(h_lo[:, k - 1, :], prod[(k - 1) % 2][:, :], h_hi[:, k - 1, :].bitcast(F32),
                                          ALU.subtract).then_inc(h_lo_s, 1)

            def post_norm(l, s):
                nb = l * 3 + s
                dve.wait_ge(ss_tot, nb + 1)
                recip_root(2, 2 * nb + 1)
                for k in range(KD + 1):
                    if k < KD:
                        g = G_POST[s] + k
                        dve.scalar_tensor_tensor(out=yT[:, k, :], in0=yT[:, k, :], scalar=gain[:, g:g + 1],
                                                 in1=rstd[:, :], op0=ALU.mult, op1=ALU.mult).then_inc(y_scaled, 1)
                    if k:
                        dve.wait_ge(y_scaled, nb * KD + k)
                        dve.tensor_tensor(xT[:, k - 1, :], xT[:, k - 1, :], yT[:, k - 1, :], ALU.add).then_inc(x_new, 1)

            def out_tiles(l, s):
                nb = l * 3 + s
                dve.memset(ss_sum[:, :], 0.0).then_inc(ss_zero, 1)
                dve.wait_ge(ss_zero, nb + 1)
                apart(dve)
                with dve.Fori(0, KD // 2) as i:
                    for m2 in range(2):
                        dve.wait_ge(y_out, nb * KD + 2 * i + m2 + 3)
                        dve.wait_ge(ss_add, nb * KD + 2 * i + m2 + 2)
                        dve.tensor_tensor(ss_sum[:, :], ss_sum[:, :], sq[m2][:, :], ALU.add).then_inc(ss_add, 1)

            def ffn(l, f):
                apart(dve)
                with dve.Fori(0, FT // 2) as i:
                    for m2 in range(2):
                        pf = (l * 2 + f) * FT + 2 * i + m2
                        dve.wait_ge(silu_s, pf + 1)
                        dve.tensor_tensor(halves(prod[m2][:, :]), halves(gate_act[m2][:, :]), pair(2 * m2 + 1),
                                          ALU.mult).then_inc(gated, 1)
                        dve.wait_ge(act_hi_s, pf + 1)
                        sel = bass.ds(2 * i + m2, 1)
                        dve.tensor_tensor(act_lo[:, sel, :].rearrange("p a n -> p (a n)"), prod[m2][:, :],
                                          act_hi[:, sel, :].bitcast(F32).rearrange("p a n -> p (a n)"),
                                          ALU.subtract).then_inc(act_lo_s, 1)
                out_tiles(l, 2 * f)

            dve.wait_ge(s_const, 15)
            dve.tensor_copy(rep8[:, :].rearrange("p (b t) -> p b t", b=DB),
                            ident[0:DS, 0:DS].unsqueeze(1).broadcast_to([DS, DB, DS])).then_inc(s_dve0, 1)
            for g, w in enumerate(POOL_WINDOWS):
                dve.tensor_scalar(recip16[:, g, :], count_i[:, :], float(w), None, ALU.min).then_inc(s_dve0, 1)
            dve.wait_ge(s_dve0, 1 + BT)
            dve.reciprocal(recip16[:, :, :], recip16[:, :, :]).then_inc(s_dve0, 1)
            for i, s_ in enumerate((gated, y_out, ss_add, z_out)):
                for j in range(2):
                    dve.memset(rstd[:, 2 * i + j:2 * i + j + 1], 0.0).then_inc(s_, 1)

            with dve.Fori(0, DEPTH) as l:
                link = Link(l)
                dve.wait_ge(s_gains, 1)
                dve.tensor_copy(gain[:, :], gains[:, bass.ds(l * NGAIN, NGAIN)]).then_inc(s_gain, 1)
                dve.wait_ge(s_gain, 2 * l + 1)
                for s in (0, 2):
                    g = gain[:, G_POST[s]:G_POST[s] + KD]
                    ins = dve.tensor_scalar(g, g, 0.5, None, ALU.mult)
                ins.then_inc(s_gain, 1)
                dve.wait_ge(s_gain, 2 * l + 2)
                pre_norm(l, 0)
                ffn(l, 0)
                post_norm(l, 0)
                pre_norm(l, 1)

                dve.memset(row_reset[:, :], 1.0)
                dve.memset(gate_q[:, :], 0.0)
                dve.memset(qm[:, :, :], 0.0)
                dve.memset(state[:, :, :], 0.0).then_inc(st_zero, 1)
                dve.memset(vt[:, :, DV], 1.0).then_inc(vt_ones, 1)
                link(dve.memset(mprev[:, :], 0.0))
                dve.memset(row_reset[:, 0:SEQ:P], 0.0)
                link(dve.memset(row_reset[:, SEQ:T:DS], 0.0))
                dve.wait_ge(mm[0], l * SLOT_USES + Q_MIX + 2)
                dve.wait_ge(mm[1], l * SLOT_USES + Q_MIX + 2)
                dve.wait_ge(s_bias, 32 * (l + 1))
                dve.tensor_scalar(halves(row_i[:, :]), pair(2)[0:HEADS], i_bias[:, 0:1], None, ALU.add)
                dve.tensor_scalar(halves(row_f[:, :]), pair(3)[0:HEADS], f_bias[:, 0:1], None, ALU.add).then_inc(row_in, 1)
                dve.wait_ge(row_sp, l + 1)
                link(dve.scalar_tensor_tensor(out=row_lf[:, :], in0=row_f[:, :], scalar=0.0, in1=row_softplus[:, :],
                                              op0=ALU.min, op1=ALU.subtract))
                link(dve.tensor_tensor_scan(row_b[:, :], row_reset[:, :], row_lf[:, :], 0.0, ALU.mult, ALU.add))
                dve.tensor_tensor(gate_q[0:HEADS, :], row_i[:, :], row_b[:, :], ALU.subtract)
                dve.tensor_copy(row_lf2[:, :], row_lf[:, :])
                dve.tensor_copy(row_i2[:, :], row_i[:, :])
                dve.wait_ge(s_m0, 16 * (l + 1))
                link(dve.tensor_tensor(m0t[:, :], row_lf[:, SEQ:T:DS], m0[:, :], ALU.add))
                dve.tensor_tensor(row_i2[:, SEQ:T:DS], row_i[:, SEQ:T:DS], m0t[:, :], ALU.max)
                link(dve.memset(row_lf2[:, SEQ:T:DS], NEG))
                link(dve.tensor_tensor_scan(row_m[:, :], row_lf2[:, :], row_i2[:, :], 0.0, ALU.add, ALU.max))
                dve.tensor_copy(mprev[:, 1:NC], row_m[:, P - 1:SEQ - 1:P])
                dve.tensor_copy(mprev[:, NC:NC + DB], m0[:, :])
                link(dve.tensor_tensor(row_bm[:, :], row_b[:, :], row_m[:, :], ALU.subtract))
                dve.tensor_tensor(dlast[:, 0:NC], row_bm[:, P - 1:SEQ:P], mprev[:, 0:NC], ALU.add)
                dve.tensor_tensor(dlast[:, NC:NC + DB], row_bm[:, SEQ + DS - 1:T:DS], mprev[:, NC:NC + DB],
                                  ALU.add).then_inc(row_decay, 1)
                pv = lambda t_, r0=0: t_[r0:r0 + HEADS, 0:SEQ].rearrange("h (c n) -> h c n", n=P)
                sv = lambda t_, r0=0: t_[r0:r0 + HEADS, SEQ:T].rearrange("h (b n) -> h b n", n=DS)
                bp = lambda t_: t_.unsqueeze(2).broadcast_to([HEADS, NC, P])
                bs = lambda t_: t_.unsqueeze(2).broadcast_to([HEADS, DB, DS])
                dve.tensor_tensor(pv(gate_q, 32), pv(row_bm), bp(mprev[:, 0:NC]), ALU.add)
                dve.tensor_tensor(sv(gate_q, 32), sv(row_bm), bs(mprev[:, NC:NC + DB]), ALU.add)
                dve.tensor_scalar(gate_q[64:64 + HEADS, :], row_m[:, :], -1.0, None, ALU.mult)
                dve.tensor_tensor(pv(gate_q, 96), pv(gate_q), bp(row_bm[:, P - 1:SEQ:P]), ALU.add)
                dve.tensor_tensor(sv(gate_q, 96), sv(gate_q), bs(row_bm[:, SEQ + DS - 1:T:DS]), ALU.add).then_inc(row_done, 1)
                dve.wait_ge(decay_ps, l + 1)
                dve.tensor_copy(decay[:, :, :], ps[:, 6, 0:HEADS * (NC + DB)].rearrange("p (h c) -> p h c", h=HEADS))\
                    .then_inc(decay_sb, 1)

                for ch in range(NC + 1):
                    t0, n = tokens(ch)
                    cc = l * (NC + 1) + ch
                    nb = l * (2 * NC + HEADS)
                    sample = ch == NC
                    inter, w_in = tok_exp[0:n, ch, 0:HEADS], tok_exp[0:n, ch, 64:64 + HEADS]
                    dve.wait_ge(vk_ps, cc + 1)
                    dve.wait_ge(tok_sb, l + 1)
                    dve.scalar_tensor_tensor(out=kw[0:n, :, :], in0=ps[0:n, 6, :].rearrange("p (h k) -> p h k", h=HEADS),
                                             scalar=QK_SCALE, in1=w_in.unsqueeze(2).broadcast_to([n, HEADS, DK]),
                                             op0=ALU.mult, op1=ALU.mult).then_inc(kw_sb, 1)
                    dve.wait_ge(qk_ps, cc + 1)
                    dve.wait_ge(dt_sb, cc + 1)
                    dve.scalar_tensor_tensor(out=wt[0:n, :, 0:n], in0=ps[0:n, 4, 0:4 * n].rearrange("p (h t) -> p h t", h=HEADS),
                                             scalar=QK_SCALE, in1=dt_[0:n, :, 0:n], op0=ALU.mult, op1=ALU.mult).then_inc(wt_sb, 1)
                    if not sample:
                        for r in range(2):
                            dve.wait_ge(num_ps, nb + 2 * ch + r + 1)
                            hs = slice(2 * r, 2 * r + 2)
                            link(dve.tensor_tensor(num[0:n, hs, :], ps[0:n, 6:8, 0:VE],
                                                   inter[:, hs].unsqueeze(2).broadcast_to([n, 2, VE]), ALU.mult))
                            dve.tensor_tensor(num[0:n, hs, :], num[0:n, hs, :], ps[0:n, 4:6, 0:VE], ALU.add).then_inc(num_sb, 1)
                        dve.wait_ge(st_ps, l * NC + ch + 1)
                        link(dve.tensor_tensor(state[:, :, :], state[:, :, :],
                                               decay[:, :, ch:ch + 1].broadcast_to([P, HEADS, VE]), ALU.mult))
                        dve.tensor_tensor(state[:, :, :], state[:, :, :], ps[:, 4:8, 0:VE], ALU.add).then_inc(st_sb, 1)
                    else:
                        dve.wait_ge(n0_ps, l + 1)
                        dve.tensor_copy(n0T[:, :, :], ps[:, 6, 0:HEADS * DB].rearrange("p (h b) -> p h b", h=HEADS))
                        link(dve.tensor_copy(decay8[:, :], ps[0:DB, 5, 0:HEADS]))
                        n3 = n0[:, :].rearrange("b (h k) -> b h k", h=HEADS)
                        link(dve.tensor_tensor(n3, n3, decay8[:, :].unsqueeze(2).broadcast_to([DB, HEADS, DK]), ALU.mult))
                        dve.tensor_tensor(n0[:, :], n0[:, :], ps[0:DB, 4, :], ALU.add).then_inc(nu_sb, 1)
                        dve.wait_ge(nu_sb, l + 1)
                        for h in range(HEADS):
                            hh_ = l * HEADS + h
                            if h:
                                dve.wait_ge(num_ps, nb + 2 * NC + h)
                            qsrc = z[:, Z_Q + h, SEQ:T].rearrange("p (b t) -> p b t", b=DB)
                            for b in range(DB):
                                ins = dve.tensor_copy(qm[:, b, b * DS:(b + 1) * DS], qsrc[:, b, :])
                            ins.then_inc(qm_sb, 1)
                            if h:
                                dve.wait_ge(cu_ps, hh_ * VH)
                            else:
                                dve.wait_ge(cT_sb, l + 1)
                            dve.tensor_tensor(kwm[:, :, :], kw[0:NS, h, :].unsqueeze(1).broadcast_to([NS, DB, DK]),
                                              block01[:, :].unsqueeze(2).broadcast_to([NS, DB, DK]), ALU.mult).then_inc(kwm_sb, 1)
                            dve.wait_ge(num_ps, nb + 2 * NC + h + 1)
                            link(dve.tensor_scalar(num[0:n, h, :], ps[0:n, 7, 0:VE], inter[:, h:h + 1], None, ALU.mult))
                            dve.tensor_tensor(num[0:n, h, :], num[0:n, h, :], ps[0:n, 6, 0:VE], ALU.add).then_inc(num_sb, 1)
                            for vh in range(VH):
                                u = hh_ * VH + vh
                                cv = c0[:, vh, :, :]
                                dve.wait_ge(c0T_ps, u + 1)
                                link(dve.tensor_tensor(cv, cv, decay[:, h, NC:NC + DB].unsqueeze(2).broadcast_to([P, DB, DK]),
                                                       ALU.mult))
                                dve.wait_ge(cu_ps, u + 1)
                                dve.tensor_tensor(cv, cv, ps[:, 4:6, :].rearrange("p b (c k) -> p (b c) k", k=DK),
                                                  ALU.add).then_inc(cu_sb, 1)
                    dve.wait_ge(num_sb, nb + (2 * ch + 2 if not sample else 2 * NC + HEADS))
                    den = num[0:n, :, DV]
                    link(dve.scalar_tensor_tensor(out=hden[0:n, :], in0=den, scalar=-1.0, in1=den, op0=ALU.mult, op1=ALU.max))
                    link(dve.tensor_tensor(hden[0:n, :], hden[0:n, :], tok_exp[0:n, ch, 32:32 + HEADS], ALU.max))
                    link(dve.reciprocal(hrec[0:n, :], hden[0:n, :]))
                    dve.wait_ge(hss_s, cc + 1)
                    link(dve.tensor_tensor(hvar[0:n, :], hss[0:n, :], hrec[0:n, :], ALU.mult))
                    link(dve.tensor_tensor(hvar[0:n, :], hvar[0:n, :], hrec[0:n, :], ALU.mult))
                    dve.tensor_scalar(hvar[0:n, :], hvar[0:n, :], 1.0 / DV, EPS, ALU.mult, ALU.add).then_inc(hvar_s, 1)
                    dve.wait_ge(hstd_s, cc + 1)
                    link(dve.reciprocal(hvar[0:n, :], hvar[0:n, :]))
                    link(dve.tensor_tensor(hvar[0:n, :], hvar[0:n, :], hrec[0:n, :], ALU.mult))
                    dve.tensor_tensor(num[0:n, :, 0:DV], num[0:n, :, 0:DV],
                                      hvar[0:n, :].unsqueeze(2).broadcast_to([n, HEADS, DV]), ALU.mult).then_inc(hc_sb, 1)

                dve.wait_ge(ws_ps, l + 1)
                dve.memset(ln_rstd[:, :], 1.0)
                m3 = mask_p[:, :].unsqueeze(1).broadcast_to([P, AT, P])
                dve.scalar_tensor_tensor(out=wsT[:, :, :], in0=m3, scalar=-0.5,
                                         in1=ps[:, 6, :].rearrange("p (g t) -> p g t", g=AT),
                                         op0=ALU.is_ge, op1=ALU.mult).then_inc(wsT_s, 1)
                dve.wait_ge(wss_ps, l + 1)
                for g in range(AT):
                    rep = ps[0:NS, 6, g * DS:(g + 1) * DS].unsqueeze(1).broadcast_to([NS, DB, DS])
                    dve.scalar_tensor_tensor(out=ws_s[:, g, :].rearrange("p (b t) -> p b t", b=DB),
                                             in0=mask_s[:, :].rearrange("p (b t) -> p b t", b=DB), scalar=-0.5, in1=rep,
                                             op0=ALU.is_ge, op1=ALU.mult)
                for ch in range(NC + 1):
                    _, n = tokens(ch)
                    dve.wait_ge(av_sb, l * (NC + 1) + ch + 1)
                    link(dve.bn_stats(ln_stats[0:n, ch, :], vn[0:n, ch, :]), True)
                    link(dve.bn_aggr(ln_mv[0:n, ch, :], ln_stats[0:n, ch, :]))
                    ins = dve.tensor_scalar(ln_rstd[0:n, ch:ch + 1], ln_mv[0:n, ch, 1:2], EPS, None, ALU.add)
                ins.then_inc(ln_var, 1)
                dve.wait_ge(ln_std, l + 1)
                link(dve.reciprocal(ln_rstd[:, :], ln_rstd[:, :]))
                for ch in range(NC + 1):
                    _, n = tokens(ch)
                    v_ = vn[0:n, ch, :]
                    link(dve.tensor_scalar(v_, v_, ln_mv[0:n, ch, 0:1], ln_rstd[0:n, ch:ch + 1], ALU.subtract, ALU.mult))
                    link(dve.tensor_tensor(v_, v_, ln_gb[0:n, 0, :], ALU.mult))
                    dve.tensor_tensor(v_, v_, ln_gb[0:n, 1, :], ALU.add).then_inc(vn_sb, 1)
                dve.wait_ge(u_gelu, l + 1)
                for ch in range(NC + 1):
                    t0, n = tokens(ch)
                    cc = l * (NC + 1) + ch
                    dve.wait_ge(mix_ps, cc + 1)
                    dst = z[:, Z_U:Z_U + AT, t0:t0 + n]
                    dve.tensor_tensor(dst, dst, ps[:, 4 + ch % 2, 0:AT * n].rearrange("p (g t) -> p g t", g=AT),
                                      ALU.mult).then_inc(a_sb, 1)

                for vh in range(VH):
                    dve.wait_ge(c0_done[vh], 16 * HEADS * (l + 1))
                link(dve.memset(seg[:, 0:BUF], 0.0))
                for g, w in enumerate(POOL_WINDOWS):
                    gg = l * BT + g
                    dve.wait_ge(seg_sb, gg + 1)
                    src, step, first, bufs = seg, 1, 0, (win_a, win_b)
                    for j in range(g + 1):
                        dst = bufs[j % 2]
                        first += step
                        link(dve.tensor_tensor(dst[:, first:WID], src[:, first:WID], src[:, first - step:WID - step], ALU.add))
                        src, step = dst, 2 * step
                    if g:
                        dve.wait_ge(pmix_ps, gg)
                    dve.scalar_tensor_tensor(out=pooled[:, 16:SEQ], in0=src[:, BUF + 16:BUF + SEQ], scalar=1.0 / w,
                                             in1=seg[:, BUF + 16:BUF + SEQ], op0=ALU.mult, op1=ALU.subtract)
                    sview = lambda t_: t_[:, BUF + SEQ:WID].rearrange("p (b r) -> p b r", b=DB)[:, :, BUF:BUF + DS]
                    dve.scalar_tensor_tensor(out=pooled[:, SEQ:T].rearrange("p (b t) -> p b t", b=DB), in0=sview(src),
                                             scalar=1.0 / w, in1=sview(seg), op0=ALU.mult, op1=ALU.subtract)
                    link(dve.tensor_tensor(pooled[:, 0:16], src[:, BUF:BUF + 16], recip16[:, g, :], ALU.mult))
                    ins = dve.tensor_tensor(pooled[:, 0:16], pooled[:, 0:16], seg[:, BUF:BUF + 16], ALU.subtract)
                    ins.then_inc(pooled_s, 1)
                    dve.wait_ge(pmix_ps, gg + 1)
                    dve.tensor_scalar(halves(z[:, Z_B + g, :]), pair(3), gain[:, G_POOL + g:G_POOL + g + 1], None,
                                      ALU.mult).then_inc(b_sb, 1)

                dve.wait_ge(a_hi_s, l + 1)
                dve.tensor_tensor(a_lo[:, :, :], z[:, Z_U:Z_U + AT, :], a_hi[:, :, :].bitcast(F32), ALU.subtract).then_inc(a_lo_s, 1)
                dve.wait_ge(a_lo_s, l + 1)
                dve.wait_ge(b_hi_s, l + 1)
                dve.tensor_tensor(b_lo[:, :, :], z[:, Z_B:Z_B + BT, :], b_hi[:, :, :].bitcast(F32), ALU.subtract).then_inc(b_lo_s, 1)
                dve.wait_ge(o_sig, l + 1)
                for t in range(CT_ + 1):
                    if t < CT_:
                        g = G_HEAD + t
                        dve.scalar_tensor_tensor(out=z[:, Z_O + t, :], in0=z[:, Z_VAL + t, :], scalar=gain[:, g:g + 1],
                                                 in1=z[:, Z_O + t, :], op0=ALU.mult, op1=ALU.mult).then_inc(c_sb, 1)
                    if t:
                        dve.wait_ge(c_hi_s, l * CT_ + t)
                        dve.tensor_tensor(c_lo[:, t - 1, :], z[:, Z_O + t - 1, :], c_hi[:, t - 1, :].bitcast(F32),
                                          ALU.subtract).then_inc(c_lo_s, 1)

                for half, m_lo in enumerate((merged_lo0, merged_lo1)):
                    apart(dve)
                    with dve.Fori(0, 2) as i:
                        for m2 in range(2):
                            m = 4 * half + m2
                            for br in range(3):
                                n = 3 * m2 + br
                                dve.wait_ge(sig_s, l * 3 * KD + 12 * half + 6 * i + n + 1)
                                if br == 0:
                                    dst = sq[m2]
                                else:
                                    dst = prod[n % 2]
                                dve.tensor_tensor(halves(dst[:, :]), halves(gate_act[n % 2][:, :]), pair(2 * (n % 2) + 1),
                                                  ALU.mult).then_inc(gated, 1)
                                dve.wait_ge(gated, l * PAIRS + G_MIX + 12 * half + 6 * i + n + 3)
                                if br == 1:
                                    dve.tensor_tensor(sq[m2][:, :], sq[m2][:, :], prod[n % 2][:, :], ALU.add).then_inc(merge1, 1)
                                if br == 2:
                                    dve.wait_ge(merge1, l * KD + 4 * half + 2 * i + m2 + 1)
                                    dve.tensor_tensor(sq[m2][:, :], sq[m2][:, :], prod[n % 2][:, :], ALU.add).then_inc(merged_s, 1)
                            dve.wait_ge(merged_hi_s, l * KD + 4 * half + 2 * i + m2 + 1)
                            hi_t = merged_hi[:, bass.ds(4 * half + 2 * i + m2, 1), :].bitcast(F32)
                            dve.tensor_tensor(m_lo[:, bass.ds(2 * i + m2, 1), :].rearrange("p a n -> p (a n)"),
                                              sq[m2][:, :], hi_t.rearrange("p a n -> p (a n)"), ALU.subtract)\
                                .then_inc(merged_lo_s, 1)
                out_tiles(l, 1)
                post_norm(l, 1)
                pre_norm(l, 2)
                ffn(l, 1)
                post_norm(l, 2)
                assert link.n == DVE_STEPS, link.n


def kernel(**inputs):
    import numpy as _np
    import concourse.bacc as _bacc
    from concourse import mybir as _mybir
    from concourse.bass_utils import run_bass_kernel_spmd as _run

    nc = _bacc.Bacc("TRN2", target_bir_lowering=False, num_devices=1)
    arrays, args = {}, {}
    for name, value in inputs.items():
        v = _np.ascontiguousarray(value)
        arrays[f"in_{name}"] = v
        args[name] = nc.dram_tensor(f"in_{name}", v.shape, _mybir.dt.from_np(v.dtype), kind="ExternalInput").ap()
    x_p, x_s, pool, c, n, m = (inputs[k].shape for k in (
        "x_prompt", "x_sample", "state_pool", "state_mlstm_C", "state_mlstm_n", "state_mlstm_m"))
    a_width = inputs["gmlp_ln_g"].shape[1]
    depth = c[0]
    shapes = {
        "y_prompt": x_p, "y_sample": x_s,
        "pool_prompt": (depth, 1, *pool[2:]), "C_prompt": (depth, 1, *c[2:]), "n_prompt": (depth, 1, *n[2:]),
        "m_prompt": (depth, 1, *m[2:]),
        "pool_sample": pool, "C_sample": c, "n_sample": n, "m_sample": m,
        "gmlp_v_sample": (depth, *x_s[:2], a_width),
    }
    outs = {k: nc.dram_tensor(f"out_{k}", s, _mybir.dt.float32, kind="ExternalOutput").ap() for k, s in shapes.items()}
    trunk_program(nc, args, outs)
    r = _run(nc, [arrays], core_ids=[0])
    return tuple(r.results[0][f"out_{k}"] for k in shapes)
```

```python
from contextlib import ExitStack

import concourse.bass as bass
from concourse import mybir

ALU = mybir.AluOpType
ACT = mybir.ActivationFunctionType
AX = mybir.AxisListType
F32 = mybir.dt.float32
F32R = mybir.dt.float32r
I32 = mybir.dt.int32

P = 128
EPS = 1e-6
NEG = -1e30
POOL_WINDOWS = (2, 4, 8, 16)


def trunk_program(nc, a, o):
    DEPTH, D, TWO_FF = a["ffn1_w_in"].shape
    SEQ = a["x_prompt"].shape[1]
    DB, DS = a["x_sample"].shape[0:2]
    NS = DB * DS
    T = SEQ + NS
    H = T // 2
    DF = TWO_FF // 2
    KD = D // P
    FT = DF // P
    AT = a["gmlp_ln_g"].shape[1] // P
    BT = a["pool_scale"].shape[1] // P
    HEADS, DV, DK = a["state_mlstm_C"].shape[2:5]
    CT_ = HEADS * DV // P
    VH = DV // P
    BUF = a["state_pool"].shape[2]
    NC = SEQ // P
    QK_SCALE = float(DK) ** -0.5
    assert D == 8 * P and DK == P and FT % 2 == 0 and AT == BT == HEADS == 4 and CT_ == 8 and NC == 4
    assert NS == 64 and DS == 8

    Z_U, Z_V, Z_B, Z_Q, Z_K, Z_VAL, Z_O = 0, 4, 8, 12, 16, 20, 28
    NZ = 36
    COL_I, COL_F, COL_G = NZ * P, NZ * P + HEADS, NZ * P + 2 * HEADS
    Z_RUNS = [(Z_Q, 16), (Z_V, 4), (Z_U, 4), (Z_B, 4), (Z_O, 8)]
    Z_ORDER = [t0 + i for t0, n in Z_RUNS for i in range(n)]
    HEAD_START = 16
    CHUNK_O = 5
    CHUNK_END = NZ - (8 - CHUNK_O)

    CHUNKS = [min(8, FT - c) for c in range(0, FT, 8)]
    NCH = len(CHUNKS)
    Q_FFN1 = 0
    Q_DOWN1 = Q_FFN1 + FT
    Q_MIX = Q_DOWN1 + KD * NCH // 2
    Q_GATE = Q_MIX + 1 + NZ // 2
    Q_OUT = Q_GATE + 3 * KD
    Q_FFN2 = Q_OUT + KD // 2
    Q_DOWN2 = Q_FFN2 + FT
    SLOT_USES = Q_DOWN2 + KD * NCH // 2
    PAIRS = 2 * FT + 3 * KD
    G_FFN = (0, FT + 3 * KD)
    G_MIX = FT

    DVE_STEPS = 125

    with ExitStack() as ctx:
        def sem(name):
            return ctx.enter_context(nc.semaphore(name))

        base = (nc.sbuf_base + 63) // 64 * 64
        top = nc.sbuf_usable_end

        def place(name, shape, dt, at):
            size = 4
            for s in shape[1:]:
                size *= s
            assert base <= at and at + size <= top, (name, at, size, top)
            return nc.alloc_sbuf_tensor_at(name, shape, dt, offset=at)

        TB = 4 * T
        X_AT = base
        H_AT = X_AT + KD * TB
        RING_AT = H_AT + 2 * KD * TB
        R_AT = RING_AT + 3 * 2 * KD * P * 4
        TAIL_AT = R_AT + NZ * TB
        R_END = R_AT + 2 * 22 * TB
        C_AT = R_END

        xT = place("xT", [P, KD, T], F32, X_AT)
        h_hi = place("h_hi", [P, KD, T], F32R, H_AT)
        h_lo = place("h_lo", [P, KD, T], F32R, H_AT + KD * TB)
        yT = place("yT", [P, KD, T], F32, H_AT + KD * TB)
        w_raw = place("w_raw", [P, 2, KD, P], F32, RING_AT)
        w_hi = place("w_hi", [P, 2, KD, P], F32R, RING_AT + 2 * KD * P * 4)
        w_lo = place("w_lo", [P, 2, KD, P], F32R, RING_AT + 4 * KD * P * 4)
        act_hi = place("act_hi", [P, FT, T], F32R, R_AT)
        act_lo = place("act_lo", [P, FT, T], F32R, R_AT + FT * TB)
        x_in = place("x_in", [P, NC + 1, D], F32, R_AT)
        z = place("z", [P, NZ, T], F32, R_AT)
        a_hi = place("a_hi", [P, AT, T], F32R, R_AT + Z_V * TB)
        a_lo = place("a_lo", [P, AT, T], F32R, TAIL_AT)
        b_hi = place("b_hi", [P, BT, T], F32R, TAIL_AT + AT * TB)
        b_lo = place("b_lo", [P, BT, T], F32R, R_AT + Z_U * TB)
        c_hi = place("c_hi", [P, CT_, T], F32R, R_AT + Z_Q * TB)
        c_lo = place("c_lo", [P, CT_, T], F32R, R_AT + Z_VAL * TB)
        merged_hi = place("merged_hi", [P, KD, T], F32R, R_AT + Z_O * TB)
        merged_lo0 = place("merged_lo0", [P, KD // 2, T], F32R, R_AT + Z_B * TB)
        rows = [place(n, [HEADS, T], F32, R_AT + (Z_O + i) * TB) for i, n in enumerate(
            ["row_i", "row_f", "row_softplus", "row_lf", "row_b", "row_reset", "row_lf2", "row_i2"])]
        row_i, row_f, row_softplus, row_lf, row_b, row_reset, row_lf2, row_i2 = rows
        row_m = place("row_m", [HEADS, T], F32, R_AT + (Z_O + 1) * TB)

        cursor = [C_AT]

        def small(name, shape, dt=F32):
            n = 4
            for s in shape[1:]:
                n *= s
            t = place(name, shape, dt, cursor[0])
            cursor[0] += (n + 31) // 32 * 32
            return t

        ident = small("ident", [P, P])
        ones = small("ones", [P, P])
        mask_p = small("mask_p", [P, P])
        mask_s = small("mask_s", [NS, NS])
        block01 = small("block01", [NS, DB])
        last01 = small("last01", [NS, DB])
        count_i = small("count_i", [P, 16], I32)
        recip16 = small("recip16", [P, BT, 16])
        rep8 = small("rep8", [DS, NS])
        NGAIN = 6 * KD + BT + CT_
        gains = small("gains", [P, DEPTH * NGAIN])
        gain = small("gain", [P, NGAIN])
        i_bias = small("i_bias", [HEADS, 1])
        f_bias = small("f_bias", [HEADS, 1])
        G_PRE = (0, 2 * KD, 4 * KD)
        G_POST = (KD, 3 * KD, 5 * KD)
        G_POOL, G_HEAD = 6 * KD, 6 * KD + BT
        TMP = cursor[0]

        gate_act = [place(f"gate_act{i}", [P, T], F32, TMP + i * TB) for i in range(2)]
        prod = [place(f"prod{i}", [P, T], F32, TMP + (2 + i) * TB) for i in range(2)]
        sq = [place(f"sq{i}", [P, T], F32, TMP + (4 + i) * TB) for i in range(2)]
        rstd = place("rstd", [P, T], F32, TMP + 6 * TB)
        ss_sum = place("ss_sum", [P, T], F32, TMP + 7 * TB)
        merged_lo1 = place("merged_lo1", [P, KD // 2, T], F32R, TMP + 8 * TB)
        gain_rows = place("gain_rows", [DEPTH * NGAIN, P], F32, TMP)

        cursor[0] = TMP
        VE = DV + 1
        vt = small("vt", [P, HEADS, VE])
        kw = small("kw", [P, HEADS, DK])
        dt_wt = small("dt_wt", [P, 2, HEADS, P])
        dt_, wt = dt_wt[:, 0], dt_wt[:, 1]
        squares = dt_wt.rearrange("p a h t -> p (a h t)").rearrange("p (h v) -> p h v", h=HEADS)
        num = small("num", [P, HEADS, VE])
        state = small("state", [P, HEADS, VE])
        tok_exp = small("tok_exp", [P, NC + 1, 96])
        tok_a = small("tok_a", [P, NC + 1, HEADS])
        decay = small("decay", [P, HEADS, NC + DB])
        row_bm = small("row_bm", [HEADS, T])
        m0 = small("m0", [HEADS, DB])
        m0t = small("m0t", [HEADS, DB])
        mprev = small("mprev", [HEADS, NC + DB])
        dlast = small("dlast", [HEADS, NC + DB])
        hden = small("hden", [P, HEADS])
        hrec = small("hrec", [P, HEADS])
        hss = small("hss", [P, HEADS])
        hvar = small("hvar", [P, HEADS])
        n0 = small("n0", [DB, HEADS * DK])
        n0T = small("n0T", [P, HEADS, DB])
        decay8 = small("decay8", [DB, HEADS])
        qm = small("qm", [P, DB, NS])
        nT_out = small("nT_out", [HEADS, DK])
        gate_q = place("gate_q", [P, T], F32, TMP + (4 * HEADS * VE + 31) // 32 * 32 + 3 * 2048)
        c0 = place("c0", [P, 2, DB, DK], F32, TAIL_AT)
        c0T = place("c0T", [P, DB, VE], F32, TAIL_AT + 2 * DB * DK * 4)
        c_out = place("c_out", [P, HEADS * VH, DK], F32, TAIL_AT + 2 * DB * DK * 4)
        cursor[0] = R_AT + (Z_O + CHUNK_O) * TB
        kwm = small("kwm", [NS, DB, DK])
        s_squares = small("s_squares", [NS, DV])
        s_num = small("s_num", [NS, VE])
        s_dt = small("s_dt", [NS, NS])
        s_wt = small("s_wt", [NS, NS])
        assert cursor[0] <= TAIL_AT
        cursor[0] = (TAIL_AT + (2 * DB * DK + DB * VE) * 4 + 31) // 32 * 32
        s_vt = small("s_vt", [NS, VE])
        s_kw = small("s_kw", [NS, DK])
        s_den = small("s_den", [NS, 1])
        s_rec = small("s_rec", [NS, 1])
        s_ss = small("s_ss", [NS, 1])
        s_var = small("s_var", [NS, 1])
        assert cursor[0] <= R_END

        cursor[0] = TMP + 2 * TB
        ln_gb = small("ln_gb", [P, 2, AT * P])
        ws_raw = small("ws_raw", [P, AT, P])
        wsT = small("wsT", [P, AT, P])
        ws_s = small("ws_s", [NS, AT, NS])
        bs_row = small("bs_row", [1, AT, P])
        vn = small("vn", [P, NC + 1, AT * P])
        ln_stats = small("ln_stats", [P, NC + 1, 6])
        ln_mvr = small("ln_mvr", [P, 3 * (NC + 1)])
        ln_mv, ln_rstd = ln_mvr[:, 0:2 * (NC + 1)].rearrange("p (c v) -> p c v", v=2), ln_mvr[:, 2 * (NC + 1):]
        pool_rows_p = small("pool_rows_p", [BUF, BT * P])
        WID = BUF + SEQ + DB * (BUF + DS)
        cursor[0] = TAIL_AT
        seg = small("seg", [P, WID])
        win_a = small("win_a", [P, WID])
        win_b = small("win_b", [P, WID])
        prev_raw = small("prev_raw", [DB * BUF, BT * P])
        prevT = small("prevT", [P, BT, DB * BUF])
        pooled = small("pooled", [P, T])
        pool_rows_s = small("pool_rows_s", [NS, BT * P])
        pool_w = place("pool_w_sb", [P, BT, P], F32, TMP + 2 * TB + 4096)

        ps = ctx.enter_context(nc.psum_tensor("ps", [P, 8, 512], F32))

        def pair(n):
            return ps[:, 2 * n:2 * n + 2, 0:H]

        def halves(t2):
            return t2.rearrange("p (b n) -> p b n", b=2)

        raw = [sem("raw0"), sem("raw1")]
        hi = [sem("hi0"), sem("hi1")]
        lo = [sem("lo0"), sem("lo1")]
        mm = [sem("mm0"), sem("mm1")]
        passed = sem("passed")
        s_const = sem("s_const")
        s_gain_in = sem("s_gain_in")
        s_gain_ps = sem("s_gain_ps")
        s_gains = sem("s_gains")
        s_gain = sem("s_gain")
        s_xin = sem("s_xin")
        s_x_ps = sem("s_x_ps")
        x_new_c = sem("x_chunk")
        s_dve0 = sem("s_dve0")
        st_zero = sem("st_zero")
        vt_ones = sem("vt_ones")
        merge1 = sem("merge1")
        x_new = sem("x_new")
        x_sq = sem("x_sq")
        x_ss = sem("x_ss")
        rs_var = sem("rs_var")
        rs_sqrt = sem("rs_sqrt")
        rs_inv = sem("rs_inv")
        h_f = sem("h_f")
        h_hi_s = sem("h_hi_s")
        h_lo_s = sem("h_lo_s")
        silu_s = sem("silu_s")
        gated = sem("gated")
        act_hi_s = sem("act_hi_s")
        act_lo_s = sem("act_lo_s")
        y_out = sem("y_out")
        ss_zero = sem("ss_zero")
        ss_add = sem("ss_add")
        ss_tot = sem("ss_tot")
        y_scaled = sem("y_scaled")
        z_out = sem("z_out")
        s_bias = sem("s_bias")
        s_m0 = sem("s_m0")
        row_in = sem("row_in")
        row_sp = sem("row_sp")
        row_done = sem("row_done")
        row_decay = sem("row_decay")
        decay_exp = sem("decay_exp")
        decay_ps = sem("decay_ps")
        decay_sb = sem("decay_sb")
        q_ps = sem("q_ps")
        tok_sb = sem("tok_sb")
        m_out = sem("m_out")
        link_a = sem("act_link")
        link_d = sem("dve_link")
        vk_ps = sem("vk_ps")
        vt_sb = sem("vt_sb")
        dt_sb = sem("dt_sb")
        kw_sb = sem("kw_sb")
        qk_ps = sem("qk_ps")
        wt_sb = sem("wt_sb")
        num_ps = sem("num_ps")
        num_sb = sem("num_sb")
        hss_s = sem("hss_s")
        hvar_s = sem("hvar_s")
        hstd_s = sem("hstd_s")
        hc_sb = sem("hc_sb")
        hct_ps = sem("hct_ps")
        hct_sb = sem("hct_sb")
        st_ps = sem("st_ps")
        st_sb = sem("st_sb")
        cT_ps = sem("cT_ps")
        cT_sb = sem("cT_sb")
        c_done = sem("c_done")
        s_in_ps = sem("s_in_ps")
        s_act = sem("s_act")
        s_dve = sem("s_dve")
        s_num_ps = sem("s_num_ps")
        s_num_sb = sem("s_num_sb")
        s_ss_s = sem("s_ss_s")
        s_var_s = sem("s_var_s")
        s_std_s = sem("s_std_s")
        s_h = sem("s_h")
        s_ht_ps = sem("s_ht_ps")
        s_ht_sb = sem("s_ht_sb")
        n0_in = sem("n0_in")
        n0_ps = sem("n0_ps")
        c0_in = [sem("c0_in0"), sem("c0_in1")]
        c0T_ps = sem("c0T_ps")
        c0T_sb = sem("c0T_sb")
        cu_ps = sem("cu_ps")
        cu_sb = sem("cu_sb")
        c0_done = [sem("c0_done0"), sem("c0_done1")]
        n0_sb = sem("n0_sb")
        n_done = sem("n_done")
        a_in = sem("a_in")
        ws_ps = sem("ws_ps")
        wsT_s = sem("wsT_s")
        wss_ps = sem("wss_ps")
        av_ps = sem("av_ps")
        av_sb = sem("av_sb")
        u_gelu = sem("u_gelu")
        ln_var = sem("ln_var")
        ln_std = sem("ln_std")
        vn_sb = sem("vn_sb")
        vn_done = sem("vn_done")
        mix_ps = sem("mix_ps")
        a_sb = sem("a_sb")
        prev_in = sem("prev_in")
        pw_in = sem("pw_in")
        prev_ps = sem("prev_ps")
        prev_sb = sem("prev_sb")
        prow_ps = sem("prow_ps")
        prow_sb = sem("prow_sb")
        prow_done = sem("prow_done")
        prev_done = sem("prev_done")
        seg_sb = sem("seg_sb")
        pooled_s = sem("pooled_s")
        pmix_ps = sem("pmix_ps")
        b_sb = sem("b_sb")
        a_hi_s = sem("a_hi_s")
        a_lo_s = sem("a_lo_s")
        b_hi_s = sem("b_hi_s")
        b_lo_s = sem("b_lo_s")
        o_sig = sem("o_sig")
        c_sb = sem("c_sb")
        c_hi_s = sem("c_hi_s")
        c_lo_s = sem("c_lo_s")
        sig_s = sem("sig_s")
        merged_s = sem("merged_s")
        merged_hi_s = sem("merged_hi_s")
        merged_lo_s = sem("merged_lo_s")
        xo_ps = sem("xo_ps")
        xo_sb = sem("xo_sb")
        xo_done = sem("xo_done")

        def cols(w, l, k0, kt, c0_, n=P):
            return w[bass.ds(l, 1), k0 * P:(k0 + kt) * P, bass.ds(c0_, n)].rearrange("a (k p) n -> p (a k) n", p=P)

        def tokens(ch):
            return (ch * P, P) if ch < NC else (SEQ, NS)

        bank = lambda i: ps[:, i, :]

        def apart(eng):
            eng.sem_inc(passed, 1)

        ctx.enter_context(nc.allow_non_contiguous_dma(reason="a few small transfers: gate biases, m, state rows"))
        block = ctx.enter_context(nc.Block())

        @block.sync
        def _(sp):
            def load(j, q, kt, src, n=P):
                sp.wait_ge(lo[j], q + 1)
                sp.dma_start(w_raw[:, j, 0:kt, 0:n], src).then_inc(raw[j], 16)

            def ffn(l, w_in, w_down, q0):
                with sp.Fori(0, FT) as m:
                    load(0, q0 + m, KD, cols(w_in, l, 0, KD, m * P))
                    load(1, q0 + m, KD, cols(w_in, l, 0, KD, DF + m * P))
                with sp.Fori(0, KD // 2) as i:
                    for n in range(2 * NCH):
                        m2, c = n // NCH, n % NCH
                        load(n % 2, q0 + FT + i * NCH + n // 2, CHUNKS[c],
                             cols(w_down, l, 8 * c, CHUNKS[c], i * 2 * P + m2 * P))

            with sp.Fori(0, DEPTH) as l:
                q0 = l * SLOT_USES
                ffn(l, a["ffn1_w_in"], a["ffn1_w_down"], q0 + Q_FFN1)
                load(0, q0 + Q_MIX, KD, cols(a["w_in"], l, 0, KD, COL_I, HEADS), HEADS)
                load(1, q0 + Q_MIX, KD, cols(a["w_in"], l, 0, KD, COL_F, HEADS), HEADS)
                n0_ = 0
                for t0, cnt in Z_RUNS:
                    with sp.Fori(0, cnt // 2) as i:
                        for j in range(2):
                            load(j, q0 + Q_MIX + 1 + n0_ // 2 + i, KD,
                                 cols(a["w_in"], l, 0, KD, (t0 + j) * P + i * 2 * P))
                    n0_ += cnt
                with sp.Fori(0, KD) as m:
                    load(0, q0 + Q_GATE + m, KD, cols(a["w_in"], l, 0, KD, COL_G + 2 * D + m * P))
                    load(1, q0 + Q_GATE + m, CT_, cols(a["proj_c"], l, 0, CT_, m * P))
                with sp.Fori(0, KD) as m:
                    for br, (w, kt) in enumerate((("proj_a", AT), ("proj_b", BT))):
                        q = q0 + Q_GATE + KD + 2 * m + br
                        load(0, q, KD, cols(a["w_in"], l, 0, KD, COL_G + br * D + m * P))
                        load(1, q, kt, cols(a[w], l, 0, kt, m * P))
                with sp.Fori(0, KD // 2) as i:
                    for j in range(2):
                        load(j, q0 + Q_OUT + i, KD, cols(a["w_out"], l, 0, KD, i * 2 * P + j * P))
                ffn(l, a["ffn2_w_in"], a["ffn2_w_down"], q0 + Q_FFN2)

        @block.gpsimd
        def _(pool):
            pool.memset(ident[:, :], 0.0).then_inc(s_const, 1)
            pool.memset(ones[:, :], 1.0).then_inc(s_const, 1)
            pool.memset(mask_p[:, :], 0.0).then_inc(s_const, 1)
            pool.memset(mask_s[:, :], 0.0).then_inc(s_const, 1)
            pool.memset(block01[:, :], 1.0).then_inc(s_const, 1)
            pool.memset(last01[:, :], 0.0).then_inc(s_const, 1)
            pool.memset(w_raw[:, 0, :, :], 0.0).then_inc(lo[0], 1)
            pool.memset(w_raw[:, 1, :, :], 0.0).then_inc(lo[1], 1)
            pool.memset(w_hi[:, 0, :, :].bitcast(F32), 0.0).then_inc(mm[0], 1)
            pool.memset(w_hi[:, 1, :, :].bitcast(F32), 0.0).then_inc(mm[1], 1)
            pool.memset(w_lo[:, :, :, :].bitcast(F32), 0.0).then_inc(s_const, 1)
            pool.iota(count_i[:, :], pattern=[[1, 16]], base=1, channel_multiplier=0).then_inc(s_const, 1)
            pool.wait_ge(s_const, 8)
            pool.affine_select(out=ident[:, :], in_=ident[:, :], compare_op=ALU.not_equal, fill=1.0, base=0,
                               pattern=[[-1, P]], channel_multiplier=1).then_inc(s_const, 1)
            pool.affine_select(out=mask_p[:, :], in_=mask_p[:, :], compare_op=ALU.is_ge, fill=NEG, base=0,
                               pattern=[[1, P]], channel_multiplier=-1).then_inc(s_const, 1)
            pool.affine_select(out=mask_s[:, :], in_=mask_s[:, :], compare_op=ALU.is_ge, fill=NEG, base=0,
                               pattern=[[1, NS]], channel_multiplier=-1).then_inc(s_const, 1)
            pool.affine_select(out=block01[:, :], in_=block01[:, :], compare_op=ALU.is_ge, fill=0.0, base=0,
                               pattern=[[-DS, DB]], channel_multiplier=1).then_inc(s_const, 1)
            pool.affine_select(out=last01[:, :], in_=last01[:, :], compare_op=ALU.not_equal, fill=1.0,
                               base=1 - DS, pattern=[[-DS, DB]], channel_multiplier=1).then_inc(s_const, 1)
            pool.wait_ge(s_const, 13)
            m3 = mask_s[:, :].rearrange("p (b t) -> p b t", b=DB)
            pool.affine_select(out=m3, in_=m3, compare_op=ALU.is_ge, fill=NEG, base=0,
                               pattern=[[-DS, DB], [0, DS]], channel_multiplier=1).then_inc(s_const, 1)
            pool.affine_select(out=block01[:, :], in_=block01[:, :], compare_op=ALU.is_ge, fill=0.0, base=DS - 1,
                               pattern=[[DS, DB]], channel_multiplier=-1).then_inc(s_const, 1)

            def lo_part(j, q, kt, n=P):
                pool.wait_ge(hi[j], q + 1)
                pool.tensor_tensor(w_lo[:, j, 0:kt, 0:n], w_raw[:, j, 0:kt, 0:n],
                                   w_hi[:, j, 0:kt, 0:n].bitcast(F32), ALU.subtract).then_inc(lo[j], 1)

            def ffn(q0):
                with pool.Fori(0, FT) as m:
                    lo_part(0, q0 + m, KD)
                    lo_part(1, q0 + m, KD)
                with pool.Fori(0, KD // 2) as i:
                    for n in range(2 * NCH):
                        lo_part(n % 2, q0 + FT + i * NCH + n // 2, CHUNKS[n % NCH])

            with pool.Fori(0, DEPTH) as l:
                q0 = l * SLOT_USES
                ffn(q0 + Q_FFN1)
                lo_part(0, q0 + Q_MIX, KD, HEADS)
                lo_part(1, q0 + Q_MIX, KD, HEADS)
                with pool.Fori(0, NZ // 2) as i:
                    for j in range(2):
                        lo_part(j, q0 + Q_MIX + 1 + i, KD)
                with pool.Fori(0, KD) as m:
                    lo_part(0, q0 + Q_GATE + m, KD)
                    lo_part(1, q0 + Q_GATE + m, CT_)
                with pool.Fori(0, KD) as m:
                    for br, kt in enumerate((AT, BT)):
                        lo_part(0, q0 + Q_GATE + KD + 2 * m + br, KD)
                        lo_part(1, q0 + Q_GATE + KD + 2 * m + br, kt)
                with pool.Fori(0, KD // 2) as i:
                    for j in range(2):
                        lo_part(j, q0 + Q_OUT + i, KD)
                ffn(q0 + Q_FFN2)

        @block.tensor
        def _(pe):
            def transpose(out, in_, n):
                return pe.transpose(out, in_, ident[0:n, 0:n])

            def unit(j, q, kt, n_ps, rhs_hi, rhs_lo, k0=0, first=True, last=True):
                pe.wait_ge(lo[j], q + 2)
                for k in range(kt):
                    for part, (w, r) in enumerate(((w_hi, rhs_hi), (w_hi, rhs_lo), (w_lo, rhs_hi))):
                        for b in range(2):
                            ins = pe.matmul(ps[:, 2 * n_ps + b, 0:H], w[:, j, k, :],
                                            r(k0 + k)[:, b * H:(b + 1) * H],
                                            start=first and k == 0 and part == 0,
                                            stop=last and k == kt - 1 and part == 2)
                ins.then_inc(mm[j], 1)

            def first_units(l, s, q, n_ps):
                for j in range(2):
                    pe.wait_ge(lo[j], q + 2)
                for k in range(KD):
                    pe.wait_ge(h_lo_s, (l * 3 + s) * KD + k + 1)
                    for j in range(2):
                        for part, (w, r) in enumerate(((w_hi, h_hi), (w_hi, h_lo), (w_lo, h_hi))):
                            for b in range(2):
                                ins = pe.matmul(ps[:, 2 * n_ps[j] + b, 0:H], w[:, j, k, :], r[:, k, b * H:(b + 1) * H],
                                                start=k == 0 and part == 0, stop=k == KD - 1 and part == 2)
                        if k == KD - 1:
                            ins.then_inc(mm[j], 1)

            hh = lambda k: h_hi[:, k, :]
            hl = lambda k: h_lo[:, k, :]

            def sum_rows(n_ps, src, start, stop):
                for b in range(2):
                    ins = pe.matmul(ps[:, 2 * n_ps + b, 0:H], ones[:, :], src[:, b * H:(b + 1) * H],
                                    start=start, stop=stop)
                return ins

            def pre_norm(l, s):
                nb = l * 3 + s
                for k in range(KD):
                    pe.wait_ge(x_sq, nb * KD + k + 1)
                    sum_rows(3, sq[k % 2][:, :], k == 0, k == KD - 1).then_inc(x_ss, 1)

            def post_norm(l, s):
                pe.wait_ge(ss_add, (l * 3 + s) * KD + KD + 2)
                sum_rows(2, ss_sum[:, :], True, True).then_inc(ss_tot, 1)

            def out_tiles(l, s, q0, chunks, rhs_hi, rhs_lo):
                n_ch = len(chunks)
                with pe.Fori(0, KD // 2) as i:
                    for m2 in range(2):
                        pe.wait_ge(y_out, (l * 3 + s) * KD + 2 * i + m2 + 1)
                        for c in range(n_ch):
                            n = m2 * n_ch + c
                            unit(n % 2, q0 + i * n_ch + n // 2, chunks[c], m2, rhs_hi, rhs_lo, 8 * c,
                                 c == 0, c == n_ch - 1)

            def ffn(l, f, q0):
                s = 2 * f
                pe.wait_ge(gated, l * PAIRS + G_FFN[f] + 1)
                first_units(l, s, q0, (0, 1))
                pe.wait_ge(gated, l * PAIRS + G_FFN[f] + 2)
                for j in range(2):
                    unit(j, q0 + 1, KD, 2 + j, hh, hl)
                with pe.Fori(1, FT // 2) as i:
                    for m2 in range(2):
                        pe.wait_ge(gated, l * PAIRS + G_FFN[f] + 2 * i + m2 + 1)
                        for j in range(2):
                            unit(j, q0 + 2 * i + m2, KD, 2 * m2 + j, hh, hl)
                pe.wait_ge(act_lo_s, (l * 2 + f + 1) * FT)
                apart(pe)
                out_tiles(l, s, q0 + FT, CHUNKS, lambda k: act_hi[:, k, :], lambda k: act_lo[:, k, :])

            pe.wait_ge(s_const, 15)
            pe.wait_ge(s_gain_in, 16 * 8 * DEPTH)
            NG = DEPTH * NGAIN
            transpose(bank(7)[:, 0:NG], gain_rows[:, :], NG).then_inc(s_gain_ps, 1)
            for ch in range(NC + 1):
                _, n = tokens(ch)
                pe.wait_ge(s_xin, 16 * (NC + 1))
                for k in range(KD):
                    if ch >= 3:
                        pe.wait_ge(x_new_c, ch - 2)
                    ins = transpose(ps[:, 2 * (ch % 3) + k // 4, (k % 4) * P:(k % 4) * P + n],
                                    x_in[0:n, ch, k * P:(k + 1) * P], n)
                ins.then_inc(s_x_ps, 1)

            with pe.Fori(0, DEPTH) as l:
                q0 = l * SLOT_USES
                pre_norm(l, 0)
                ffn(l, 0, q0 + Q_FFN1)
                post_norm(l, 0)
                pre_norm(l, 1)

                first_units(l, 1, q0 + Q_MIX, (2, 3))

                def z_tile(n, i=0, pair_=None, left=1):
                    pe.wait_ge(z_out, l * NZ + n + 2 * i + 2 - left)
                    unit(n % 2, q0 + Q_MIX + 1 + n // 2 + i, KD, n % 2 if pair_ is None else pair_, hh, hl)

                with pe.Fori(0, HEAD_START // 4) as i:
                    z_tile(0, i)
                    z_tile(1, i)
                pe.wait_ge(decay_exp, l + 1)
                for h in range(HEADS):
                    ins = pe.matmul(ps[:, 6, h * (NC + DB):(h + 1) * (NC + DB)],
                                    ident[0:HEADS, h:h + 1].broadcast_to([HEADS, P]), dlast[:, :],
                                    start=h == 0, stop=h == HEADS - 1, skip_group_check=True)
                ins.then_inc(decay_ps, 1)
                pe.wait_ge(row_done, l + 1)
                for ch in range(NC + 1):
                    t0, n = tokens(ch)
                    ins = transpose(ps[0:n, 4 + ch // 4, (ch % 4) * P:(ch % 4 + 1) * P], gate_q[:, t0:t0 + n], P)
                ins.then_inc(q_ps, 1)
                with pe.Fori(HEAD_START // 4, HEAD_START // 2) as i:
                    z_tile(0, i)
                    z_tile(1, i)

                pe.wait_ge(z_out, l * NZ + HEAD_START + 2)
                pe.wait_ge(tok_sb, l + 1)
                pe.wait_ge(decay_sb, l + 1)
                pe.wait_ge(n0_in, 16 * (l + 1))
                apart(pe)
                for h in range(HEADS):
                    transpose(ps[:, 2, h * DB:(h + 1) * DB], n0[:, h * DK:(h + 1) * DK], DB)
                pe.matmul(ps[0:DB, 3, 0:HEADS], last01[:, :], tok_exp[0:NS, NC, 0:HEADS], start=True, stop=True)\
                    .then_inc(n0_ps, 1)

                zn = HEAD_START
                n = P
                for ch in range(NC):
                    h = ch
                    t0 = ch * P
                    cc = l * NC + ch
                    hs = l * HEADS + h

                    def z_next():
                        nonlocal zn
                        z_tile(zn, pair_=0, left=0)
                        zn += 1

                    z_next()
                    if h:
                        pe.wait_ge(s_ht_sb, hs)
                    else:
                        pe.wait_ge(n0_sb, l + 1)
                    apart(pe)
                    for vh in range(VH):
                        transpose(ps[0:NS, 2, vh * P:(vh + 1) * P], z[:, Z_VAL + h * VH + vh, SEQ:T], P)
                    pe.matmul(ps[0:NS, 2, DV:DV + NS], ident[0:NS, 0:NS], mask_s[:, :], start=True, stop=False)
                    pe.matmul(ps[0:NS, 2, DV:DV + NS], ident[0:HEADS, h:h + 1].broadcast_to([HEADS, NS]), row_bm[:, SEQ:T],
                              start=False, stop=True)
                    transpose(ps[0:NS, 3, 0:DK], z[:, Z_K + h, SEQ:T], P)
                    pe.matmul(ps[0:NS, 3, DK:DK + NS], z[:, Z_K + h, SEQ:T], z[:, Z_Q + h, SEQ:T], start=True, stop=True)\
                        .then_inc(s_in_ps, 1)
                    if ch:
                        pe.wait_ge(hct_sb, cc)
                    apart(pe)
                    for i in range(CT_):
                        transpose(ps[:, 4 + i // 4, (i % 4) * P:(i % 4 + 1) * P], z[:, Z_VAL + i, t0:t0 + n], P)
                    for i in range(HEADS):
                        transpose(ps[:, 6, i * P:(i + 1) * P], z[:, Z_K + i, t0:t0 + n], P)
                    for i in range(HEADS):
                        pe.matmul(ps[:, 7, i * n:(i + 1) * n], ident[:, :], mask_p[:, :], start=i == 0,
                                  stop=False, skip_group_check=True)
                    for i in range(HEADS):
                        ins = pe.matmul(ps[:, 7, i * n:(i + 1) * n], ident[0:HEADS, i:i + 1].broadcast_to([HEADS, n]),
                                        row_bm[:, t0:t0 + n], start=False, stop=i == HEADS - 1, skip_group_check=True)
                    ins.then_inc(vk_ps, 1)
                    z_next()

                    def c0_transposed(vh):
                        pe.wait_ge(c0_in[vh], 16 * (hs + 1))
                        apart(pe)
                        for b in range(DB):
                            ins = transpose(ps[:, 2 + b // 4, (b % 4) * P:(b % 4 + 1) * P], c0[:, vh, b, :], P)
                        ins.then_inc(c0T_ps, 1)

                    pe.wait_ge(s_act, hs + 1)
                    pe.wait_ge(s_dve, hs + 1)
                    c0_transposed(0)
                    pe.wait_ge(vt_sb, cc + 1)
                    apart(pe)
                    for i in range(HEADS):
                        ins = pe.matmul(ps[:, 4, i * n:(i + 1) * n], z[:, Z_K + i, t0:t0 + n], z[:, Z_Q + i, t0:t0 + n],
                                        start=i == 0, stop=i == HEADS - 1, skip_group_check=True)
                    ins.then_inc(qk_ps, 1)
                    z_next()
                    pe.wait_ge(c0T_sb, hs * VH + 1)
                    c0_transposed(1)
                    pe.wait_ge(wt_sb, cc + 1)
                    pe.wait_ge(kw_sb, cc + 1)
                    pe.wait_ge(dt_sb, cc + 1)
                    if ch > 0:
                        pe.wait_ge(st_sb, l * NC + ch)
                    else:
                        pe.wait_ge(st_zero, l + 1)

                    def two_heads(r):
                        for h2 in range(2):
                            i = 2 * r + h2
                            pe.matmul(ps[:, 4 + h2, 0:VE], wt[:, i, :], vt[:, i, :], start=True, stop=True)
                            ins = pe.matmul(ps[:, 6 + h2, 0:VE], z[:, Z_Q + i, t0:t0 + n], state[:, i, :],
                                            start=True, stop=True)
                        ins.then_inc(num_ps, 1)

                    two_heads(0)
                    pe.wait_ge(c0T_sb, (hs + 1) * VH)
                    apart(pe)
                    pe.matmul(ps[0:NS, 2, 0:VE], s_wt[:, :], s_vt[:, :], start=True, stop=True)
                    pe.matmul(ps[0:DB, 2, 384:384 + DK], block01[:, :], s_kw[:, :], start=True, stop=True)
                    for b in range(DB):
                        ins = pe.matmul(ps[0:NS, 3, 0:VE], qm[:, b, :], c0T[:, b, :], start=b == 0, stop=b == DB - 1)
                    ins.then_inc(s_num_ps, 1)
                    pe.wait_ge(num_sb, l * 2 * NC + 2 * ch + 1)
                    two_heads(1)
                    z_next()

                    def c0_update(vh):
                        for b in range(2):
                            ins = pe.matmul(ps[:, 2 + b, :], s_vt[:, vh * P:(vh + 1) * P],
                                            kwm[:, b * (DB // 2):(b + 1) * (DB // 2), :], start=True, stop=True)
                        ins.then_inc(cu_ps, 1)

                    pe.wait_ge(s_num_sb, hs + 1)
                    c0_update(0)
                    pe.wait_ge(num_sb, l * 2 * NC + 2 * ch + 2)
                    for i in range(HEADS):
                        ins = pe.matmul(ps[:, 4 + i, 0:VE], kw[:, i, :], vt[:, i, :], start=True, stop=True)
                    ins.then_inc(st_ps, 1)
                    if ch == NC - 1:
                        z_next()
                    pe.wait_ge(cu_sb, hs * VH + 1)
                    c0_update(1)
                    pe.wait_ge(st_sb, l * NC + ch + 1)
                    pe.wait_ge(hc_sb, cc + 1)
                    apart(pe)
                    for i in range(CT_):
                        ins = transpose(ps[:, 4 + i // 4, (i % 4) * P:(i % 4 + 1) * P],
                                        num[:, i // VH, (i % VH) * P:(i % VH + 1) * P], n)
                    ins.then_inc(hct_ps, 1)
                    pe.wait_ge(cu_sb, (hs + 1) * VH)
                    pe.wait_ge(s_h, hs + 1)
                    apart(pe)
                    for vh in range(VH):
                        ins = transpose(ps[:, 2, vh * NS:(vh + 1) * NS], s_num[:, vh * P:(vh + 1) * P], NS)
                    ins.then_inc(s_ht_ps, 1)
                assert zn == CHUNK_END

                pe.wait_ge(hct_sb, (l + 1) * NC)
                apart(pe)
                for i in range(HEADS * VH):
                    h, vh = i // VH, i % VH
                    transpose(ps[:, 4 + i // 4, (i % 4) * P:(i % 4 + 1) * P], state[:, h, vh * P:(vh + 1) * P], P)
                transpose(ps[0:HEADS, 6, 0:P], state[:, :, DV:DV + 1].rearrange("p h o -> p (h o)"), P).then_inc(cT_ps, 1)
                pe.wait_ge(s_ht_sb, (l + 1) * HEADS)

                pe.wait_ge(a_in, 16 * 4 * (l + 1))
                pe.wait_ge(cT_sb, l + 1)
                for g in range(AT):
                    ins = transpose(ps[:, 6, g * P:(g + 1) * P], ws_raw[:, g, :], P)
                ins.then_inc(ws_ps, 1)
                for ch in range(NC + 1):
                    t0, n = tokens(ch)
                    bk = (4, 5, 4, 5, 7)[ch]
                    if ch in (2, 3):
                        pe.wait_ge(av_sb, l * (NC + 1) + ch - 1)
                    for g in range(AT):
                        ins = transpose(ps[0:n, bk, g * P:(g + 1) * P], z[:, Z_V + g, t0:t0 + n], P)
                    ins.then_inc(av_ps, 1)
                pe.wait_ge(wsT_s, l + 1)
                pe.matmul(ps[0:NS, 6, 0:AT * DS], rep8[:, :], wsT[0:DS, :, 0:DS], start=True, stop=True)\
                    .then_inc(wss_ps, 1)
                while zn < NZ:
                    z_tile(zn)
                    zn += 1

                def mix_a(ch):
                    t0, n = tokens(ch)
                    cc = l * (NC + 1) + ch
                    bk = 4 + ch % 2
                    pe.wait_ge(vn_sb, cc + 1)
                    if ch >= 2:
                        pe.wait_ge(a_sb, cc - 1)
                    for g in range(AT):
                        out = ps[:, bk, g * n:(g + 1) * n]
                        if ch < NC:
                            bias, weights = bs_row[0:1, g, :], wsT[:, g, :]
                        else:
                            bias, weights = bs_row[0:1, g:g + 1, 0:DS].broadcast_to([1, DB, DS]), ws_s[:, g, :]
                            out_b = out.rearrange("p (b t) -> p b t", b=DB)
                        pe.matmul(out if ch < NC else out_b, ones[0:1, :], bias, start=g == 0, stop=False,
                                  skip_group_check=True)
                        ins = pe.matmul(out, vn[0:n, ch, g * P:(g + 1) * P], weights, start=False,
                                        stop=g == AT - 1, skip_group_check=True)
                    ins.then_inc(mix_ps, 1)

                def rows_b():
                    pe.wait_ge(prev_in, 16 * (l + 1))
                    pe.wait_ge(a_sb, l * (NC + 1) + NC)
                    apart(pe)
                    NPREV = DB * BUF
                    for g in range(BT):
                        transpose(ps[:, 6, g * NPREV:(g + 1) * NPREV], prev_raw[:, g * P:(g + 1) * P], NPREV)
                    for g in range(BT):
                        transpose(ps[0:BUF, 7, g * P:(g + 1) * P], z[:, Z_B + g, SEQ - BUF:SEQ], P)
                    for g in range(BT):
                        ins = transpose(ps[0:NS, 5, g * P:(g + 1) * P], z[:, Z_B + g, SEQ:T], P)
                    ins.then_inc(prow_ps, 1)

                def mix_b(g):
                    gg = l * BT + g
                    if g == 0:
                        pe.wait_ge(pw_in, 16 * (l + 1))
                        pe.wait_ge(prow_sb, l + 1)
                    else:
                        pe.wait_ge(b_sb, gg)
                    pe.wait_ge(pooled_s, gg + 1)
                    for b in range(2):
                        ins = pe.matmul(ps[:, 6 + b, 0:H], pool_w[:, g, :], pooled[:, b * H:(b + 1) * H],
                                        start=True, stop=True)
                    ins.then_inc(pmix_ps, 1)

                between = {(0, 0): lambda: (mix_a(0), mix_a(1)), (0, 1): lambda: (mix_a(2), mix_a(3)),
                           (1, 0): lambda: (mix_a(4), rows_b())}
                for g in range(BT):
                    between[(2 + g, 0)] = lambda g=g: mix_b(g)
                for m in range(KD):
                    q = q0 + Q_GATE + m
                    if m == 0:
                        pe.wait_ge(z_out, l * NZ + NZ + 2)
                    else:
                        pe.wait_ge(sig_s, l * 3 * KD + m)
                    unit(0, q, KD, 1, hh, hl)
                    if (m, 0) in between:
                        between[(m, 0)]()
                    if m == 0:
                        pe.wait_ge(c_lo_s, (l + 1) * CT_)
                    else:
                        pe.wait_ge(gated, l * PAIRS + G_MIX + m + 2)
                    unit(1, q, CT_, 0, lambda k: c_hi[:, k, :], lambda k: c_lo[:, k, :])
                    if (m, 1) in between:
                        between[(m, 1)]()

                pe.wait_ge(a_lo_s, l + 1)
                pe.wait_ge(b_lo_s, l + 1)
                pe.wait_ge(gated, l * PAIRS + G_MIX + KD + 2)
                apart(pe)
                branches = ((a_hi, a_lo, AT), (b_hi, b_lo, BT))
                with pe.Fori(0, KD // 2) as i:
                    for m2 in range(2):
                        for br, (bh, bl, kt) in enumerate(branches):
                            n = 2 * m2 + br
                            pe.wait_ge(gated, l * PAIRS + G_MIX + KD + 4 * i + n + 1)
                            q = q0 + Q_GATE + KD + 4 * i + n
                            unit(0, q, KD, 2 * (n % 2), hh, hl)
                            unit(1, q, kt, 2 * (n % 2) + 1, lambda k: bh[:, k, :], lambda k: bl[:, k, :])
                pe.wait_ge(merged_lo_s, (l + 1) * KD)
                apart(pe)
                out_tiles(l, 1, q0 + Q_OUT, [KD], lambda k: merged_hi[:, k, :],
                          lambda k: (merged_lo0 if k < KD // 2 else merged_lo1)[:, k % (KD // 2), :])
                post_norm(l, 1)
                pre_norm(l, 2)
                ffn(l, 1, q0 + Q_FFN2)
                post_norm(l, 2)

            pe.wait_ge(x_new, (DEPTH * 3 + 1) * KD)
            for ch in range(NC + 1):
                t0, n = tokens(ch)
                if ch >= 3:
                    pe.wait_ge(xo_sb, ch - 2)
                for k in range(KD):
                    ins = transpose(ps[0:n, 2 * (ch % 3) + k // 4, (k % 4) * P:(k % 4 + 1) * P],
                                    xT[:, k, t0:t0 + n], P)
                ins.then_inc(xo_ps, 1)

        @block.scalar
        def _(act):
            act_steps = 2

            class Link:
                def __init__(self, l):
                    self.base, self.n = l * act_steps, 0

                def __call__(self, ins):
                    self.n += 1
                    ins.then_inc(link_a, 1)
                    act.wait_ge(link_a, self.base + self.n)

            def pre_norm(l, s):
                nb = l * 3 + s
                for k in range(KD):
                    act.wait_ge(x_new, nb * KD + k + 1)
                    if k >= 2:
                        act.wait_ge(x_ss, nb * KD + k - 1)
                    act.activation(sq[k % 2][:, :], xT[:, k, :], ACT.Square).then_inc(x_sq, 1)
                root(2 * nb)
                for k in range(KD):
                    act.wait_ge(h_f, nb * KD + k + 1)
                    act.activation(h_hi[:, k, :], prod[k % 2][:, :], ACT.Copy).then_inc(h_hi_s, 1)

            def hi_part(j, q):
                act.wait_ge(raw[j], (q + 1) * 16)
                act.wait_ge(mm[j], q + 1)
                act.activation(w_hi[:, j, :, :], w_raw[:, j, :, :], ACT.Copy).then_inc(hi[j], 1)

            def root(ri):
                act.wait_ge(rs_var, ri + 1)
                act.activation(rstd[:, :], rstd[:, :], ACT.Sqrt).then_inc(rs_sqrt, 1)

            def out_tiles(l, s, q0, n_ch):
                yb = (l * 3 + s) * KD

                def two_tiles(i, left):
                    for m2 in range(2):
                        for c in range(n_ch):
                            n = m2 * n_ch + c
                            if n < left:
                                hi_part(n % 2, q0 + i * n_ch + n // 2 + 1)
                        act.wait_ge(mm[n % 2], q0 + i * n_ch + n // 2 + 2)
                        act.activation(yT[:, bass.ds(2 * i + m2, 1), :].rearrange("p a (b n) -> p (a b) n", b=2),
                                       pair(m2), ACT.Copy)
                        act.wait_ge(ss_add, yb + 2 * i + m2 + 1)
                        act.activation(halves(sq[m2][:, :]), pair(m2), ACT.Square).then_inc(y_out, 1)

                whole = KD // 2 if s < 2 else KD // 2 - 1
                with act.Fori(0, whole) as i:
                    two_tiles(i, 2 * n_ch)
                if s == 2:
                    two_tiles(whole, 2 * n_ch - 2)

            def ffn(l, f, q0):
                with act.Fori(0, FT // 2) as i:
                    for m2 in range(2):
                        pg = l * PAIRS + G_FFN[f] + 2 * i + m2
                        hi_part(0, q0 + 2 * i + m2 + 1)
                        hi_part(1, q0 + 2 * i + m2 + 1)
                        act.wait_ge(gated, pg + 1)
                        act.activation(halves(gate_act[m2][:, :]), pair(2 * m2), ACT.Silu).then_inc(silu_s, 1)
                        act.wait_ge(gated, pg + 3)
                        act.activation(act_hi[:, bass.ds(2 * i + m2, 1), :].rearrange("p a n -> p (a n)"),
                                       prod[m2][:, :], ACT.Copy).then_inc(act_hi_s, 1)
                out_tiles(l, 2 * f, q0 + FT, NCH)

            for ch in range(NC + 1):
                t0, n = tokens(ch)
                src = a["x_prompt"][0, t0:t0 + n, :] if ch < NC else a["x_sample"].rearrange("b t d -> (b t) d")
                act.dma_start(x_in[0:n, ch, :], src).then_inc(s_xin, 16)
            kinds = ["ffn1_norm_pre", "ffn1_norm_post", "mix_norm_pre", "mix_norm_post", "ffn2_norm_pre",
                     "ffn2_norm_post", "pool_scale", "mlstm_norm_g"]
            for l0 in range(DEPTH):
                r0 = l0 * NGAIN
                for kind in kinds:
                    n = a[kind].shape[1] // P
                    act.dma_start(gain_rows[r0:r0 + n, :], a[kind][l0].rearrange("(k p) -> k p", p=P))\
                        .then_inc(s_gain_in, 16)
                    r0 += n
            act.wait_ge(s_gain_ps, 1)
            act.activation(gains[:, :], bank(7)[:, 0:DEPTH * NGAIN], ACT.Copy).then_inc(s_gains, 1)
            for ch in range(NC + 1):
                t0, n = tokens(ch)
                act.wait_ge(s_x_ps, ch + 1)
                for half in range(2):
                    src = ps[:, 2 * (ch % 3) + half, :].rearrange("p (k n) -> p k n", k=4)[:, :, 0:n]
                    ins = act.activation(xT[:, 4 * half:4 * half + 4, t0:t0 + n], src, ACT.Copy)
                ins.then_inc(x_new_c, 1)
            act.wait_ge(x_new_c, NC + 1)
            act.wait_ge(s_const, 15)
            for k in range(KD):
                act.activation(rstd[:, 16 + k:17 + k], ones[:, k:k + 1], ACT.Copy).then_inc(x_new, 1)

            with act.Fori(0, DEPTH) as l:
                link = Link(l)
                q0 = l * SLOT_USES
                hi_part(0, q0)
                hi_part(1, q0)
                pre_norm(l, 0)
                ffn(l, 0, q0 + Q_FFN1)
                root(2 * (l * 3) + 1)
                pre_norm(l, 1)

                lsl = bass.ds(l, 1)
                act.dma_start(i_bias[:, :], a["mlstm_i_bias"][lsl, :].rearrange("a h -> h a")).then_inc(s_bias, 16)
                act.dma_start(f_bias[:, :], a["mlstm_f_bias"][lsl, :].rearrange("a h -> h a")).then_inc(s_bias, 16)
                act.dma_start(m0[:, :], a["state_mlstm_m"][lsl, :, :].rearrange("a b h -> h (a b)")).then_inc(s_m0, 16)
                act.dma_start(n0[:, :], a["state_mlstm_n"][lsl].rearrange("a b h k -> (a b) (h k)")).then_inc(n0_in, 16)
                for j in range(2):
                    hi_part(j, q0 + Q_MIX + 1)
                act.wait_ge(row_in, l + 1)
                link(act.activation(row_softplus[:, :], row_f[:, :], ACT.Abs))
                link(act.activation(row_softplus[:, :], row_softplus[:, :], ACT.Exp, scale=-1.0))
                act.activation(row_softplus[:, :], row_softplus[:, :], ACT.Ln, bias=ones[0:HEADS, 0:1]).then_inc(row_sp, 1)

                def z_tile(n, t, i=0, pair_=None):
                    hi_part(n % 2, q0 + Q_MIX + 1 + n // 2 + i + 1)
                    dst = z[:, bass.ds(t + 2 * i, 1), :].rearrange("p a (b n) -> p (a b) n", b=2)
                    act.activation(dst, pair(n % 2 if pair_ is None else pair_), ACT.Copy).then_inc(z_out, 1)

                with act.Fori(0, HEAD_START // 4) as i:
                    z_tile(0, Z_Q, i)
                    z_tile(1, Z_Q + 1, i)
                act.wait_ge(row_decay, l + 1)
                act.activation(dlast[:, :], dlast[:, :], ACT.Exp).then_inc(decay_exp, 1)
                act.wait_ge(row_done, l + 1)
                act.dma_start(o["m_prompt"][lsl, 0, :].rearrange("a h -> h a"), row_m[:, SEQ - 1:SEQ]).then_inc(m_out, 16)
                act.dma_start(o["m_sample"][lsl, :, :].rearrange("a b h -> h (a b)"),
                              row_m[:, SEQ + DS - 1:T:DS]).then_inc(m_out, 16)
                act.wait_ge(q_ps, l + 1)
                tp = ps[:, 4, :].rearrange("p (c n) -> p c n", c=NC)
                act.activation(tok_exp[:, 0:NC, :], tp[:, :, 32:P], ACT.Exp)
                act.activation(tok_a[:, 0:NC, :], tp[:, :, 0:HEADS], ACT.Copy)
                act.activation(tok_exp[0:NS, NC, :], ps[0:NS, 5, 32:P], ACT.Exp)
                act.activation(tok_a[0:NS, NC, :], ps[0:NS, 5, 0:HEADS], ACT.Copy).then_inc(tok_sb, 1)
                with act.Fori(HEAD_START // 4, HEAD_START // 2) as i:
                    z_tile(0, Z_Q, i)
                    z_tile(1, Z_Q + 1, i)
                act.wait_ge(m_out, 32 * (l + 1))

                def load_c0(h, vh):
                    src = a["state_mlstm_C"][lsl, :, h, vh * P:(vh + 1) * P, :]
                    act.dma_start(c0[:, vh, :, :], src.rearrange("a b v k -> v (a b) k")).then_inc(c0_in[vh], 16)

                load_c0(0, 0)
                load_c0(0, 1)
                zn = HEAD_START
                for ch in range(NC):
                    h = ch
                    t0, n = ch * P, P
                    cc = l * NC + ch
                    hs = l * HEADS + h

                    def z_next():
                        nonlocal zn
                        z_tile(zn, Z_ORDER[zn], pair_=0)
                        zn += 1

                    z_next()
                    if h:
                        act.wait_ge(c0_done[1], 16 * hs)
                        load_c0(h, 1)
                    act.wait_ge(s_in_ps, hs + 1)
                    if ch == 0:
                        act.wait_ge(vt_ones, l + 1)
                        act.wait_ge(tok_sb, l + 1)
                    act.activation(s_vt[:, 0:DV], ps[0:NS, 2, 0:DV], ACT.Copy)
                    act.activation(s_dt[:, :], ps[0:NS, 2, DV:DV + NS], ACT.Exp, bias=tok_a[0:NS, NC, h:h + 1]).then_inc(s_act, 1)
                    act.wait_ge(vk_ps, cc + 1)
                    if ch:
                        act.wait_ge(st_ps, l * NC + ch)
                    for i in range(2):
                        src = ps[:, 4 + i, :].rearrange("p (h v) -> p h v", h=2)
                        ins = act.activation(vt[:, 2 * i:2 * i + 2, 0:DV], src, ACT.Copy)
                    ins.then_inc(vt_sb, 1)
                    for i in range(HEADS):
                        ins = act.activation(dt_[:, i, :], ps[:, 7, i * n:(i + 1) * n], ACT.Exp, bias=tok_a[:, ch, i:i + 1])
                    ins.then_inc(dt_sb, 1)
                    z_next()
                    for vh in range(VH):
                        act.wait_ge(c0T_ps, hs * VH + vh + 1)
                        if vh == 0:
                            act.wait_ge(n0_sb, l + 1)
                            act.activation(c0T[:, :, DV], n0T[:, h, :], ACT.Copy)
                        for b in range(2):
                            ins = act.activation(c0T[:, 4 * b:4 * b + 4, vh * P:(vh + 1) * P],
                                                 ps[:, 2 + b, :].rearrange("p (b k) -> p b k", b=4), ACT.Copy)
                        ins.then_inc(c0T_sb, 1)
                        if vh == 0:
                            z_next()
                    act.wait_ge(s_num_sb, hs + 1)
                    act.activation(s_squares[:, :], s_num[:, 0:DV], ACT.Square, accum_out=s_ss[:, :]).then_inc(s_ss_s, 1)
                    act.wait_ge(num_sb, l * 2 * NC + 2 * ch + 2)
                    for i in range(HEADS):
                        ins = act.activation(squares[:, i, :], num[:, i, 0:DV], ACT.Square, accum_out=hss[:, i:i + 1])
                    ins.then_inc(hss_s, 1)
                    act.wait_ge(s_var_s, hs + 1)
                    act.activation(s_var[:, :], s_var[:, :], ACT.Sqrt).then_inc(s_std_s, 1)
                    act.wait_ge(hvar_s, cc + 1)
                    act.activation(hvar[:, :], hvar[:, :], ACT.Sqrt).then_inc(hstd_s, 1)
                    z_next()

                    def store_c0(vh):
                        act.wait_ge(cu_sb, hs * VH + vh + 1)
                        dst = o["C_sample"][lsl, :, h, vh * P:(vh + 1) * P, :]
                        act.dma_start(dst.rearrange("a b v k -> v (a b) k"), c0[:, vh, :, :]).then_inc(c0_done[vh], 16)

                    store_c0(0)
                    if ch == NC - 1:
                        z_next()
                    store_c0(1)
                    act.wait_ge(hct_ps, cc + 1)
                    for i in range(2):
                        src = ps[:, 4 + i, 0:4 * n].rearrange("p (c n) -> p c n", c=4)
                        ins = act.activation(z[:, Z_VAL + 4 * i:Z_VAL + 4 * i + 4, t0:t0 + n], src, ACT.Copy)
                    ins.then_inc(hct_sb, 1)
                    act.wait_ge(s_ht_ps, hs + 1)
                    act.activation(z[:, Z_VAL + VH * h:Z_VAL + VH * (h + 1), SEQ:T],
                                   ps[:, 2, 0:VH * NS].rearrange("p (c n) -> p c n", c=VH), ACT.Copy).then_inc(s_ht_sb, 1)
                    if h < HEADS - 1:
                        act.wait_ge(c0_done[0], 16 * (hs + 1))
                        load_c0(h + 1, 0)
                act.wait_ge(cT_ps, l + 1)
                act.activation(c_out[:, 0:4, :], ps[:, 4, :].rearrange("p (i k) -> p i k", i=4), ACT.Copy)
                act.activation(c_out[:, 4:8, :], ps[:, 5, :].rearrange("p (i k) -> p i k", i=4), ACT.Copy)
                act.activation(nT_out[:, :], ps[0:HEADS, 6, 0:P], ACT.Copy).then_inc(cT_sb, 1)
                act.wait_ge(cT_sb, l + 1)
                act.dma_start(o["C_prompt"][lsl, 0].rearrange("a h (w v) k -> v (a h w) k", v=P),
                              c_out[:, :, :]).then_inc(c_done, 16)
                act.dma_start(o["n_prompt"][lsl, 0].rearrange("a h k -> (a h) k"), nT_out[:, :]).then_inc(c_done, 16)
                act.dma_start(o["n_sample"][lsl].rearrange("a b h k -> (a b) (h k)"), n0[:, :]).then_inc(n_done, 16)

                act.wait_ge(n_done, 16 * (l + 1))
                act.dma_start(ws_raw[:, :, :], a["gmlp_w_s"][lsl].rearrange("a g t s -> t (a g) s")).then_inc(a_in, 16)
                act.dma_start(bs_row[:, :, :], a["gmlp_b_s"][lsl]).then_inc(a_in, 16)
                act.dma_start(ln_gb[:, 0, :], a["gmlp_ln_g"][lsl, :].broadcast_to([P, AT * P])).then_inc(a_in, 16)
                act.dma_start(ln_gb[:, 1, :], a["gmlp_ln_b"][lsl, :].broadcast_to([P, AT * P])).then_inc(a_in, 16)
                act.wait_ge(c_done, 32 * (l + 1))
                act.dma_start(prev_raw[:, :], a["state_pool"][lsl].rearrange("a b r c -> (a b r) c")).then_inc(prev_in, 16)
                act.dma_start(o["pool_sample"][lsl, :, 0:BUF - DS, :], a["state_pool"][lsl, :, DS:BUF, :]).then_inc(prow_done, 16)
                for ch in range(NC + 1):
                    t0, n = tokens(ch)
                    bk = (4, 5, 4, 5, 7)[ch]
                    act.wait_ge(av_ps, l * (NC + 1) + ch + 1)
                    act.activation(vn[0:n, ch, :], ps[0:n, bk, :], ACT.Gelu_apprx_tanh).then_inc(av_sb, 1)
                act.activation(z[:, Z_U:Z_U + AT, :], z[:, Z_U:Z_U + AT, :], ACT.Gelu_apprx_tanh).then_inc(u_gelu, 1)
                act.wait_ge(ln_var, l + 1)
                act.activation(ln_rstd, ln_rstd, ACT.Sqrt).then_inc(ln_std, 1)

                def sigmoid_o(t0, t1):
                    act.activation(z[:, Z_O + t0:Z_O + t1, :], z[:, Z_O + t0:Z_O + t1, :], ACT.Sigmoid).then_inc(o_sig, 1)

                def c_hi_parts(t0, t1):
                    for t in range(t0, t1):
                        act.wait_ge(c_sb, l * CT_ + t + 1)
                        act.activation(c_hi[:, t, :], z[:, Z_O + t, :], ACT.Copy).then_inc(c_hi_s, 1)

                sigmoid_o(0, CHUNK_O)
                z_tile(zn, Z_ORDER[zn])
                zn += 1
                c_hi_parts(0, CHUNK_O)
                act.wait_ge(wsT_s, l + 1)
                act.dma_start(pool_w[:, :, :], a["pool_w"][lsl].rearrange("a g c d -> c (a g) d")).then_inc(pw_in, 16)
                while zn < NZ:
                    z_tile(zn, Z_ORDER[zn])
                    zn += 1
                act.wait_ge(z_out, (l + 1) * NZ + 2)
                sigmoid_o(CHUNK_O, CT_)
                c_hi_parts(CHUNK_O, CT_)
                NPREV = DB * BUF

                def rows_b():
                    act.wait_ge(prow_ps, l + 1)
                    act.activation(prevT[:, :, :], ps[:, 6, 0:BT * NPREV].rearrange("p (g r) -> p g r", g=BT), ACT.Copy)
                    act.activation(pool_rows_p[:, :], ps[0:BUF, 7, :], ACT.Copy)
                    act.activation(pool_rows_s[:, :], ps[0:NS, 5, :], ACT.Copy).then_inc(prow_sb, 1)
                    act.wait_ge(prow_sb, l + 1)
                    act.dma_start(o["pool_prompt"][lsl, 0].rearrange("a r c -> (a r) c"), pool_rows_p[:, :]).then_inc(prow_done, 16)
                    act.dma_start(o["pool_sample"][lsl, :, BUF - DS:BUF, :], pool_rows_s[:, :]).then_inc(prow_done, 16)
                    act.dma_start(o["gmlp_v_sample"][lsl].rearrange("a b t c -> (a b t) c"), vn[0:NS, NC, :]).then_inc(vn_done, 16)

                def seg_b(g):
                    gg = l * BT + g
                    if g:
                        act.wait_ge(pooled_s, gg)
                    act.activation(seg[:, BUF:BUF + SEQ], z[:, Z_B + g, 0:SEQ], ACT.Copy)
                    ss = seg[:, BUF + SEQ:WID].rearrange("p (b r) -> p b r", b=DB)
                    act.activation(ss[:, :, 0:BUF], prevT[:, g, :].rearrange("p (b r) -> p b r", b=DB), ACT.Copy)
                    act.activation(ss[:, :, BUF:BUF + DS], z[:, Z_B + g, SEQ:T].rearrange("p (b t) -> p b t", b=DB),
                                   ACT.Copy).then_inc(seg_sb, 1)

                for m in range(KD):
                    hi_part(0, q0 + Q_GATE + m + 1)
                    act.wait_ge(gated, l * PAIRS + G_MIX + m + 1)
                    act.activation(halves(gate_act[m % 2][:, :]), pair(1), ACT.Sigmoid).then_inc(sig_s, 1)
                    if m == 1:
                        rows_b()
                    if 1 <= m <= BT:
                        seg_b(m - 1)
                    if m == KD - 2:
                        act.wait_ge(a_sb, (l + 1) * (NC + 1))
                        act.activation(a_hi[:, :, :], z[:, Z_U:Z_U + AT, :], ACT.Copy).then_inc(a_hi_s, 1)
                        act.wait_ge(b_sb, (l + 1) * BT)
                        act.wait_ge(prow_done, 48 * (l + 1))
                        act.activation(b_hi[:, :, :], z[:, Z_B:Z_B + BT, :], ACT.Copy).then_inc(b_hi_s, 1)
                    hi_part(1, q0 + Q_GATE + m + 1)
                act.wait_ge(vn_done, 16 * (l + 1))
                for half in range(2):
                    with act.Fori(2 * half, 2 * half + 2) as i:
                        for m2 in range(2):
                            for br in range(2):
                                n = 2 * m2 + br
                                for j in range(2):
                                    hi_part(j, q0 + Q_GATE + KD + 4 * i + n + 1)
                                act.wait_ge(gated, l * PAIRS + G_MIX + KD + 4 * i + n + 1)
                                act.activation(halves(gate_act[n % 2][:, :]), pair(2 * (n % 2)), ACT.Sigmoid)\
                                    .then_inc(sig_s, 1)
                            act.wait_ge(merged_s, l * KD + 2 * i + m2 + 1)
                            act.activation(merged_hi[:, bass.ds(2 * i + m2, 1), :].rearrange("p a n -> p (a n)"),
                                           sq[m2][:, :], ACT.Copy).then_inc(merged_hi_s, 1)
                out_tiles(l, 1, q0 + Q_OUT, 1)
                root(2 * (l * 3 + 1) + 1)
                pre_norm(l, 2)
                ffn(l, 1, q0 + Q_FFN2)
                root(2 * (l * 3 + 2) + 1)

            for ch in range(NC + 1):
                t0, n = tokens(ch)
                act.wait_ge(xo_ps, ch + 1)
                act.activation(x_in[0:n, ch, 0:512], ps[0:n, 2 * (ch % 3), :], ACT.Copy)
                act.activation(x_in[0:n, ch, 512:1024], ps[0:n, 2 * (ch % 3) + 1, :], ACT.Copy).then_inc(xo_sb, 1)
                act.wait_ge(xo_sb, ch + 1)
                dst = o["y_prompt"][0, t0:t0 + n, :] if ch < NC else o["y_sample"].rearrange("b t d -> (b t) d")
                act.dma_start(dst, x_in[0:n, ch, :]).then_inc(xo_done, 16)
            act.wait_ge(xo_done, 16 * (NC + 1))
            act.wait_ge(m_out, 32 * DEPTH)
            act.wait_ge(c_done, 32 * DEPTH)
            act.wait_ge(n_done, 16 * DEPTH)
            act.wait_ge(vn_done, 16 * DEPTH)
            act.wait_ge(prow_done, 48 * DEPTH)
            for vh in range(VH):
                act.wait_ge(c0_done[vh], 16 * HEADS * DEPTH)

        @block.vector
        def _(dve):
            class Link:
                def __init__(self, l):
                    self.base, self.n = l * DVE_STEPS, 0

                def __call__(self, ins, alone=False):
                    self.n += 1
                    ins.then_inc(link_d, 1)
                    dve.wait_ge(link_d, self.base + self.n)
                    if alone:
                        apart(dve)

            def recip_root(n_ps, ri):
                dve.tensor_scalar(halves(rstd[:, :]), pair(n_ps), 1.0 / D, EPS, ALU.mult, ALU.add).then_inc(rs_var, 1)
                dve.wait_ge(rs_sqrt, ri + 1)
                dve.reciprocal(rstd[:, :], rstd[:, :]).then_inc(rs_inv, 1)
                dve.wait_ge(rs_inv, ri + 1)

            def pre_norm(l, s):
                nb = l * 3 + s
                dve.wait_ge(x_ss, nb * KD + KD)
                recip_root(3, 2 * nb)
                for k in range(KD + 1):
                    if k < KD:
                        if k >= 2:
                            dve.wait_ge(h_lo_s, nb * KD + k - 1)
                        g = G_PRE[s] + k
                        dve.scalar_tensor_tensor(out=prod[k % 2][:, :], in0=xT[:, k, :], scalar=gain[:, g:g + 1],
                                                 in1=rstd[:, :], op0=ALU.mult, op1=ALU.mult).then_inc(h_f, 1)
                    if k:
                        dve.wait_ge(h_hi_s, nb * KD + k)
                        dve.tensor_tensor(h_lo[:, k - 1, :], prod[(k - 1) % 2][:, :], h_hi[:, k - 1, :].bitcast(F32),
                                          ALU.subtract).then_inc(h_lo_s, 1)

            def post_norm(l, s):
                nb = l * 3 + s
                dve.wait_ge(ss_tot, nb + 1)
                recip_root(2, 2 * nb + 1)
                for k in range(KD + 1):
                    if k < KD:
                        g = G_POST[s] + k
                        dve.scalar_tensor_tensor(out=yT[:, k, :], in0=yT[:, k, :], scalar=gain[:, g:g + 1],
                                                 in1=rstd[:, :], op0=ALU.mult, op1=ALU.mult).then_inc(y_scaled, 1)
                    if k:
                        dve.wait_ge(y_scaled, nb * KD + k)
                        dve.tensor_tensor(xT[:, k - 1, :], xT[:, k - 1, :], yT[:, k - 1, :], ALU.add).then_inc(x_new, 1)

            def out_tiles(l, s):
                nb = l * 3 + s
                dve.memset(ss_sum[:, :], 0.0).then_inc(ss_zero, 1)
                dve.wait_ge(ss_zero, nb + 1)
                apart(dve)
                with dve.Fori(0, KD // 2) as i:
                    for m2 in range(2):
                        dve.wait_ge(y_out, nb * KD + 2 * i + m2 + 3)
                        dve.wait_ge(ss_add, nb * KD + 2 * i + m2 + 2)
                        dve.tensor_tensor(ss_sum[:, :], ss_sum[:, :], sq[m2][:, :], ALU.add).then_inc(ss_add, 1)

            def ffn(l, f):
                apart(dve)
                with dve.Fori(0, FT // 2) as i:
                    for m2 in range(2):
                        pf = (l * 2 + f) * FT + 2 * i + m2
                        dve.wait_ge(silu_s, pf + 1)
                        dve.tensor_tensor(halves(prod[m2][:, :]), halves(gate_act[m2][:, :]), pair(2 * m2 + 1),
                                          ALU.mult).then_inc(gated, 1)
                        dve.wait_ge(act_hi_s, pf + 1)
                        sel = bass.ds(2 * i + m2, 1)
                        dve.tensor_tensor(act_lo[:, sel, :].rearrange("p a n -> p (a n)"), prod[m2][:, :],
                                          act_hi[:, sel, :].bitcast(F32).rearrange("p a n -> p (a n)"),
                                          ALU.subtract).then_inc(act_lo_s, 1)
                out_tiles(l, 2 * f)

            dve.wait_ge(s_const, 15)
            dve.tensor_copy(rep8[:, :].rearrange("p (b t) -> p b t", b=DB),
                            ident[0:DS, 0:DS].unsqueeze(1).broadcast_to([DS, DB, DS])).then_inc(s_dve0, 1)
            for g, w in enumerate(POOL_WINDOWS):
                dve.tensor_scalar(recip16[:, g, :], count_i[:, :], float(w), None, ALU.min).then_inc(s_dve0, 1)
            dve.wait_ge(s_dve0, 1 + BT)
            dve.reciprocal(recip16[:, :, :], recip16[:, :, :]).then_inc(s_dve0, 1)
            for i, s_ in enumerate((gated, y_out, ss_add, z_out)):
                for j in range(2):
                    dve.memset(rstd[:, 2 * i + j:2 * i + j + 1], 0.0).then_inc(s_, 1)

            with dve.Fori(0, DEPTH) as l:
                link = Link(l)
                dve.wait_ge(s_gains, 1)
                dve.tensor_copy(gain[:, :], gains[:, bass.ds(l * NGAIN, NGAIN)]).then_inc(s_gain, 1)
                dve.wait_ge(s_gain, 2 * l + 1)
                for s in (0, 2):
                    g = gain[:, G_POST[s]:G_POST[s] + KD]
                    ins = dve.tensor_scalar(g, g, 0.5, None, ALU.mult)
                ins.then_inc(s_gain, 1)
                dve.wait_ge(s_gain, 2 * l + 2)
                pre_norm(l, 0)
                ffn(l, 0)
                post_norm(l, 0)
                pre_norm(l, 1)

                dve.memset(row_reset[:, :], 1.0)
                dve.memset(gate_q[:, :], 0.0)
                dve.memset(qm[:, :, :], 0.0)
                dve.memset(state[:, :, :], 0.0).then_inc(st_zero, 1)
                dve.memset(s_vt[:, DV:VE], 1.0)
                dve.memset(vt[:, :, DV], 1.0).then_inc(vt_ones, 1)
                link(dve.memset(mprev[:, :], 0.0))
                dve.memset(row_reset[:, 0:SEQ:P], 0.0)
                link(dve.memset(row_reset[:, SEQ:T:DS], 0.0))
                dve.wait_ge(mm[0], l * SLOT_USES + Q_MIX + 2)
                dve.wait_ge(mm[1], l * SLOT_USES + Q_MIX + 2)
                dve.wait_ge(s_bias, 32 * (l + 1))
                dve.tensor_scalar(halves(row_i[:, :]), pair(2)[0:HEADS], i_bias[:, 0:1], None, ALU.add)
                dve.tensor_scalar(halves(row_f[:, :]), pair(3)[0:HEADS], f_bias[:, 0:1], None, ALU.add).then_inc(row_in, 1)
                dve.wait_ge(row_sp, l + 1)
                link(dve.scalar_tensor_tensor(out=row_lf[:, :], in0=row_f[:, :], scalar=0.0, in1=row_softplus[:, :],
                                              op0=ALU.min, op1=ALU.subtract))
                link(dve.tensor_tensor_scan(row_b[:, :], row_reset[:, :], row_lf[:, :], 0.0, ALU.mult, ALU.add))
                dve.tensor_tensor(gate_q[0:HEADS, :], row_i[:, :], row_b[:, :], ALU.subtract)
                dve.tensor_copy(row_lf2[:, :], row_lf[:, :])
                dve.tensor_copy(row_i2[:, :], row_i[:, :])
                dve.wait_ge(s_m0, 16 * (l + 1))
                link(dve.tensor_tensor(m0t[:, :], row_lf[:, SEQ:T:DS], m0[:, :], ALU.add))
                dve.tensor_tensor(row_i2[:, SEQ:T:DS], row_i[:, SEQ:T:DS], m0t[:, :], ALU.max)
                link(dve.memset(row_lf2[:, SEQ:T:DS], NEG))
                link(dve.tensor_tensor_scan(row_m[:, :], row_lf2[:, :], row_i2[:, :], 0.0, ALU.add, ALU.max))
                dve.tensor_copy(mprev[:, 1:NC], row_m[:, P - 1:SEQ - 1:P])
                dve.tensor_copy(mprev[:, NC:NC + DB], m0[:, :])
                link(dve.tensor_tensor(row_bm[:, :], row_b[:, :], row_m[:, :], ALU.subtract))
                dve.tensor_tensor(dlast[:, 0:NC], row_bm[:, P - 1:SEQ:P], mprev[:, 0:NC], ALU.add)
                dve.tensor_tensor(dlast[:, NC:NC + DB], row_bm[:, SEQ + DS - 1:T:DS], mprev[:, NC:NC + DB],
                                  ALU.add).then_inc(row_decay, 1)
                pv = lambda t_, r0=0: t_[r0:r0 + HEADS, 0:SEQ].rearrange("h (c n) -> h c n", n=P)
                sv = lambda t_, r0=0: t_[r0:r0 + HEADS, SEQ:T].rearrange("h (b n) -> h b n", n=DS)
                bp = lambda t_: t_.unsqueeze(2).broadcast_to([HEADS, NC, P])
                bs = lambda t_: t_.unsqueeze(2).broadcast_to([HEADS, DB, DS])
                dve.tensor_tensor(pv(gate_q, 32), pv(row_bm), bp(mprev[:, 0:NC]), ALU.add)
                dve.tensor_tensor(sv(gate_q, 32), sv(row_bm), bs(mprev[:, NC:NC + DB]), ALU.add)
                dve.tensor_scalar(gate_q[64:64 + HEADS, :], row_m[:, :], -1.0, None, ALU.mult)
                dve.tensor_tensor(pv(gate_q, 96), pv(gate_q), bp(row_bm[:, P - 1:SEQ:P]), ALU.add)
                dve.tensor_tensor(sv(gate_q, 96), sv(gate_q), bs(row_bm[:, SEQ + DS - 1:T:DS]), ALU.add).then_inc(row_done, 1)
                dve.wait_ge(decay_ps, l + 1)
                dve.tensor_copy(decay[:, :, :], ps[:, 6, 0:HEADS * (NC + DB)].rearrange("p (h c) -> p h c", h=HEADS))\
                    .then_inc(decay_sb, 1)

                dve.wait_ge(n0_ps, l + 1)
                dve.tensor_copy(n0T[:, :, :], ps[:, 2, 0:HEADS * DB].rearrange("p (h b) -> p h b", h=HEADS))
                link(dve.tensor_copy(decay8[:, :], ps[0:DB, 3, 0:HEADS]))
                n3 = n0[:, :].rearrange("b (h k) -> b h k", h=HEADS)
                dve.tensor_tensor(n3, n3, decay8[:, :].unsqueeze(2).broadcast_to([DB, HEADS, DK]), ALU.mult)\
                    .then_inc(n0_sb, 1)

                def head_norm(num_, sum_ready, ss, den_, rec, var, floor, var_s, std_s, count, out_s):
                    den = num_[:, :, DV]
                    n, heads = den.shape
                    link(dve.scalar_tensor_tensor(out=den_, in0=den, scalar=-1.0, in1=den, op0=ALU.mult, op1=ALU.max))
                    link(dve.tensor_tensor(den_, den_, floor, ALU.max))
                    link(dve.reciprocal(rec, den_))
                    dve.wait_ge(sum_ready, count)
                    link(dve.tensor_tensor(var, ss, rec, ALU.mult))
                    link(dve.tensor_tensor(var, var, rec, ALU.mult))
                    dve.tensor_scalar(var, var, 1.0 / DV, EPS, ALU.mult, ALU.add).then_inc(var_s, 1)
                    dve.wait_ge(std_s, count)
                    link(dve.reciprocal(var, var))
                    link(dve.tensor_tensor(var, var, rec, ALU.mult))
                    dve.tensor_tensor(num_[:, :, 0:DV], num_[:, :, 0:DV],
                                      var.unsqueeze(2).broadcast_to([n, heads, DV]), ALU.mult).then_inc(out_s, 1)

                s_inter = tok_exp[0:NS, NC, 0:HEADS]
                s_win = tok_exp[0:NS, NC, 64:64 + HEADS]
                for ch in range(NC):
                    h = ch
                    t0, n = ch * P, P
                    cc = l * NC + ch
                    hs = l * HEADS + h
                    inter, w_in = tok_exp[:, ch, 0:HEADS], tok_exp[:, ch, 64:64 + HEADS]
                    dve.wait_ge(s_in_ps, hs + 1)
                    if ch == 0:
                        dve.wait_ge(tok_sb, l + 1)
                    link(dve.scalar_tensor_tensor(out=s_kw[:, :], in0=ps[0:NS, 3, 0:DK], scalar=QK_SCALE,
                                                  in1=s_win[:, h:h + 1].broadcast_to([NS, DK]), op0=ALU.mult, op1=ALU.mult))
                    dve.tensor_tensor(kwm[:, :, :], s_kw[:, :].unsqueeze(1).broadcast_to([NS, DB, DK]),
                                      block01[:, :].unsqueeze(2).broadcast_to([NS, DB, DK]), ALU.mult)
                    qsrc = z[:, Z_Q + h, SEQ:T].rearrange("p (b t) -> p b t", b=DB)
                    for b in range(DB):
                        dve.tensor_copy(qm[:, b, b * DS:(b + 1) * DS], qsrc[:, b, :])
                    dve.wait_ge(s_act, hs + 1)
                    dve.scalar_tensor_tensor(out=s_wt[:, :], in0=ps[0:NS, 3, DK:DK + NS], scalar=QK_SCALE, in1=s_dt[:, :],
                                             op0=ALU.mult, op1=ALU.mult).then_inc(s_dve, 1)
                    dve.wait_ge(vk_ps, cc + 1)
                    dve.scalar_tensor_tensor(out=kw[:, :, :], in0=ps[:, 6, :].rearrange("p (h k) -> p h k", h=HEADS),
                                             scalar=QK_SCALE, in1=w_in.unsqueeze(2).broadcast_to([n, HEADS, DK]),
                                             op0=ALU.mult, op1=ALU.mult).then_inc(kw_sb, 1)

                    def c0_decay(vh):
                        dve.wait_ge(c0T_ps, hs * VH + vh + 1)
                        cv = c0[:, vh, :, :]
                        return dve.tensor_tensor(cv, cv, decay[:, h, NC:NC + DB].unsqueeze(2).broadcast_to([P, DB, DK]),
                                                 ALU.mult)

                    c0_decay(0)
                    dve.wait_ge(qk_ps, cc + 1)
                    dve.wait_ge(dt_sb, cc + 1)
                    dve.scalar_tensor_tensor(out=wt[:, :, :], in0=ps[:, 4, :].rearrange("p (h t) -> p h t", h=HEADS),
                                             scalar=QK_SCALE, in1=dt_[:, :, :], op0=ALU.mult, op1=ALU.mult).then_inc(wt_sb, 1)
                    link(c0_decay(1))

                    def two_heads(r):
                        dve.wait_ge(num_ps, l * 2 * NC + 2 * ch + r + 1)
                        hr = slice(2 * r, 2 * r + 2)
                        link(dve.tensor_tensor(num[:, hr, :], ps[:, 6:8, 0:VE],
                                               inter[:, hr].unsqueeze(2).broadcast_to([n, 2, VE]), ALU.mult))
                        dve.tensor_tensor(num[:, hr, :], num[:, hr, :], ps[:, 4:6, 0:VE], ALU.add).then_inc(num_sb, 1)

                    two_heads(0)
                    dve.wait_ge(s_num_ps, hs + 1)
                    link(dve.tensor_scalar(s_num[:, :], ps[0:NS, 3, 0:VE], s_inter[:, h:h + 1], None, ALU.mult))
                    dve.wait_ge(n0_sb, l + 1)
                    dve.tensor_tensor(n0[:, h * DK:(h + 1) * DK], n0[:, h * DK:(h + 1) * DK], ps[0:DB, 2, 384:384 + DK],
                                      ALU.add)
                    dve.tensor_tensor(s_num[:, :], s_num[:, :], ps[0:NS, 2, 0:VE], ALU.add).then_inc(s_num_sb, 1)
                    two_heads(1)
                    dve.wait_ge(s_num_sb, hs + 1)
                    head_norm(s_num[:, :].unsqueeze(1), s_ss_s, s_ss[:, :], s_den[:, :], s_rec[:, :], s_var[:, :],
                              tok_exp[0:NS, NC, 32 + h:33 + h], s_var_s, s_std_s, hs + 1, s_h)
                    dve.wait_ge(num_sb, l * 2 * NC + 2 * ch + 2)
                    head_norm(num[:, :, :], hss_s, hss[:, :], hden[:, :], hrec[:, :], hvar[:, :],
                              tok_exp[:, ch, 32:32 + HEADS], hvar_s, hstd_s, cc + 1, hc_sb)

                    def c0_add(vh):
                        dve.wait_ge(cu_ps, hs * VH + vh + 1)
                        cv = c0[:, vh, :, :]
                        dve.tensor_tensor(cv, cv, ps[:, 2:4, :].rearrange("p b (c k) -> p (b c) k", k=DK),
                                          ALU.add).then_inc(cu_sb, 1)

                    c0_add(0)
                    dve.wait_ge(st_ps, l * NC + ch + 1)
                    link(dve.tensor_tensor(state[:, :, :], state[:, :, :],
                                           decay[:, :, ch:ch + 1].broadcast_to([P, HEADS, VE]), ALU.mult))
                    dve.tensor_tensor(state[:, :, :], state[:, :, :], ps[:, 4:8, 0:VE], ALU.add).then_inc(st_sb, 1)
                    c0_add(1)

                dve.wait_ge(ws_ps, l + 1)
                dve.memset(ln_rstd, 1.0)
                m3 = mask_p[:, :].unsqueeze(1).broadcast_to([P, AT, P])
                dve.scalar_tensor_tensor(out=wsT[:, :, :], in0=m3, scalar=-0.5,
                                         in1=ps[:, 6, :].rearrange("p (g t) -> p g t", g=AT),
                                         op0=ALU.is_ge, op1=ALU.mult).then_inc(wsT_s, 1)
                dve.wait_ge(wss_ps, l + 1)
                for g in range(AT):
                    rep = ps[0:NS, 6, g * DS:(g + 1) * DS].unsqueeze(1).broadcast_to([NS, DB, DS])
                    dve.scalar_tensor_tensor(out=ws_s[:, g, :].rearrange("p (b t) -> p b t", b=DB),
                                             in0=mask_s[:, :].rearrange("p (b t) -> p b t", b=DB), scalar=-0.5, in1=rep,
                                             op0=ALU.is_ge, op1=ALU.mult)
                for ch in range(NC + 1):
                    _, n = tokens(ch)
                    dve.wait_ge(av_sb, l * (NC + 1) + ch + 1)
                    link(dve.bn_stats(ln_stats[0:n, ch, :], vn[0:n, ch, :]), True)
                    link(dve.bn_aggr(ln_mv[0:n, ch, :], ln_stats[0:n, ch, :]))
                    ins = dve.tensor_scalar(ln_rstd[0:n, ch:ch + 1], ln_mv[0:n, ch, 1:2], EPS, None, ALU.add)
                ins.then_inc(ln_var, 1)

                def branch_c(t0, t1):
                    for t in range(t0, t1 + 1):
                        if t < t1:
                            g = G_HEAD + t
                            dve.scalar_tensor_tensor(out=z[:, Z_O + t, :], in0=z[:, Z_VAL + t, :], scalar=gain[:, g:g + 1],
                                                     in1=z[:, Z_O + t, :], op0=ALU.mult, op1=ALU.mult).then_inc(c_sb, 1)
                        if t > t0:
                            dve.wait_ge(c_hi_s, l * CT_ + t)
                            dve.tensor_tensor(c_lo[:, t - 1, :], z[:, Z_O + t - 1, :], c_hi[:, t - 1, :].bitcast(F32),
                                              ALU.subtract).then_inc(c_lo_s, 1)

                dve.wait_ge(o_sig, 2 * l + 1)
                branch_c(0, CHUNK_O)
                dve.wait_ge(ln_std, l + 1)
                link(dve.reciprocal(ln_rstd, ln_rstd))
                for ch in range(NC + 1):
                    _, n = tokens(ch)
                    v_ = vn[0:n, ch, :]
                    link(dve.tensor_scalar(v_, v_, ln_mv[0:n, ch, 0:1], ln_rstd[0:n, ch:ch + 1], ALU.subtract, ALU.mult))
                    link(dve.tensor_tensor(v_, v_, ln_gb[0:n, 0, :], ALU.mult))
                    dve.tensor_tensor(v_, v_, ln_gb[0:n, 1, :], ALU.add).then_inc(vn_sb, 1)
                dve.wait_ge(o_sig, 2 * l + 2)
                branch_c(CHUNK_O, CT_)
                dve.wait_ge(u_gelu, l + 1)

                def gate_a(ch):
                    t0, n = tokens(ch)
                    dve.wait_ge(mix_ps, l * (NC + 1) + ch + 1)
                    dst = z[:, Z_U:Z_U + AT, t0:t0 + n]
                    dve.tensor_tensor(dst, dst, ps[:, 4 + ch % 2, 0:AT * n].rearrange("p (g t) -> p g t", g=AT),
                                      ALU.mult).then_inc(a_sb, 1)

                def pool_b(g):
                    w = POOL_WINDOWS[g]
                    gg = l * BT + g
                    dve.wait_ge(seg_sb, gg + 1)
                    src, step, first, bufs = seg, 1, 0, (win_a, win_b)
                    for j in range(g + 1):
                        dst = bufs[j % 2]
                        first += step
                        link(dve.tensor_tensor(dst[:, first:WID], src[:, first:WID], src[:, first - step:WID - step], ALU.add))
                        src, step = dst, 2 * step
                    if g:
                        dve.wait_ge(pmix_ps, gg)
                    dve.scalar_tensor_tensor(out=pooled[:, 16:SEQ], in0=src[:, BUF + 16:BUF + SEQ], scalar=1.0 / w,
                                             in1=seg[:, BUF + 16:BUF + SEQ], op0=ALU.mult, op1=ALU.subtract)
                    sview = lambda t_: t_[:, BUF + SEQ:WID].rearrange("p (b r) -> p b r", b=DB)[:, :, BUF:BUF + DS]
                    dve.scalar_tensor_tensor(out=pooled[:, SEQ:T].rearrange("p (b t) -> p b t", b=DB), in0=sview(src),
                                             scalar=1.0 / w, in1=sview(seg), op0=ALU.mult, op1=ALU.subtract)
                    link(dve.tensor_tensor(pooled[:, 0:16], src[:, BUF:BUF + 16], recip16[:, g, :], ALU.mult))
                    ins = dve.tensor_tensor(pooled[:, 0:16], pooled[:, 0:16], seg[:, BUF:BUF + 16], ALU.subtract)
                    ins.then_inc(pooled_s, 1)

                def scale_b(g):
                    dve.wait_ge(pmix_ps, l * BT + g + 1)
                    dve.tensor_scalar(halves(z[:, Z_B + g, :]), pair(3), gain[:, G_POOL + g:G_POOL + g + 1], None,
                                      ALU.mult).then_inc(b_sb, 1)

                gate_a(0)
                gate_a(1)
                for m in range(KD):
                    if m == 1:
                        gate_a(4)
                        for vh in range(VH):
                            dve.wait_ge(c0_done[vh], 16 * HEADS * (l + 1))
                        link(dve.memset(seg[:, 0:BUF], 0.0))
                        pool_b(0)
                    if 2 <= m < 2 + BT:
                        scale_b(m - 2)
                        if m < 1 + BT:
                            pool_b(m - 1)
                    dve.wait_ge(sig_s, l * 3 * KD + m + 1)
                    dve.wait_ge(mm[1], l * SLOT_USES + Q_GATE + m + 2)
                    dve.tensor_tensor(halves(z[:, Z_O + m, :]), halves(gate_act[m % 2][:, :]), pair(0), ALU.mult)\
                        .then_inc(gated, 1)
                    if m == 0:
                        gate_a(2)
                        gate_a(3)
                    if m == KD - 2:
                        dve.wait_ge(a_hi_s, l + 1)
                        dve.tensor_tensor(a_lo[:, :, :], z[:, Z_U:Z_U + AT, :], a_hi[:, :, :].bitcast(F32), ALU.subtract)\
                            .then_inc(a_lo_s, 1)
                        dve.wait_ge(a_lo_s, l + 1)
                        dve.wait_ge(b_hi_s, l + 1)
                        dve.tensor_tensor(b_lo[:, :, :], z[:, Z_B:Z_B + BT, :], b_hi[:, :, :].bitcast(F32), ALU.subtract)\
                            .then_inc(b_lo_s, 1)

                for half, m_lo in enumerate((merged_lo0, merged_lo1)):
                    apart(dve)
                    with dve.Fori(0, 2) as i:
                        for m2 in range(2):
                            m = 4 * half + 2 * i + m2
                            for br in range(2):
                                n = 2 * m2 + br
                                dve.wait_ge(sig_s, l * 3 * KD + KD + 8 * half + 4 * i + n + 1)
                                dst = prod[m2] if br else sq[m2]
                                dve.tensor_tensor(halves(dst[:, :]), halves(gate_act[n % 2][:, :]), pair(2 * (n % 2) + 1),
                                                  ALU.mult).then_inc(gated, 1)
                                dve.wait_ge(gated, l * PAIRS + G_MIX + KD + 8 * half + 4 * i + n + 3)
                                if br == 0:
                                    c_m = z[:, bass.ds(Z_O + m, 1), :].rearrange("p a n -> p (a n)")
                                    dve.tensor_tensor(sq[m2][:, :], sq[m2][:, :], c_m, ALU.add).then_inc(merge1, 1)
                                else:
                                    dve.wait_ge(merge1, l * KD + m + 1)
                                    dve.tensor_tensor(sq[m2][:, :], sq[m2][:, :], prod[m2][:, :], ALU.add).then_inc(merged_s, 1)
                            dve.wait_ge(merged_hi_s, l * KD + m + 1)
                            hi_t = merged_hi[:, bass.ds(m, 1), :].bitcast(F32)
                            dve.tensor_tensor(m_lo[:, bass.ds(2 * i + m2, 1), :].rearrange("p a n -> p (a n)"),
                                              sq[m2][:, :], hi_t.rearrange("p a n -> p (a n)"), ALU.subtract)\
                                .then_inc(merged_lo_s, 1)
                out_tiles(l, 1)
                post_norm(l, 1)
                pre_norm(l, 2)
                ffn(l, 1)
                post_norm(l, 2)
                assert link.n == DVE_STEPS, link.n


def kernel(**inputs):
    import numpy as _np
    import concourse.bacc as _bacc
    from concourse import mybir as _mybir
    from concourse.bass_utils import run_bass_kernel_spmd as _run

    nc = _bacc.Bacc("TRN2", target_bir_lowering=False, num_devices=1)
    arrays, args = {}, {}
    for name, value in inputs.items():
        v = _np.ascontiguousarray(value)
        arrays[f"in_{name}"] = v
        args[name] = nc.dram_tensor(f"in_{name}", v.shape, _mybir.dt.from_np(v.dtype), kind="ExternalInput").ap()
    x_p, x_s, pool, c, n, m = (inputs[k].shape for k in (
        "x_prompt", "x_sample", "state_pool", "state_mlstm_C", "state_mlstm_n", "state_mlstm_m"))
    a_width = inputs["gmlp_ln_g"].shape[1]
    depth = c[0]
    shapes = {
        "y_prompt": x_p, "y_sample": x_s,
        "pool_prompt": (depth, 1, *pool[2:]), "C_prompt": (depth, 1, *c[2:]), "n_prompt": (depth, 1, *n[2:]),
        "m_prompt": (depth, 1, *m[2:]),
        "pool_sample": pool, "C_sample": c, "n_sample": n, "m_sample": m,
        "gmlp_v_sample": (depth, *x_s[:2], a_width),
    }
    outs = {k: nc.dram_tensor(f"out_{k}", s, _mybir.dt.float32, kind="ExternalOutput").ap() for k, s in shapes.items()}
    trunk_program(nc, args, outs)
    r = _run(nc, [arrays], core_ids=[0])
    return tuple(r.results[0][f"out_{k}"] for k in shapes)
```

```python
from contextlib import ExitStack

import concourse.bass as bass
from concourse import mybir

ALU = mybir.AluOpType
ACT = mybir.ActivationFunctionType
AX = mybir.AxisListType
F32 = mybir.dt.float32
F32R = mybir.dt.float32r
I32 = mybir.dt.int32

P = 128
EPS = 1e-6
NEG = -1e30
POOL_WINDOWS = (2, 4, 8, 16)


def trunk_program(nc, a, o):
    DEPTH, D, TWO_FF = a["ffn1_w_in"].shape
    SEQ = a["x_prompt"].shape[1]
    DB, DS = a["x_sample"].shape[0:2]
    NS = DB * DS
    T = SEQ + NS
    H = T // 2
    DF = TWO_FF // 2
    KD = D // P
    FT = DF // P
    AT = a["gmlp_ln_g"].shape[1] // P
    BT = a["pool_scale"].shape[1] // P
    HEADS, DV, DK = a["state_mlstm_C"].shape[2:5]
    CT_ = HEADS * DV // P
    VH = DV // P
    BUF = a["state_pool"].shape[2]
    NC = SEQ // P
    QK_SCALE = float(DK) ** -0.5
    assert D == 8 * P and DK == P and FT % 2 == 0 and AT == BT == HEADS == 4 and CT_ == 8 and NC == 4
    assert NS == 64 and DS == 8

    Z_U, Z_V, Z_B, Z_Q, Z_K, Z_VAL, Z_O = 0, 4, 8, 12, 16, 20, 28
    NZ = 36
    COL_I, COL_F, COL_G = NZ * P, NZ * P + HEADS, NZ * P + 2 * HEADS
    Z_RUNS = [(Z_Q, 16), (Z_V, 4), (Z_U, 4), (Z_B, 4), (Z_O, 8)]
    Z_ORDER = [t0 + i for t0, n in Z_RUNS for i in range(n)]
    HEAD_START = 16
    CHUNK_O = 4
    CHUNK_END = NZ - (8 - CHUNK_O)

    CHUNKS = [min(8, FT - c) for c in range(0, FT, 8)]
    NCH = len(CHUNKS)
    Q_FFN1 = 0
    Q_DOWN1 = Q_FFN1 + FT
    Q_MIX = Q_DOWN1 + KD * NCH // 2
    Q_GATE = Q_MIX + 1 + NZ // 2
    Q_OUT = Q_GATE + 3 * KD
    Q_FFN2 = Q_OUT + KD // 2
    Q_DOWN2 = Q_FFN2 + FT
    SLOT_USES = Q_DOWN2 + KD * NCH // 2
    PAIRS = 2 * FT + 3 * KD
    G_FFN = (0, FT + 3 * KD)
    G_MIX = FT

    SQ_ADDED = (KD - 1, KD - 3, KD - 1)

    DVE_STEPS = 125

    with ExitStack() as ctx:
        def sem(name):
            return ctx.enter_context(nc.semaphore(name))

        base = (nc.sbuf_base + 63) // 64 * 64
        top = nc.sbuf_usable_end

        def place(name, shape, dt, at):
            size = 4
            for s in shape[1:]:
                size *= s
            assert base <= at and at + size <= top, (name, at, size, top)
            return nc.alloc_sbuf_tensor_at(name, shape, dt, offset=at)

        TB = 4 * T
        X_AT = base
        H_AT = X_AT + KD * TB
        RING_AT = H_AT + 2 * KD * TB
        R_AT = RING_AT + 3 * 2 * KD * P * 4
        TAIL_AT = R_AT + NZ * TB
        R_END = R_AT + 2 * 22 * TB
        C_AT = R_END

        xT = place("xT", [P, KD, T], F32, X_AT)
        h_hi = place("h_hi", [P, KD, T], F32R, H_AT)
        h_lo = place("h_lo", [P, KD, T], F32R, H_AT + KD * TB)
        yT = place("yT", [P, KD, T], F32, H_AT + KD * TB)
        w_raw = place("w_raw", [P, 2, KD, P], F32, RING_AT)
        w_hi = place("w_hi", [P, 2, KD, P], F32R, RING_AT + 2 * KD * P * 4)
        w_lo = place("w_lo", [P, 2, KD, P], F32R, RING_AT + 4 * KD * P * 4)
        act_hi = place("act_hi", [P, FT, T], F32R, R_AT)
        act_lo = place("act_lo", [P, FT, T], F32R, R_AT + FT * TB)
        x_in = place("x_in", [P, NC + 1, D], F32, R_AT)
        z = place("z", [P, NZ, T], F32, R_AT)
        a_hi = place("a_hi", [P, AT, T], F32R, R_AT + Z_V * TB)
        a_lo = place("a_lo", [P, AT, T], F32R, TAIL_AT)
        b_hi = place("b_hi", [P, BT, T], F32R, TAIL_AT + AT * TB)
        b_lo = place("b_lo", [P, BT, T], F32R, R_AT + Z_U * TB)
        c_hi = place("c_hi", [P, CT_, T], F32R, R_AT + Z_Q * TB)
        c_lo = place("c_lo", [P, CT_, T], F32R, R_AT + Z_VAL * TB)
        merged_hi = place("merged_hi", [P, KD, T], F32R, R_AT + Z_O * TB)
        merged_lo0 = place("merged_lo0", [P, KD // 2, T], F32R, R_AT + Z_B * TB)
        rows = [place(n, [HEADS, T], F32, R_AT + (Z_O + i) * TB) for i, n in enumerate(
            ["row_i", "row_f", "row_softplus", "row_lf", "row_b", "row_reset", "row_lf2", "row_i2"])]
        row_i, row_f, row_softplus, row_lf, row_b, row_reset, row_lf2, row_i2 = rows
        row_m = place("row_m", [HEADS, T], F32, R_AT + (Z_O + 1) * TB)

        cursor = [C_AT]

        def small(name, shape, dt=F32):
            n = 4
            for s in shape[1:]:
                n *= s
            t = place(name, shape, dt, cursor[0])
            cursor[0] += (n + 31) // 32 * 32
            return t

        ident = small("ident", [P, P])
        ones = small("ones", [P, P])
        mask_p = small("mask_p", [P, P])
        mask_s = small("mask_s", [NS, NS])
        block01 = small("block01", [NS, DB])
        last01 = small("last01", [NS, DB])
        count_i = small("count_i", [P, 16], I32)
        recip16 = small("recip16", [P, BT, 16])
        rep8 = small("rep8", [DS, NS])
        NGAIN = 6 * KD + BT + CT_
        gains = small("gains", [P, DEPTH * NGAIN])
        gain = small("gain", [P, NGAIN])
        if_bias = small("if_bias", [HEADS, 2])
        i_bias, f_bias = if_bias[:, 0:1], if_bias[:, 1:2]
        rstd_t = small("rstd_t", [P, NC + 1])
        G_PRE = (0, 2 * KD, 4 * KD)
        G_POST = (KD, 3 * KD, 5 * KD)
        G_POOL, G_HEAD = 6 * KD, 6 * KD + BT
        TMP = cursor[0]

        gate_act = [place(f"gate_act{i}", [P, T], F32, TMP + i * TB) for i in range(2)]
        prod = [place(f"prod{i}", [P, T], F32, TMP + (2 + i) * TB) for i in range(2)]
        sq = [place(f"sq{i}", [P, T], F32, TMP + (4 + i) * TB) for i in range(2)]
        diag = place("diag", [P, NC + 1, P], F32, TMP + 6 * TB)
        DIAG = (NC + 1) * P * 4
        ss_sum = place("ss_sum", [P, T], F32, TMP + 6 * TB + DIAG)
        merged_lo1 = place("merged_lo1", [P, KD // 2, T], F32R, TMP + 7 * TB + DIAG)
        rstd = place("rstd", [P, T], F32, TMP + 7 * TB + DIAG)
        gain_rows = place("gain_rows", [DEPTH * NGAIN, P], F32, TMP)

        cursor[0] = TMP
        VE = DV + 1
        vt = small("vt", [P, HEADS, VE])
        kw = small("kw", [P, HEADS, DK])
        dt_wt = small("dt_wt", [P, 2, HEADS, P])
        dt_, wt = dt_wt[:, 0], dt_wt[:, 1]
        squares = dt_wt.rearrange("p a h t -> p (a h t)").rearrange("p (h v) -> p h v", h=HEADS)
        num = small("num", [P, HEADS, VE])
        state = small("state", [P, HEADS, VE])
        tok_exp = small("tok_exp", [P, NC + 1, 96])
        tok_a = small("tok_a", [P, NC + 1, HEADS])
        decay = small("decay", [P, HEADS, NC + DB])
        row_bm = small("row_bm", [HEADS, T])
        m0 = small("m0", [HEADS, DB])
        m0t = small("m0t", [HEADS, DB])
        mprev = small("mprev", [HEADS, NC + DB])
        dlast = small("dlast", [HEADS, NC + DB])
        hden = small("hden", [P, HEADS])
        hrec = small("hrec", [P, HEADS])
        hss = small("hss", [P, HEADS])
        hvar = small("hvar", [P, HEADS])
        n0 = small("n0", [DB, HEADS * DK])
        n0T = small("n0T", [P, HEADS, DB])
        decay8 = small("decay8", [DB, HEADS])
        qm = small("qm", [P, DB, NS])
        nT_out = small("nT_out", [HEADS, DK])
        gate_q = place("gate_q", [P, T], F32, TMP + (4 * HEADS * VE + 31) // 32 * 32 + 3 * 2048)
        c0 = place("c0", [P, 2, DB, DK], F32, TAIL_AT)
        c0T = place("c0T", [P, DB, VE], F32, TAIL_AT + 2 * DB * DK * 4)
        c_out = place("c_out", [P, HEADS * VH, DK], F32, TAIL_AT + 2 * DB * DK * 4)
        cursor[0] = R_AT + (Z_O + CHUNK_O) * TB
        kwm = small("kwm", [NS, DB, DK])
        s_squares = small("s_squares", [NS, DV])
        s_num = small("s_num", [NS, VE])
        s_dt = small("s_dt", [NS, NS])
        s_wt = small("s_wt", [NS, NS])
        assert cursor[0] <= TAIL_AT
        cursor[0] = (TAIL_AT + (2 * DB * DK + DB * VE) * 4 + 31) // 32 * 32
        s_vt = small("s_vt", [NS, VE])
        s_kw = small("s_kw", [NS, DK])
        s_den = small("s_den", [NS, 1])
        s_rec = small("s_rec", [NS, 1])
        s_ss = small("s_ss", [NS, 1])
        s_var = small("s_var", [NS, 1])
        assert cursor[0] <= R_END

        cursor[0] = TMP + 2 * TB
        ln_gb = small("ln_gb", [P, 2, AT * P])
        ws_raw = small("ws_raw", [P, AT, P])
        wsT = small("wsT", [P, AT, P])
        ws_s = small("ws_s", [NS, AT, NS])
        bs_row = small("bs_row", [1, AT, P])
        vn = small("vn", [P, NC + 1, AT * P])
        ln_stats = small("ln_stats", [P, NC + 1, 6])
        ln_mvr = small("ln_mvr", [P, 3 * (NC + 1)])
        ln_mv, ln_rstd = ln_mvr[:, 0:2 * (NC + 1)].rearrange("p (c v) -> p c v", v=2), ln_mvr[:, 2 * (NC + 1):]
        pool_rows_p = small("pool_rows_p", [BUF, BT * P])
        WID = BUF + SEQ + DB * (BUF + DS)
        cursor[0] = TAIL_AT
        seg = small("seg", [P, WID])
        win_a = small("win_a", [P, WID])
        win_b = small("win_b", [P, WID])
        prev_raw = small("prev_raw", [DB * BUF, BT * P])
        prevT = small("prevT", [P, BT, DB * BUF])
        pooled = small("pooled", [P, T])
        pool_rows_s = small("pool_rows_s", [NS, BT * P])
        pool_w = place("pool_w_sb", [P, BT, P], F32, TMP + 2 * TB + 4096)

        ps = ctx.enter_context(nc.psum_tensor("ps", [P, 8, 512], F32))

        def pair(n):
            return ps[:, 2 * n:2 * n + 2, 0:H]

        def halves(t2):
            return t2.rearrange("p (b n) -> p b n", b=2)

        raw = [sem("raw0"), sem("raw1")]
        hi = [sem("hi0"), sem("hi1")]
        lo = [sem("lo0"), sem("lo1")]
        lo_half = sem("lo_half")
        mm = [sem("mm0"), sem("mm1")]
        passed = sem("passed")
        s_ident = sem("s_ident")
        s_const = sem("s_const")
        s_gain_in = sem("s_gain_in")
        s_gain_ps = sem("s_gain_ps")
        s_gains = sem("s_gains")
        s_gain = sem("s_gain")
        s_xin = sem("s_xin")
        s_x_ps = sem("s_x_ps")
        x_new_c = sem("x_chunk")
        s_dve0 = sem("s_dve0")
        st_zero = sem("st_zero")
        vt_ones = sem("vt_ones")
        merge1 = sem("merge1")
        x_new = sem("x_new")
        x_sq = sem("x_sq")
        x_ss = sem("x_ss")
        rs_var = sem("rs_var")
        rs_sqrt = sem("rs_sqrt")
        rs_inv = sem("rs_inv")
        rs_diag = sem("rs_diag")
        rs_ps = sem("rs_ps")
        rs_sb = sem("rs_sb")
        x_add = sem("x_add")
        g_scaled = sem("g_scaled")
        prod_s = sem("prod_s")
        h_f = sem("h_f")
        h_hi_s = sem("h_hi_s")
        h_lo_s = sem("h_lo_s")
        silu_s = sem("silu_s")
        gated = sem("gated")
        act_hi_s = sem("act_hi_s")
        act_lo_s = sem("act_lo_s")
        y_sq = sem("y_sq")
        y_out = sem("y_out")
        ss_zero = sem("ss_zero")
        ss_add = sem("ss_add")
        ss_tot = sem("ss_tot")
        y_scaled = sem("y_scaled")
        z_out = sem("z_out")
        s_bias = sem("s_bias")
        s_m0 = sem("s_m0")
        row_in = sem("row_in")
        row_sp = sem("row_sp")
        row_done = sem("row_done")
        row_decay = sem("row_decay")
        decay_exp = sem("decay_exp")
        decay_ps = sem("decay_ps")
        decay_sb = sem("decay_sb")
        q_ps = sem("q_ps")
        tok_sb = sem("tok_sb")
        m_out = sem("m_out")
        link_a = sem("act_link")
        link_d = sem("dve_link")
        vk_ps = sem("vk_ps")
        vt_sb = sem("vt_sb")
        dt_sb = sem("dt_sb")
        kw_sb = sem("kw_sb")
        qk_ps = sem("qk_ps")
        wt_sb = sem("wt_sb")
        num_ps = sem("num_ps")
        num_sb = sem("num_sb")
        hss_s = sem("hss_s")
        hvar_s = sem("hvar_s")
        hstd_s = sem("hstd_s")
        hc_sb = sem("hc_sb")
        hct_ps = sem("hct_ps")
        hct_sb = sem("hct_sb")
        st_ps = sem("st_ps")
        st_sb = sem("st_sb")
        cT_ps = sem("cT_ps")
        cT_sb = sem("cT_sb")
        c_done = sem("c_done")
        s_in_ps = sem("s_in_ps")
        s_act = sem("s_act")
        s_dve = sem("s_dve")
        s_num_ps = sem("s_num_ps")
        s_num_sb = sem("s_num_sb")
        s_ss_s = sem("s_ss_s")
        s_var_s = sem("s_var_s")
        s_std_s = sem("s_std_s")
        s_h = sem("s_h")
        s_ht_ps = sem("s_ht_ps")
        s_ht_sb = sem("s_ht_sb")
        n0_in = sem("n0_in")
        n0_ps = sem("n0_ps")
        c0_in = [sem("c0_in0"), sem("c0_in1")]
        c0T_ps = sem("c0T_ps")
        c0T_sb = sem("c0T_sb")
        cu_ps = sem("cu_ps")
        cu_sb = sem("cu_sb")
        c0_done = [sem("c0_done0"), sem("c0_done1")]
        n0_sb = sem("n0_sb")
        n_done = sem("n_done")
        a_in = sem("a_in")
        ws_ps = sem("ws_ps")
        wsT_s = sem("wsT_s")
        wss_ps = sem("wss_ps")
        av_ps = sem("av_ps")
        av_sb = sem("av_sb")
        u_gelu = sem("u_gelu")
        ln_var = sem("ln_var")
        ln_std = sem("ln_std")
        vn_sb = sem("vn_sb")
        vn_done = sem("vn_done")
        mix_ps = sem("mix_ps")
        a_sb = sem("a_sb")
        prev_in = sem("prev_in")
        pw_in = sem("pw_in")
        prow_ps = sem("prow_ps")
        prow_sb = sem("prow_sb")
        prow_done = sem("prow_done")
        seg_sb = sem("seg_sb")
        pooled_s = sem("pooled_s")
        pmix_ps = sem("pmix_ps")
        b_sb = sem("b_sb")
        a_hi_s = sem("a_hi_s")
        a_lo_s = sem("a_lo_s")
        b_hi_s = sem("b_hi_s")
        b_lo_s = sem("b_lo_s")
        o_sig = sem("o_sig")
        c_sb = sem("c_sb")
        c_hi_s = sem("c_hi_s")
        c_lo_s = sem("c_lo_s")
        sig_s = sem("sig_s")
        merged_s = sem("merged_s")
        merged_hi_s = sem("merged_hi_s")
        merged_lo_s = sem("merged_lo_s")
        xo_ps = sem("xo_ps")
        xo_sb = sem("xo_sb")
        xo_sb_d = sem("xo_sb_dve")
        xo_done = sem("xo_done")

        sq4 = sq + prod

        def squares_added(l, s):
            return l * sum(SQ_ADDED) + sum(SQ_ADDED[:s])

        def cols(w, l, k0, kt, c0_, n=P):
            return w[bass.ds(l, 1), k0 * P:(k0 + kt) * P, bass.ds(c0_, n)].rearrange("a (k p) n -> p (a k) n", p=P)

        def tokens(ch):
            return (ch * P, P) if ch < NC else (SEQ, NS)

        bank = lambda i: ps[:, i, :]
        Y_PAIR = (0, 1, 3, 2, 0)

        def apart(eng):
            eng.sem_inc(passed, 1)

        ctx.enter_context(nc.allow_non_contiguous_dma(reason="a few small transfers: gate biases, m, state rows"))
        block = ctx.enter_context(nc.Block())

        @block.sync
        def _(sp):
            def load(j, q, kt, src, n=P):
                sp.wait_ge(lo[j], q + 1)
                sp.dma_start(w_raw[:, j, 0:kt, 0:n], src).then_inc(raw[j], 16)

            def ffn(l, w_in, w_down, q0):
                with sp.Fori(0, FT) as m:
                    load(0, q0 + m, KD, cols(w_in, l, 0, KD, m * P))
                    load(1, q0 + m, KD, cols(w_in, l, 0, KD, DF + m * P))
                with sp.Fori(0, KD // 2) as i:
                    for n in range(2 * NCH):
                        m2, c = n // NCH, n % NCH
                        load(n % 2, q0 + FT + i * NCH + n // 2, CHUNKS[c],
                             cols(w_down, l, 8 * c, CHUNKS[c], i * 2 * P + m2 * P))

            kinds = ["ffn1_norm_pre", "ffn1_norm_post", "mix_norm_pre", "mix_norm_post", "ffn2_norm_pre",
                     "ffn2_norm_post", "pool_scale", "mlstm_norm_g"]
            for l0 in range(DEPTH):
                r0 = l0 * NGAIN
                for kind in kinds:
                    n = a[kind].shape[1] // P
                    sp.dma_start(gain_rows[r0:r0 + n, :], a[kind][l0].rearrange("(k p) -> k p", p=P))\
                        .then_inc(s_gain_in, 16)
                    r0 += n

            with sp.Fori(0, DEPTH) as l:
                q0 = l * SLOT_USES
                ffn(l, a["ffn1_w_in"], a["ffn1_w_down"], q0 + Q_FFN1)
                load(0, q0 + Q_MIX, KD, cols(a["w_in"], l, 0, KD, COL_I, HEADS), HEADS)
                load(1, q0 + Q_MIX, KD, cols(a["w_in"], l, 0, KD, COL_F, HEADS), HEADS)
                n0_ = 0
                for t0, cnt in Z_RUNS:
                    with sp.Fori(0, cnt // 2) as i:
                        for j in range(2):
                            load(j, q0 + Q_MIX + 1 + n0_ // 2 + i, KD,
                                 cols(a["w_in"], l, 0, KD, (t0 + j) * P + i * 2 * P))
                    n0_ += cnt
                with sp.Fori(0, KD) as m:
                    load(0, q0 + Q_GATE + m, KD, cols(a["w_in"], l, 0, KD, COL_G + 2 * D + m * P))
                    load(1, q0 + Q_GATE + m, CT_, cols(a["proj_c"], l, 0, CT_, m * P))
                with sp.Fori(0, KD) as m:
                    for br, (w, kt) in enumerate((("proj_a", AT), ("proj_b", BT))):
                        q = q0 + Q_GATE + KD + 2 * m + br
                        gate = (br, KD, cols(a["w_in"], l, 0, KD, COL_G + br * D + m * P))
                        proj = (1 - br, kt, cols(a[w], l, 0, kt, m * P))
                        for j, n, src in (proj, gate) if br else (gate, proj):
                            load(j, q, n, src)
                with sp.Fori(0, KD // 2) as i:
                    for j in range(2):
                        load(j, q0 + Q_OUT + i, KD, cols(a["w_out"], l, 0, KD, i * 2 * P + j * P))
                ffn(l, a["ffn2_w_in"], a["ffn2_w_down"], q0 + Q_FFN2)

        @block.gpsimd
        def _(pool):
            pool.memset(ident[:, :], 0.0).then_inc(s_ident, 1)
            pool.wait_ge(s_ident, 1)
            pool.affine_select(out=ident[:, :], in_=ident[:, :], compare_op=ALU.not_equal, fill=1.0, base=0,
                               pattern=[[-1, P]], channel_multiplier=1).then_inc(s_ident, 1)
            pool.memset(ones[:, :], 1.0).then_inc(s_const, 1)
            pool.memset(mask_p[:, :], 0.0).then_inc(s_const, 1)
            pool.memset(mask_s[:, :], 0.0).then_inc(s_const, 1)
            pool.memset(block01[:, :], 1.0).then_inc(s_const, 1)
            pool.memset(last01[:, :], 0.0).then_inc(s_const, 1)
            pool.memset(w_raw[:, 0, :, :], 0.0).then_inc(lo[0], 1)
            pool.memset(w_raw[:, 1, :, :], 0.0).then_inc(lo[1], 1)
            pool.memset(w_hi[:, 0, :, :].bitcast(F32), 0.0).then_inc(mm[0], 1)
            pool.memset(w_hi[:, 1, :, :].bitcast(F32), 0.0).then_inc(mm[1], 1)
            pool.memset(w_lo[:, :, :, :].bitcast(F32), 0.0).then_inc(s_const, 1)
            pool.iota(count_i[:, :], pattern=[[1, 16]], base=1, channel_multiplier=0).then_inc(s_const, 1)
            pool.wait_ge(s_const, 7)
            pool.affine_select(out=mask_p[:, :], in_=mask_p[:, :], compare_op=ALU.is_ge, fill=NEG, base=0,
                               pattern=[[1, P]], channel_multiplier=-1).then_inc(s_const, 1)
            pool.affine_select(out=mask_s[:, :], in_=mask_s[:, :], compare_op=ALU.is_ge, fill=NEG, base=0,
                               pattern=[[1, NS]], channel_multiplier=-1).then_inc(s_const, 1)
            pool.affine_select(out=block01[:, :], in_=block01[:, :], compare_op=ALU.is_ge, fill=0.0, base=0,
                               pattern=[[-DS, DB]], channel_multiplier=1).then_inc(s_const, 1)
            pool.affine_select(out=last01[:, :], in_=last01[:, :], compare_op=ALU.not_equal, fill=1.0,
                               base=1 - DS, pattern=[[-DS, DB]], channel_multiplier=1).then_inc(s_const, 1)
            pool.wait_ge(s_const, 11)
            m3 = mask_s[:, :].rearrange("p (b t) -> p b t", b=DB)
            pool.affine_select(out=m3, in_=m3, compare_op=ALU.is_ge, fill=NEG, base=0,
                               pattern=[[-DS, DB], [0, DS]], channel_multiplier=1).then_inc(s_const, 1)
            pool.affine_select(out=block01[:, :], in_=block01[:, :], compare_op=ALU.is_ge, fill=0.0, base=DS - 1,
                               pattern=[[DS, DB]], channel_multiplier=-1).then_inc(s_const, 1)

            def lo_part(j, q, kt, n=P):
                pool.wait_ge(hi[j], q + 1)
                pool.tensor_tensor(w_lo[:, j, 0:kt, 0:n], w_raw[:, j, 0:kt, 0:n],
                                   w_hi[:, j, 0:kt, 0:n].bitcast(F32), ALU.subtract).then_inc(lo[j], 1)

            def norm_squares(l, s):
                nb = l * 3 + s
                for k in range(1, SQ_ADDED[s] + 1):
                    pool.wait_ge(x_sq, nb * KD + k + 1)
                    if k > 1:
                        pool.wait_ge(x_add, squares_added(l, s) + k - 1)
                    pool.tensor_tensor(ss_sum[:, :], sq4[0][:, :] if k == 1 else ss_sum[:, :], sq4[k % 4][:, :], ALU.add)\
                        .then_inc(x_add, 1)

            def ffn(l, s, q0):
                lo_part(0, q0, KD)
                lo_part(1, q0, KD)
                norm_squares(l, s)
                with pool.Fori(1, FT) as m:
                    lo_part(0, q0 + m, KD)
                    lo_part(1, q0 + m, KD)
                with pool.Fori(0, KD // 2) as i:
                    for n in range(2 * NCH):
                        lo_part(n % 2, q0 + FT + i * NCH + n // 2, CHUNKS[n % NCH])

            with pool.Fori(0, DEPTH) as l:
                q0 = l * SLOT_USES
                ffn(l, 0, q0 + Q_FFN1)
                lo_part(0, q0 + Q_MIX, KD, HEADS)
                lo_part(1, q0 + Q_MIX, KD, HEADS)
                norm_squares(l, 1)
                with pool.Fori(0, NZ // 2) as i:
                    for j in range(2):
                        lo_part(j, q0 + Q_MIX + 1 + i, KD)
                with pool.Fori(0, KD) as m:
                    lo_part(0, q0 + Q_GATE + m, KD)
                    lo_part(1, q0 + Q_GATE + m, CT_)
                with pool.Fori(0, KD) as m:
                    for j, n, q in ((0, KD, 0), (1, AT, 0), (0, BT, 1)):
                        lo_part(j, q0 + Q_GATE + KD + 2 * m + q, n)
                    pool.wait_ge(hi[1], q0 + Q_GATE + KD + 2 * m + 2)
                    for k, ready in ((0, lo_half), (KD // 2, lo[1])):
                        ks = slice(k, k + KD // 2)
                        pool.tensor_tensor(w_lo[:, 1, ks, :], w_raw[:, 1, ks, :], w_hi[:, 1, ks, :].bitcast(F32),
                                           ALU.subtract).then_inc(ready, 1)
                with pool.Fori(0, KD // 2) as i:
                    for j in range(2):
                        lo_part(j, q0 + Q_OUT + i, KD)
                ffn(l, 2, q0 + Q_FFN2)

        @block.tensor
        def _(pe):
            def transpose(out, in_, n):
                return pe.transpose(out, in_, ident[0:n, 0:n])

            def unit(j, q, kt, n_ps, rhs_hi, rhs_lo, k0=0, first=True, last=True, ready=None, halves_done=None):
                if halves_done is None:
                    pe.wait_ge(lo[j], q + 2)
                else:
                    pe.wait_ge(lo_half, halves_done)
                for k in range(kt):
                    if ready:
                        ready(k0 + k)
                    if halves_done is not None and k == kt // 2:
                        pe.wait_ge(lo[j], q + 2)
                    for part, (w, r) in enumerate(((w_hi, rhs_hi), (w_hi, rhs_lo), (w_lo, rhs_hi))):
                        for b in range(2):
                            ins = pe.matmul(ps[:, 2 * n_ps + b, 0:H], w[:, j, k, :],
                                            r(k0 + k)[:, b * H:(b + 1) * H],
                                            start=first and k == 0 and part == 0,
                                            stop=last and k == kt - 1 and part == 2)
                ins.then_inc(mm[j], 1)

            def first_units(l, s, q, n_ps):
                for j in range(2):
                    pe.wait_ge(lo[j], q + 2)
                behind = 3
                for k0 in range(KD + behind):
                    if k0 < KD:
                        pe.wait_ge(h_lo_s, (l * 3 + s) * KD + k0 + 1)
                    for j, k in ((0, k0), (1, k0 - behind)):
                        if not 0 <= k < KD:
                            continue
                        for part, (w, r) in enumerate(((w_hi, h_hi), (w_hi, h_lo), (w_lo, h_hi))):
                            for b in range(2):
                                ins = pe.matmul(ps[:, 2 * n_ps[j] + b, 0:H], w[:, j, k, :], r[:, k, b * H:(b + 1) * H],
                                                start=k == 0 and part == 0, stop=k == KD - 1 and part == 2)
                        if k == KD - 1:
                            ins.then_inc(mm[j], 1)

            hh = lambda k: h_hi[:, k, :]
            hl = lambda k: h_lo[:, k, :]

            def sum_rows(src, start, stop):
                for ch in range(NC + 1):
                    t0, n = tokens(ch)
                    ins = pe.matmul(ps[0:n, 7, ch:ch + 1], src[:, t0:t0 + n], ones[:, 0:1], start=start and ch == 0,
                                    stop=stop and ch == NC, skip_group_check=True)
                return ins

            def spread(n_ps, ri):
                pe.wait_ge(rs_diag, ri + 1)
                for b in range(2):
                    cuts = sorted({b * H, (b + 1) * H, *(c * P for c in range(NC + 1) if b * H < c * P < (b + 1) * H)})
                    for u, v in zip(cuts, cuts[1:]):
                        ch = u // P
                        n = tokens(ch)[1]
                        ins = pe.matmul(ps[:, 2 * n_ps + b, u - b * H:v - b * H], ones[0:n, :],
                                        diag[0:n, ch, u - ch * P:v - ch * P], start=u == cuts[0], stop=v == cuts[-1],
                                        skip_group_check=True)
                ins.then_inc(rs_ps, 1)

            def norm_sums(l, s):
                rest = range(SQ_ADDED[s] + 1, KD)
                for k in rest[:-1]:
                    pe.wait_ge(x_sq, (l * 3 + s) * KD + k + 1)
                    sum_rows(sq4[k % 4][:, :], k == rest[0], False)
                pe.wait_ge(x_add, squares_added(l, s) + SQ_ADDED[s])
                ins = sum_rows(ss_sum[:, :], len(rest) < 2, not rest)
                for k in rest[-1:]:
                    pe.wait_ge(x_sq, (l * 3 + s) * KD + k + 1)
                    ins = sum_rows(sq4[k % 4][:, :], False, True)
                ins.then_inc(x_ss, 1)

            def post_norm(l, s):
                nb = l * 3 + s
                pe.wait_ge(ss_add, nb * KD + KD + 2)
                sum_rows(ss_sum[:, :], True, True).then_inc(ss_tot, 1)
                spread(2, 2 * nb + 1)

            def out_tiles(l, s, q0, chunks, rhs_hi, rhs_lo, ready):
                n_ch = len(chunks)
                with pe.Fori(0, KD // 2) as i:
                    for m2 in range(2):
                        pe.wait_ge(y_out, (l * 3 + s) * KD + 2 * i + m2 + 1)
                        for c in range(n_ch):
                            n = m2 * n_ch + c
                            unit(n % 2, q0 + i * n_ch + n // 2, chunks[c], m2, rhs_hi, rhs_lo, 8 * c,
                                 c == 0, c == n_ch - 1, ready)

            def ffn(l, f, q0):
                s = 2 * f
                pe.wait_ge(gated, l * PAIRS + G_FFN[f] + 1)
                unit(0, q0, KD, 0, hh, hl, ready=lambda k: pe.wait_ge(h_lo_s, (l * 3 + s) * KD + k + 1))
                norm_sums(l, s)
                unit(1, q0, KD, 1, hh, hl)
                pe.wait_ge(gated, l * PAIRS + G_FFN[f] + 2)
                spread(3, 2 * (l * 3 + s))
                unit(0, q0 + 1, KD, 2, hh, hl)
                pe.wait_ge(rs_sb, l * 2 + f + 1)
                unit(1, q0 + 1, KD, 3, hh, hl)
                with pe.Fori(1, FT // 2) as i:
                    for m2 in range(2):
                        pe.wait_ge(gated, l * PAIRS + G_FFN[f] + 2 * i + m2 + 1)
                        for j in range(2):
                            unit(j, q0 + 2 * i + m2, KD, 2 * m2 + j, hh, hl)
                pe.wait_ge(gated, l * PAIRS + G_FFN[f] + FT + 1)
                apart(pe)

                def act_ready(k):
                    if k == 0 or k > FT - 4:
                        pe.wait_ge(act_lo_s, (l * 2 + f) * FT + max(k, FT - 4) + 1)

                out_tiles(l, s, q0 + FT, CHUNKS, lambda k: act_hi[:, k, :], lambda k: act_lo[:, k, :], act_ready)

            pe.wait_ge(s_ident, 2)
            for ch in range(NC + 1):
                _, n = tokens(ch)
                pe.wait_ge(s_xin, 16 * (NC + 1))
                for k in range(KD):
                    if ch >= 3:
                        pe.wait_ge(x_new_c, ch - 2)
                    ins = transpose(ps[:, 2 * (ch % 3) + k // 4, (k % 4) * P:(k % 4) * P + n],
                                    x_in[0:n, ch, k * P:(k + 1) * P], n)
                ins.then_inc(s_x_ps, 1)
            pe.wait_ge(s_gain_in, 16 * 8 * DEPTH)
            NG = DEPTH * NGAIN
            transpose(bank(7)[:, 0:NG], gain_rows[:, :], NG).then_inc(s_gain_ps, 1)

            with pe.Fori(0, DEPTH) as l:
                q0 = l * SLOT_USES
                ffn(l, 0, q0 + Q_FFN1)
                post_norm(l, 0)
                norm_sums(l, 1)
                spread(3, 2 * (l * 3 + 1))

                first_units(l, 1, q0 + Q_MIX, (0, 1))
                pe.wait_ge(row_in, l + 1)
                apart(pe)

                def z_tile(n, i=0, pair_=None, left=1):
                    pe.wait_ge(z_out, l * NZ + n + 2 * i + 2 - left)
                    unit(n % 2, q0 + Q_MIX + 1 + n // 2 + i, KD, n % 2 if pair_ is None else pair_, hh, hl)

                with pe.Fori(0, HEAD_START // 4) as i:
                    z_tile(0, i)
                    z_tile(1, i)
                z_tile(HEAD_START // 2)
                pe.wait_ge(decay_exp, l + 1)
                for h in range(HEADS):
                    ins = pe.matmul(ps[:, 6, h * (NC + DB):(h + 1) * (NC + DB)],
                                    ident[0:HEADS, h:h + 1].broadcast_to([HEADS, P]), dlast[:, :],
                                    start=h == 0, stop=h == HEADS - 1, skip_group_check=True)
                ins.then_inc(decay_ps, 1)
                pe.wait_ge(row_done, l + 1)
                for ch in range(NC + 1):
                    t0, n = tokens(ch)
                    ins = transpose(ps[0:n, 4 + ch // 4, (ch % 4) * P:(ch % 4 + 1) * P], gate_q[:, t0:t0 + n], P)
                ins.then_inc(q_ps, 1)
                z_tile(HEAD_START // 2 + 1)
                with pe.Fori(HEAD_START // 4 + 1, HEAD_START // 2) as i:
                    z_tile(0, i)
                    z_tile(1, i)

                z_tile(HEAD_START, pair_=0)
                pe.wait_ge(z_out, l * NZ + HEAD_START + 2)
                pe.wait_ge(tok_sb, l + 1)
                pe.wait_ge(decay_sb, l + 1)
                pe.wait_ge(n0_in, 16 * (l + 1))
                apart(pe)
                for h in range(HEADS):
                    transpose(ps[:, 2, h * DB:(h + 1) * DB], n0[:, h * DK:(h + 1) * DK], DB)
                pe.matmul(ps[0:DB, 3, 0:HEADS], last01[:, :], tok_exp[0:NS, NC, 0:HEADS], start=True, stop=True)\
                    .then_inc(n0_ps, 1)

                zn = HEAD_START + 1
                n = P
                for ch in range(NC):
                    h = ch
                    t0 = ch * P
                    cc = l * NC + ch
                    hs = l * HEADS + h

                    def z_next():
                        nonlocal zn
                        z_tile(zn, pair_=0, left=0)
                        zn += 1

                    if ch:
                        z_next()
                    if h:
                        pe.wait_ge(s_ht_sb, hs)
                    else:
                        pe.wait_ge(n0_sb, l + 1)
                    apart(pe)
                    for vh in range(VH):
                        transpose(ps[0:NS, 2, vh * P:(vh + 1) * P], z[:, Z_VAL + h * VH + vh, SEQ:T], P)
                    pe.matmul(ps[0:NS, 2, DV:DV + NS], ident[0:NS, 0:NS], mask_s[:, :], start=True, stop=False)
                    pe.matmul(ps[0:NS, 2, DV:DV + NS], ident[0:HEADS, h:h + 1].broadcast_to([HEADS, NS]), row_bm[:, SEQ:T],
                              start=False, stop=True)
                    transpose(ps[0:NS, 3, 0:DK], z[:, Z_K + h, SEQ:T], P)
                    pe.matmul(ps[0:NS, 3, DK:DK + NS], z[:, Z_K + h, SEQ:T], z[:, Z_Q + h, SEQ:T], start=True, stop=True)\
                        .then_inc(s_in_ps, 1)
                    if ch:
                        pe.wait_ge(hct_sb, cc)
                    apart(pe)
                    for i in range(CT_):
                        transpose(ps[:, 4 + i // 4, (i % 4) * P:(i % 4 + 1) * P], z[:, Z_VAL + i, t0:t0 + n], P)
                    for i in range(HEADS):
                        transpose(ps[:, 6, i * P:(i + 1) * P], z[:, Z_K + i, t0:t0 + n], P)
                    for i in range(HEADS):
                        pe.matmul(ps[:, 7, i * n:(i + 1) * n], ident[:, :], mask_p[:, :], start=i == 0,
                                  stop=False, skip_group_check=True)
                    for i in range(HEADS):
                        ins = pe.matmul(ps[:, 7, i * n:(i + 1) * n], ident[0:HEADS, i:i + 1].broadcast_to([HEADS, n]),
                                        row_bm[:, t0:t0 + n], start=False, stop=i == HEADS - 1, skip_group_check=True)
                    ins.then_inc(vk_ps, 1)
                    z_next()

                    def c0_transposed(vh):
                        pe.wait_ge(c0_in[vh], 16 * (hs + 1))
                        apart(pe)
                        for b in range(DB):
                            ins = transpose(ps[:, 2 + b // 4, (b % 4) * P:(b % 4 + 1) * P], c0[:, vh, b, :], P)
                        ins.then_inc(c0T_ps, 1)

                    pe.wait_ge(s_act, hs + 1)
                    pe.wait_ge(s_dve, hs + 1)
                    c0_transposed(0)
                    pe.wait_ge(vt_sb, cc + 1)
                    apart(pe)
                    for i in range(HEADS):
                        ins = pe.matmul(ps[:, 4, i * n:(i + 1) * n], z[:, Z_K + i, t0:t0 + n], z[:, Z_Q + i, t0:t0 + n],
                                        start=i == 0, stop=i == HEADS - 1, skip_group_check=True)
                    ins.then_inc(qk_ps, 1)
                    z_next()
                    pe.wait_ge(c0T_sb, hs * VH + 1)
                    c0_transposed(1)
                    pe.wait_ge(wt_sb, cc + 1)
                    pe.wait_ge(kw_sb, cc + 1)
                    pe.wait_ge(dt_sb, cc + 1)
                    if ch > 0:
                        pe.wait_ge(st_sb, l * NC + ch)
                    else:
                        pe.wait_ge(st_zero, l + 1)

                    def two_heads(r):
                        for h2 in range(2):
                            i = 2 * r + h2
                            pe.matmul(ps[:, 4 + h2, 0:VE], wt[:, i, :], vt[:, i, :], start=True, stop=True)
                            ins = pe.matmul(ps[:, 6 + h2, 0:VE], z[:, Z_Q + i, t0:t0 + n], state[:, i, :],
                                            start=True, stop=True)
                        ins.then_inc(num_ps, 1)

                    two_heads(0)
                    pe.wait_ge(c0T_sb, (hs + 1) * VH)
                    apart(pe)
                    pe.matmul(ps[0:NS, 2, 0:VE], s_wt[:, :], s_vt[:, :], start=True, stop=True)
                    pe.matmul(ps[0:DB, 2, 384:384 + DK], block01[:, :], s_kw[:, :], start=True, stop=True)
                    for b in range(DB):
                        ins = pe.matmul(ps[0:NS, 3, 0:VE], qm[:, b, :], c0T[:, b, :], start=b == 0, stop=b == DB - 1)
                    ins.then_inc(s_num_ps, 1)
                    pe.wait_ge(num_sb, l * 2 * NC + 2 * ch + 1)
                    two_heads(1)
                    z_next()

                    def c0_update(vh):
                        for b in range(2):
                            ins = pe.matmul(ps[:, 2 + b, :], s_vt[:, vh * P:(vh + 1) * P],
                                            kwm[:, b * (DB // 2):(b + 1) * (DB // 2), :], start=True, stop=True)
                        ins.then_inc(cu_ps, 1)

                    pe.wait_ge(s_num_sb, hs + 1)
                    c0_update(0)
                    pe.wait_ge(num_sb, l * 2 * NC + 2 * ch + 2)
                    for i in range(HEADS):
                        ins = pe.matmul(ps[:, 4 + i, 0:VE], kw[:, i, :], vt[:, i, :], start=True, stop=True)
                    ins.then_inc(st_ps, 1)
                    pe.wait_ge(cu_sb, hs * VH + 1)
                    c0_update(1)
                    pe.wait_ge(st_sb, l * NC + ch + 1)
                    pe.wait_ge(hc_sb, cc + 1)
                    apart(pe)
                    for i in range(CT_):
                        ins = transpose(ps[:, 4 + i // 4, (i % 4) * P:(i % 4 + 1) * P],
                                        num[:, i // VH, (i % VH) * P:(i % VH + 1) * P], n)
                    ins.then_inc(hct_ps, 1)
                    pe.wait_ge(cu_sb, (hs + 1) * VH)
                    pe.wait_ge(s_h, hs + 1)
                    apart(pe)
                    for vh in range(VH):
                        ins = transpose(ps[:, 2, vh * NS:(vh + 1) * NS], s_num[:, vh * P:(vh + 1) * P], NS)
                    ins.then_inc(s_ht_ps, 1)
                assert zn == CHUNK_END

                pe.wait_ge(hct_sb, (l + 1) * NC)
                apart(pe)
                for i in range(HEADS * VH):
                    h, vh = i // VH, i % VH
                    transpose(ps[:, 4 + i // 4, (i % 4) * P:(i % 4 + 1) * P], state[:, h, vh * P:(vh + 1) * P], P)
                transpose(ps[0:HEADS, 6, 0:P], state[:, :, DV:DV + 1].rearrange("p h o -> p (h o)"), P).then_inc(cT_ps, 1)

                pe.wait_ge(s_ht_sb, (l + 1) * HEADS)
                z_tile(zn, pair_=1, left=0)
                pe.wait_ge(cT_sb, l + 1)
                for ch in range(NC + 1):
                    t0, n = tokens(ch)
                    bk = (4 + ch) % 8
                    for g in range(AT):
                        ins = transpose(ps[0:n, bk, g * P:(g + 1) * P], z[:, Z_V + g, t0:t0 + n], P)
                    ins.then_inc(av_ps, 1)
                z_tile(zn + 1, left=0)
                pe.wait_ge(a_in, 16 * 4 * (l + 1))
                pe.wait_ge(av_sb, (l + 1) * (NC + 1))
                for g in range(AT):
                    ins = transpose(ps[:, 6, g * P:(g + 1) * P], ws_raw[:, g, :], P)
                ins.then_inc(ws_ps, 1)
                z_tile(zn + 2)
                z_tile(zn + 3)
                assert zn + 4 == NZ and zn % 2 == 0
                pe.wait_ge(wsT_s, l + 1)
                pe.matmul(ps[0:NS, 6, 0:AT * DS], rep8[:, :], wsT[0:DS, :, 0:DS], start=True, stop=True)\
                    .then_inc(wss_ps, 1)

                def mix_a(ch):
                    t0, n = tokens(ch)
                    cc = l * (NC + 1) + ch
                    bk = 4 + ch % 2
                    pe.wait_ge(vn_sb, cc + 1)
                    if ch >= 2:
                        pe.wait_ge(a_sb, cc - 1)
                    for g in range(AT):
                        out = ps[:, bk, g * n:(g + 1) * n]
                        if ch < NC:
                            bias, weights = bs_row[0:1, g, :], wsT[:, g, :]
                        else:
                            bias, weights = bs_row[0:1, g:g + 1, 0:DS].broadcast_to([1, DB, DS]), ws_s[:, g, :]
                            out_b = out.rearrange("p (b t) -> p b t", b=DB)
                        pe.matmul(out if ch < NC else out_b, ones[0:1, :], bias, start=g == 0, stop=False,
                                  skip_group_check=True)
                        ins = pe.matmul(out, vn[0:n, ch, g * P:(g + 1) * P], weights, start=False,
                                        stop=g == AT - 1, skip_group_check=True)
                    ins.then_inc(mix_ps, 1)

                def rows_b():
                    pe.wait_ge(prev_in, 16 * (l + 1))
                    pe.wait_ge(a_sb, l * (NC + 1) + NC)
                    apart(pe)
                    NPREV = DB * BUF
                    for g in range(BT):
                        transpose(ps[:, 6, g * NPREV:(g + 1) * NPREV], prev_raw[:, g * P:(g + 1) * P], NPREV)
                    for g in range(BT):
                        transpose(ps[0:BUF, 7, g * P:(g + 1) * P], z[:, Z_B + g, SEQ - BUF:SEQ], P)
                    for g in range(BT):
                        ins = transpose(ps[0:NS, 5, g * P:(g + 1) * P], z[:, Z_B + g, SEQ:T], P)
                    ins.then_inc(prow_ps, 1)

                def mix_b(g):
                    gg = l * BT + g
                    if g == 0:
                        pe.wait_ge(pw_in, 16 * (l + 1))
                        pe.wait_ge(prow_sb, l + 1)
                    else:
                        pe.wait_ge(b_sb, gg)
                    pe.wait_ge(pooled_s, gg + 1)
                    for b in range(2):
                        ins = pe.matmul(ps[:, 6 + b, 0:H], pool_w[:, g, :], pooled[:, b * H:(b + 1) * H],
                                        start=True, stop=True)
                    ins.then_inc(pmix_ps, 1)

                between = {(0, 0): lambda: (mix_a(0), mix_a(1)), (0, 1): lambda: (mix_a(2), mix_a(3)),
                           (1, 0): lambda: (mix_a(4), rows_b())}
                for g in range(BT):
                    between[(2 + g, 0)] = lambda g=g: mix_b(g)
                for m in range(KD):
                    q = q0 + Q_GATE + m
                    if m == 0:
                        pe.wait_ge(z_out, l * NZ + NZ + 1)
                    else:
                        pe.wait_ge(sig_s, l * 3 * KD + m)
                    unit(0, q, KD, 0, hh, hl)
                    if (m, 0) in between:
                        between[(m, 0)]()
                    if m == 0:
                        pe.wait_ge(z_out, l * NZ + NZ + 2)
                        pe.wait_ge(c_lo_s, (l + 1) * CT_)
                    else:
                        pe.wait_ge(gated, l * PAIRS + G_MIX + m + 2)
                    unit(1, q, CT_, 1, lambda k: c_hi[:, k, :], lambda k: c_lo[:, k, :])
                    if (m, 1) in between:
                        between[(m, 1)]()

                pe.wait_ge(a_lo_s, l + 1)
                pe.wait_ge(b_lo_s, l + 1)
                pe.wait_ge(gated, l * PAIRS + G_MIX + KD + 2)
                apart(pe)
                branches = ((a_hi, a_lo, AT), (b_hi, b_lo, BT))
                with pe.Fori(0, KD // 2) as i:
                    for m2 in range(2):
                        for br, (bh, bl, kt) in enumerate(branches):
                            n = 2 * m2 + br
                            pe.wait_ge(gated, l * PAIRS + G_MIX + KD + 4 * i + n + 1)
                            q = q0 + Q_GATE + KD + 4 * i + n
                            gate = (KD, 2 * (n % 2), hh, hl)
                            proj = (kt, 2 * (n % 2) + 1, lambda k: bh[:, k, :], lambda k: bl[:, k, :])
                            for j, u in enumerate((proj, gate) if br else (gate, proj)):
                                if br and j:
                                    unit(j, q, *u, halves_done=l * KD + 2 * i + m2 + 1)
                                else:
                                    unit(j, q, *u)
                pe.wait_ge(gated, l * PAIRS + G_MIX + 3 * KD + 1)
                apart(pe)

                def merged_ready(k):
                    if k == 0 or k > KD - 3:
                        pe.wait_ge(merged_lo_s, l * KD + max(k, KD - 3) + 1)

                out_tiles(l, 1, q0 + Q_OUT, [KD], lambda k: merged_hi[:, k, :],
                          lambda k: (merged_lo0 if k < KD // 2 else merged_lo1)[:, k % (KD // 2), :], merged_ready)
                post_norm(l, 1)
                ffn(l, 1, q0 + Q_FFN2)
                post_norm(l, 2)

            def y_transposed(ch, k):
                t0, n = tokens(ch)
                return transpose(ps[0:n, 2 * Y_PAIR[ch] + k // 4, (k % 4) * P:(k % 4 + 1) * P], xT[:, k, t0:t0 + n], P)

            for k in range(KD):
                pe.wait_ge(x_new, DEPTH * 3 * KD + k + 1)
                for ch in range(3):
                    ins = y_transposed(ch, k)
                    if k == KD - 1:
                        ins.then_inc(xo_ps, 1)
            for ch in range(3, NC + 1):
                if ch == NC:
                    pe.wait_ge(xo_sb, 1)
                    pe.wait_ge(xo_sb_d, 1)
                for k in range(KD):
                    ins = y_transposed(ch, k)
                ins.then_inc(xo_ps, 1)

        @block.scalar
        def _(act):
            act_steps = 2

            class Link:
                def __init__(self, l):
                    self.base, self.n = l * act_steps, 0

                def __call__(self, ins):
                    self.n += 1
                    ins.then_inc(link_a, 1)
                    act.wait_ge(link_a, self.base + self.n)

            def pre_norm(l, s):
                nb = l * 3 + s
                for k in range(KD):
                    act.wait_ge(x_new, nb * KD + k + 1)
                    if s != 1:
                        if k == 0:
                            act.wait_ge(s_gain, 2 * l + 2)
                        g = G_PRE[s] + k
                        act.activation(h_hi[:, k, :], xT[:, k, :], ACT.Copy, scale=gain[:, g:g + 1]).then_inc(h_hi_s, 1)
                    if k >= 4:
                        act.wait_ge(x_add, squares_added(l, s) + max(k - 4, 1))
                    act.activation(sq4[k % 4][:, :], xT[:, k, :], ACT.Square).then_inc(x_sq, 1)

            def norm_hi(l, s):
                nb = l * 3 + s
                for k in range(KD):
                    act.wait_ge(h_f, (l * KD) + k + 1)
                    act.activation(h_hi[:, k, :], prod[k % 2][:, :], ACT.Copy).then_inc(h_hi_s, 1)

            def hi_part(j, q):
                act.wait_ge(raw[j], (q + 1) * 16)
                act.wait_ge(mm[j], q + 1)
                act.activation(w_hi[:, j, :, :], w_raw[:, j, :, :], ACT.Copy).then_inc(hi[j], 1)

            def root(ri):
                act.wait_ge(rs_var, ri + 1)
                act.activation(rstd_t[:, :], rstd_t[:, :], ACT.Sqrt).then_inc(rs_sqrt, 1)

            def out_tiles(l, s, q0, n_ch):
                yb = (l * 3 + s) * KD

                def two_tiles(i, last=False):
                    for m2 in range(2):
                        units = range(m2 * n_ch, (m2 + 1) * n_ch)
                        late = [n for n in units if last and m2 and n >= 2 * n_ch - 2]
                        for n in units:
                            if n not in late:
                                hi_part(n % 2, q0 + i * n_ch + n // 2 + 1)
                        act.wait_ge(mm[n % 2], q0 + i * n_ch + n // 2 + 2)
                        act.wait_ge(ss_add, yb + 2 * i + m2 + 1)
                        act.activation(halves(sq[m2][:, :]), pair(m2), ACT.Square).then_inc(y_sq, 1)
                        act.activation(yT[:, bass.ds(2 * i + m2, 1), :].rearrange("p a (b n) -> p (a b) n", b=2),
                                       pair(m2), ACT.Copy).then_inc(y_out, 1)
                        for n in late if s < 2 else ():
                            hi_part(n % 2, q0 + i * n_ch + n // 2 + 1)

                with act.Fori(0, KD // 2 - 1) as i:
                    two_tiles(i)
                two_tiles(KD // 2 - 1, last=True)

            def ffn(l, f, q0):
                def silu_pair(i, m2, behind=None):
                    pf = (l * 2 + f) * FT + 2 * i + m2
                    if behind is None:
                        hi_part(0, q0 + 2 * i + m2 + 1)
                    else:
                        behind()
                    act.wait_ge(g_scaled, pf + 1)
                    act.activation(gate_act[m2][:, :], gate_act[m2][:, :], ACT.Silu).then_inc(silu_s, 1)
                    if behind is None:
                        hi_part(1, q0 + 2 * i + m2 + 1)
                    act.wait_ge(prod_s, pf + 1)
                    act.activation(act_hi[:, bass.ds(2 * i + m2, 1), :].rearrange("p a n -> p (a n)"),
                                   prod[m2][:, :], ACT.Copy).then_inc(act_hi_s, 1)

                def with_root():
                    hi_part(0, q0 + 1)
                    root(2 * (l * 3 + 2 * f))
                    hi_part(1, q0 + 1)

                silu_pair(0, 0, with_root)
                silu_pair(0, 1)
                with act.Fori(1, FT // 2) as i:
                    silu_pair(i, 0)
                    silu_pair(i, 1)
                out_tiles(l, 2 * f, q0 + FT, NCH)

            for ch in range(NC + 1):
                t0, n = tokens(ch)
                src = a["x_prompt"][0, t0:t0 + n, :] if ch < NC else a["x_sample"].rearrange("b t d -> (b t) d")
                act.dma_start(x_in[0:n, ch, :], src).then_inc(s_xin, 16)
            for ch in range(NC + 1):
                t0, n = tokens(ch)
                act.wait_ge(s_x_ps, ch + 1)
                for half in range(2):
                    src = ps[:, 2 * (ch % 3) + half, :].rearrange("p (k n) -> p k n", k=4)[:, :, 0:n]
                    ins = act.activation(xT[:, 4 * half:4 * half + 4, t0:t0 + n], src, ACT.Copy)
                ins.then_inc(x_new_c, 1)
            act.wait_ge(s_gain_ps, 1)
            act.activation(gains[:, :], bank(7)[:, 0:DEPTH * NGAIN], ACT.Copy).then_inc(s_gains, 1)
            act.wait_ge(x_new_c, NC + 1)
            act.wait_ge(s_const, 13)
            for k in range(KD):
                act.activation(gate_act[0][:, k:k + 1], ones[:, k:k + 1], ACT.Copy).then_inc(x_new, 1)

            with act.Fori(0, DEPTH) as l:
                link = Link(l)
                q0 = l * SLOT_USES
                hi_part(0, q0)
                hi_part(1, q0)
                pre_norm(l, 0)
                ffn(l, 0, q0 + Q_FFN1)
                root(2 * (l * 3) + 1)
                pre_norm(l, 1)
                root(2 * (l * 3 + 1))
                norm_hi(l, 1)

                lsl = bass.ds(l, 1)
                act.dma_start(i_bias, a["mlstm_i_bias"][lsl, :].rearrange("a h -> h a")).then_inc(s_bias, 16)
                act.dma_start(f_bias, a["mlstm_f_bias"][lsl, :].rearrange("a h -> h a")).then_inc(s_bias, 16)
                act.dma_start(m0[:, :], a["state_mlstm_m"][lsl, :, :].rearrange("a b h -> h (a b)")).then_inc(s_m0, 16)
                act.dma_start(n0[:, :], a["state_mlstm_n"][lsl].rearrange("a b h k -> (a b) (h k)")).then_inc(n0_in, 16)
                for j in range(2):
                    hi_part(j, q0 + Q_MIX + 1)
                act.wait_ge(row_in, l + 1)
                link(act.activation(row_softplus[:, :], row_f[:, :], ACT.Abs))
                link(act.activation(row_softplus[:, :], row_softplus[:, :], ACT.Exp, scale=-1.0))
                act.activation(row_softplus[:, :], row_softplus[:, :], ACT.Ln, bias=ones[0:HEADS, 0:1]).then_inc(row_sp, 1)

                def z_tile(n, t, i=0, pair_=None):
                    hi_part(n % 2, q0 + Q_MIX + 1 + n // 2 + i + 1)
                    dst = z[:, bass.ds(t + 2 * i, 1), :].rearrange("p a (b n) -> p (a b) n", b=2)
                    act.activation(dst, pair(n % 2 if pair_ is None else pair_), ACT.Copy).then_inc(z_out, 1)

                with act.Fori(0, HEAD_START // 4) as i:
                    z_tile(0, Z_Q, i)
                    z_tile(1, Z_Q + 1, i)
                act.wait_ge(row_decay, l + 1)
                act.activation(dlast[:, :], dlast[:, :], ACT.Exp).then_inc(decay_exp, 1)
                act.wait_ge(row_done, l + 1)
                act.dma_start(o["m_prompt"][lsl, 0, :].rearrange("a h -> h a"), row_m[:, SEQ - 1:SEQ]).then_inc(m_out, 16)
                act.dma_start(o["m_sample"][lsl, :, :].rearrange("a b h -> h (a b)"),
                              row_m[:, SEQ + DS - 1:T:DS]).then_inc(m_out, 16)
                z_tile(HEAD_START // 2, Z_Q + HEAD_START // 2)
                act.wait_ge(q_ps, l + 1)
                tp = ps[:, 4, :].rearrange("p (c n) -> p c n", c=NC)
                act.activation(tok_exp[:, 0:NC, :], tp[:, :, 32:P], ACT.Exp)
                act.activation(tok_a[:, 0:NC, :], tp[:, :, 0:HEADS], ACT.Copy)
                act.activation(tok_exp[0:NS, NC, :], ps[0:NS, 5, 32:P], ACT.Exp)
                act.activation(tok_a[0:NS, NC, :], ps[0:NS, 5, 0:HEADS], ACT.Copy).then_inc(tok_sb, 1)
                z_tile(HEAD_START // 2 + 1, Z_Q + HEAD_START // 2 + 1)
                with act.Fori(HEAD_START // 4 + 1, HEAD_START // 2) as i:
                    z_tile(0, Z_Q, i)
                    z_tile(1, Z_Q + 1, i)
                act.wait_ge(m_out, 32 * (l + 1))

                def load_c0(h, vh):
                    src = a["state_mlstm_C"][lsl, :, h, vh * P:(vh + 1) * P, :]
                    act.dma_start(c0[:, vh, :, :], src.rearrange("a b v k -> v (a b) k")).then_inc(c0_in[vh], 16)

                load_c0(0, 0)
                load_c0(0, 1)
                zn = HEAD_START
                for ch in range(NC):
                    h = ch
                    t0, n = ch * P, P
                    cc = l * NC + ch
                    hs = l * HEADS + h

                    def z_next():
                        nonlocal zn
                        z_tile(zn, Z_ORDER[zn], pair_=0)
                        zn += 1

                    z_next()
                    if h:
                        act.wait_ge(c0_done[1], 16 * hs)
                        load_c0(h, 1)
                    act.wait_ge(s_in_ps, hs + 1)
                    if ch == 0:
                        act.wait_ge(vt_ones, l + 1)
                        act.wait_ge(tok_sb, l + 1)
                    act.activation(s_vt[:, 0:DV], ps[0:NS, 2, 0:DV], ACT.Copy)
                    act.activation(s_dt[:, :], ps[0:NS, 2, DV:DV + NS], ACT.Exp, bias=tok_a[0:NS, NC, h:h + 1]).then_inc(s_act, 1)
                    act.wait_ge(vk_ps, cc + 1)
                    if ch:
                        act.wait_ge(st_ps, l * NC + ch)
                    for i in range(2):
                        src = ps[:, 4 + i, :].rearrange("p (h v) -> p h v", h=2)
                        ins = act.activation(vt[:, 2 * i:2 * i + 2, 0:DV], src, ACT.Copy)
                    ins.then_inc(vt_sb, 1)
                    for i in range(HEADS):
                        ins = act.activation(dt_[:, i, :], ps[:, 7, i * n:(i + 1) * n], ACT.Exp, bias=tok_a[:, ch, i:i + 1])
                    ins.then_inc(dt_sb, 1)
                    z_next()
                    for vh in range(VH):
                        act.wait_ge(c0T_ps, hs * VH + vh + 1)
                        if vh == 0:
                            act.wait_ge(n0_sb, l + 1)
                            act.activation(c0T[:, :, DV], n0T[:, h, :], ACT.Copy)
                        for b in range(2):
                            ins = act.activation(c0T[:, 4 * b:4 * b + 4, vh * P:(vh + 1) * P],
                                                 ps[:, 2 + b, :].rearrange("p (b k) -> p b k", b=4), ACT.Copy)
                        ins.then_inc(c0T_sb, 1)
                        if vh == 0:
                            z_next()
                    act.wait_ge(s_num_sb, hs + 1)
                    act.activation(s_squares[:, :], s_num[:, 0:DV], ACT.Square, accum_out=s_ss[:, :]).then_inc(s_ss_s, 1)
                    act.wait_ge(num_sb, l * 2 * NC + 2 * ch + 2)
                    for i in range(HEADS):
                        ins = act.activation(squares[:, i, :], num[:, i, 0:DV], ACT.Square, accum_out=hss[:, i:i + 1])
                    ins.then_inc(hss_s, 1)
                    act.wait_ge(s_var_s, hs + 1)
                    act.activation(s_var[:, :], s_var[:, :], ACT.Sqrt).then_inc(s_std_s, 1)
                    act.wait_ge(hvar_s, cc + 1)
                    act.activation(hvar[:, :], hvar[:, :], ACT.Sqrt).then_inc(hstd_s, 1)
                    z_next()

                    def store_c0(vh):
                        act.wait_ge(cu_sb, hs * VH + vh + 1)
                        dst = o["C_sample"][lsl, :, h, vh * P:(vh + 1) * P, :]
                        act.dma_start(dst.rearrange("a b v k -> v (a b) k"), c0[:, vh, :, :]).then_inc(c0_done[vh], 16)

                    store_c0(0)
                    store_c0(1)
                    act.wait_ge(hct_ps, cc + 1)
                    for i in range(2):
                        src = ps[:, 4 + i, 0:4 * n].rearrange("p (c n) -> p c n", c=4)
                        ins = act.activation(z[:, Z_VAL + 4 * i:Z_VAL + 4 * i + 4, t0:t0 + n], src, ACT.Copy)
                    ins.then_inc(hct_sb, 1)
                    act.wait_ge(s_ht_ps, hs + 1)
                    act.activation(z[:, Z_VAL + VH * h:Z_VAL + VH * (h + 1), SEQ:T],
                                   ps[:, 2, 0:VH * NS].rearrange("p (c n) -> p c n", c=VH), ACT.Copy).then_inc(s_ht_sb, 1)
                    if h < HEADS - 1:
                        act.wait_ge(c0_done[0], 16 * (hs + 1))
                        load_c0(h + 1, 0)
                act.wait_ge(cT_ps, l + 1)
                act.activation(c_out[:, 0:4, :], ps[:, 4, :].rearrange("p (i k) -> p i k", i=4), ACT.Copy)
                act.activation(c_out[:, 4:8, :], ps[:, 5, :].rearrange("p (i k) -> p i k", i=4), ACT.Copy)
                act.activation(nT_out[:, :], ps[0:HEADS, 6, 0:P], ACT.Copy).then_inc(cT_sb, 1)
                act.wait_ge(cT_sb, l + 1)
                act.dma_start(o["C_prompt"][lsl, 0].rearrange("a h (w v) k -> v (a h w) k", v=P),
                              c_out[:, :, :]).then_inc(c_done, 16)
                act.dma_start(o["n_prompt"][lsl, 0].rearrange("a h k -> (a h) k"), nT_out[:, :]).then_inc(c_done, 16)
                act.dma_start(o["n_sample"][lsl].rearrange("a b h k -> (a b) (h k)"), n0[:, :]).then_inc(n_done, 16)

                act.wait_ge(n_done, 16 * (l + 1))
                act.dma_start(ws_raw[:, :, :], a["gmlp_w_s"][lsl].rearrange("a g t s -> t (a g) s")).then_inc(a_in, 16)
                act.dma_start(bs_row[:, :, :], a["gmlp_b_s"][lsl]).then_inc(a_in, 16)
                act.dma_start(ln_gb[:, 0, :], a["gmlp_ln_g"][lsl, :].broadcast_to([P, AT * P])).then_inc(a_in, 16)
                act.dma_start(ln_gb[:, 1, :], a["gmlp_ln_b"][lsl, :].broadcast_to([P, AT * P])).then_inc(a_in, 16)
                z_tile(zn, Z_ORDER[zn], pair_=1)
                zn += 1
                for ch in range(NC + 1):
                    t0, n = tokens(ch)
                    bk = (4 + ch) % 8
                    act.wait_ge(av_ps, l * (NC + 1) + ch + 1)
                    act.activation(vn[0:n, ch, :], ps[0:n, bk, :], ACT.Gelu_apprx_tanh).then_inc(av_sb, 1)
                act.wait_ge(c_done, 32 * (l + 1))
                act.dma_start(prev_raw[:, :], a["state_pool"][lsl].rearrange("a b r c -> (a b r) c")).then_inc(prev_in, 16)
                act.dma_start(o["pool_sample"][lsl, :, 0:BUF - DS, :], a["state_pool"][lsl, :, DS:BUF, :]).then_inc(prow_done, 16)
                act.activation(z[:, Z_U:Z_U + AT, :], z[:, Z_U:Z_U + AT, :], ACT.Gelu_apprx_tanh).then_inc(u_gelu, 1)
                def sigmoid_o(t0, t1):
                    act.activation(z[:, Z_O + t0:Z_O + t1, :], z[:, Z_O + t0:Z_O + t1, :], ACT.Sigmoid).then_inc(o_sig, 1)

                def c_hi_parts(t0, t1):
                    for t in range(t0, t1):
                        act.wait_ge(c_sb, l * CT_ + t + 1)
                        act.activation(c_hi[:, t, :], z[:, Z_O + t, :], ACT.Copy).then_inc(c_hi_s, 1)

                sigmoid_o(0, CHUNK_O)
                z_tile(zn, Z_ORDER[zn])
                zn += 1
                c_hi_parts(0, CHUNK_O)
                act.wait_ge(ln_var, l + 1)
                act.activation(ln_rstd, ln_rstd, ACT.Sqrt).then_inc(ln_std, 1)
                act.wait_ge(wsT_s, l + 1)
                act.dma_start(pool_w[:, :, :], a["pool_w"][lsl].rearrange("a g c d -> c (a g) d")).then_inc(pw_in, 16)
                while zn < NZ:
                    z_tile(zn, Z_ORDER[zn])
                    zn += 1
                act.wait_ge(z_out, (l + 1) * NZ + 2)
                sigmoid_o(CHUNK_O, CT_)
                c_hi_parts(CHUNK_O, CT_)
                NPREV = DB * BUF

                def rows_b():
                    act.wait_ge(prow_ps, l + 1)
                    act.activation(prevT[:, :, :], ps[:, 6, 0:BT * NPREV].rearrange("p (g r) -> p g r", g=BT), ACT.Copy)
                    act.activation(pool_rows_p[:, :], ps[0:BUF, 7, :], ACT.Copy)
                    act.activation(pool_rows_s[:, :], ps[0:NS, 5, :], ACT.Copy).then_inc(prow_sb, 1)
                    act.wait_ge(prow_sb, l + 1)
                    act.dma_start(o["pool_prompt"][lsl, 0].rearrange("a r c -> (a r) c"), pool_rows_p[:, :]).then_inc(prow_done, 16)
                    act.dma_start(o["pool_sample"][lsl, :, BUF - DS:BUF, :], pool_rows_s[:, :]).then_inc(prow_done, 16)
                    act.dma_start(o["gmlp_v_sample"][lsl].rearrange("a b t c -> (a b t) c"), vn[0:NS, NC, :]).then_inc(vn_done, 16)

                def seg_b(g):
                    gg = l * BT + g
                    if g:
                        act.wait_ge(pooled_s, gg)
                    act.activation(seg[:, BUF:BUF + SEQ], z[:, Z_B + g, 0:SEQ], ACT.Copy)
                    ss = seg[:, BUF + SEQ:WID].rearrange("p (b r) -> p b r", b=DB)
                    act.activation(ss[:, :, 0:BUF], prevT[:, g, :].rearrange("p (b r) -> p b r", b=DB), ACT.Copy)
                    act.activation(ss[:, :, BUF:BUF + DS], z[:, Z_B + g, SEQ:T].rearrange("p (b t) -> p b t", b=DB),
                                   ACT.Copy).then_inc(seg_sb, 1)

                for m in range(KD):
                    hi_part(0, q0 + Q_GATE + m + 1)
                    act.wait_ge(gated, l * PAIRS + G_MIX + m + 1)
                    act.activation(halves(gate_act[m % 2][:, :]), pair(0), ACT.Sigmoid).then_inc(sig_s, 1)
                    if m == 1:
                        rows_b()
                    if 1 <= m <= BT:
                        seg_b(m - 1)
                    if m == KD - 2:
                        act.wait_ge(a_sb, (l + 1) * (NC + 1))
                        act.activation(a_hi[:, :, :], z[:, Z_U:Z_U + AT, :], ACT.Copy).then_inc(a_hi_s, 1)
                        act.wait_ge(b_sb, (l + 1) * BT)
                        act.wait_ge(prow_done, 48 * (l + 1))
                        act.activation(b_hi[:, :, :], z[:, Z_B:Z_B + BT, :], ACT.Copy).then_inc(b_hi_s, 1)
                    hi_part(1, q0 + Q_GATE + m + 1)
                act.wait_ge(vn_done, 16 * (l + 1))
                for half in range(2):
                    with act.Fori(2 * half, 2 * half + 2) as i:
                        for m2 in range(2):
                            for br in range(2):
                                n = 2 * m2 + br
                                for j in range(2):
                                    hi_part(j, q0 + Q_GATE + KD + 4 * i + n + 1)
                                act.wait_ge(gated, l * PAIRS + G_MIX + KD + 4 * i + n + 1)
                                act.activation(halves(gate_act[n % 2][:, :]), pair(2 * (n % 2)), ACT.Sigmoid)\
                                    .then_inc(sig_s, 1)
                            act.wait_ge(merged_s, l * KD + 2 * i + m2 + 1)
                            act.activation(merged_hi[:, bass.ds(2 * i + m2, 1), :].rearrange("p a n -> p (a n)"),
                                           sq[m2][:, :], ACT.Copy).then_inc(merged_hi_s, 1)
                out_tiles(l, 1, q0 + Q_OUT, 1)
                root(2 * (l * 3 + 1) + 1)
                pre_norm(l, 2)
                ffn(l, 1, q0 + Q_FFN2)
                root(2 * (l * 3 + 2) + 1)

            for ch in range(NC + 1):
                t0, n = tokens(ch)
                act.wait_ge(xo_ps, ch + 1)
                act.activation(x_in[0:n, ch, 0:D // 2], ps[0:n, 2 * Y_PAIR[ch], :], ACT.Copy).then_inc(xo_sb, 1)
                act.wait_ge(xo_sb, ch + 1)
                act.wait_ge(xo_sb_d, ch + 1)
                dst = o["y_prompt"][0, t0:t0 + n, :] if ch < NC else o["y_sample"].rearrange("b t d -> (b t) d")
                act.dma_start(dst, x_in[0:n, ch, :]).then_inc(xo_done, 16)
            act.wait_ge(xo_done, 16 * (NC + 1))
            act.wait_ge(m_out, 32 * DEPTH)
            act.wait_ge(c_done, 32 * DEPTH)
            act.wait_ge(n_done, 16 * DEPTH)
            act.wait_ge(vn_done, 16 * DEPTH)
            act.wait_ge(prow_done, 48 * DEPTH)
            for vh in range(VH):
                act.wait_ge(c0_done[vh], 16 * HEADS * DEPTH)

        @block.vector
        def _(dve):
            class Link:
                def __init__(self, l):
                    self.base, self.n = l * DVE_STEPS, 0

                def __call__(self, ins, alone=False):
                    self.n += 1
                    ins.then_inc(link_d, 1)
                    dve.wait_ge(link_d, self.base + self.n)
                    if alone:
                        apart(dve)

            def recip_root(ri):
                for r, n in ((slice(0, NC), P), (slice(NC, NC + 1), NS)):
                    ins = dve.tensor_scalar(rstd_t[0:n, r], ps[0:n, 7, r], 1.0 / D, EPS, ALU.mult, ALU.add)
                ins.then_inc(rs_var, 1)
                dve.wait_ge(rs_sqrt, ri + 1)
                dve.reciprocal(rstd_t[:, :], rstd_t[:, :]).then_inc(rs_inv, 1)
                dve.wait_ge(rs_inv, ri + 1)
                dve.tensor_tensor(diag[:, :, :], ident[:, :].unsqueeze(1).broadcast_to([P, NC + 1, P]),
                                  rstd_t[:, :].unsqueeze(2).broadcast_to([P, NC + 1, P]), ALU.mult).then_inc(rs_diag, 1)
                dve.wait_ge(rs_ps, ri + 1)

            def pre_norm(l, s):
                nb = l * 3 + s
                dve.wait_ge(x_ss, nb + 1)
                recip_root(2 * nb)
                for k in range(KD + 1):
                    if k < KD:
                        if k >= 2:
                            dve.wait_ge(h_lo_s, nb * KD + k - 1)
                        g = G_PRE[s] + k
                        dve.scalar_tensor_tensor(out=halves(prod[k % 2][:, :]), in0=halves(xT[:, k, :]),
                                                 scalar=gain[:, g:g + 1], in1=pair(3), op0=ALU.mult, op1=ALU.mult).then_inc(h_f, 1)
                    if k:
                        dve.wait_ge(h_hi_s, nb * KD + k)
                        dve.tensor_tensor(h_lo[:, k - 1, :], prod[(k - 1) % 2][:, :], h_hi[:, k - 1, :].bitcast(F32),
                                          ALU.subtract).then_inc(h_lo_s, 1)

            def pre_norm_ffn(l, s):
                nb = l * 3 + s
                for k in range(KD):
                    g = G_PRE[s] + k
                    dve.wait_ge(h_hi_s, nb * KD + k + 1)
                    dve.scalar_tensor_tensor(out=h_lo[:, k, :], in0=xT[:, k, :], scalar=gain[:, g:g + 1],
                                             in1=h_hi[:, k, :].bitcast(F32), op0=ALU.mult, op1=ALU.subtract).then_inc(h_lo_s, 1)
                dve.wait_ge(x_ss, nb + 1)
                recip_root(2 * nb)
                dve.tensor_copy(halves(rstd[:, :]), pair(3)).then_inc(rs_sb, 1)
                dve.wait_ge(rs_sb, l * 2 + s // 2 + 1)

            def post_norm(l, s):
                nb = l * 3 + s
                dve.wait_ge(ss_tot, nb + 1)
                recip_root(2 * nb + 1)
                for k in range(KD + 1):
                    if k < KD:
                        g = G_POST[s] + k
                        dve.scalar_tensor_tensor(out=halves(yT[:, k, :]), in0=halves(yT[:, k, :]),
                                                 scalar=gain[:, g:g + 1], in1=pair(2), op0=ALU.mult, op1=ALU.mult).then_inc(y_scaled, 1)
                    if k:
                        dve.wait_ge(y_scaled, nb * KD + k)
                        dve.tensor_tensor(xT[:, k - 1, :], xT[:, k - 1, :], yT[:, k - 1, :], ALU.add).then_inc(x_new, 1)

            def out_tiles(l, s):
                nb = l * 3 + s
                dve.memset(ss_sum[:, :], 0.0).then_inc(ss_zero, 1)
                dve.wait_ge(ss_zero, nb + 1)
                apart(dve)
                with dve.Fori(0, KD // 2) as i:
                    for m2 in range(2):
                        dve.wait_ge(y_sq, nb * KD + 2 * i + m2 + 1)
                        dve.wait_ge(ss_add, nb * KD + 2 * i + m2 + 2)
                        dve.tensor_tensor(ss_sum[:, :], ss_sum[:, :], sq[m2][:, :], ALU.add).then_inc(ss_add, 1)

            def ffn(l, f, q0):
                apart(dve)
                with dve.Fori(0, FT // 2) as i:
                    for m2 in range(2):
                        n = 2 * i + m2
                        pf = (l * 2 + f) * FT + n
                        gate, prod_ = gate_act[m2][:, :], prod[m2][:, :]
                        dve.wait_ge(mm[0], q0 + n + 2)
                        dve.tensor_tensor(halves(gate), pair(2 * m2), halves(rstd[:, :]), ALU.mult).then_inc(g_scaled, 1)
                        dve.wait_ge(silu_s, pf + 1)
                        dve.wait_ge(mm[1], q0 + n + 2)
                        dve.tensor_tensor(halves(prod_), halves(gate), pair(2 * m2 + 1), ALU.mult).then_inc(gated, 1)
                        dve.wait_ge(gated, l * PAIRS + G_FFN[f] + n + 3)
                        dve.tensor_tensor(prod_, prod_, rstd[:, :], ALU.mult).then_inc(prod_s, 1)
                        dve.wait_ge(act_hi_s, pf + 1)
                        sel = bass.ds(n, 1)
                        dve.tensor_tensor(act_lo[:, sel, :].rearrange("p a n -> p (a n)"), prod_,
                                          act_hi[:, sel, :].bitcast(F32).rearrange("p a n -> p (a n)"),
                                          ALU.subtract).then_inc(act_lo_s, 1)
                out_tiles(l, 2 * f)

            dve.wait_ge(s_const, 13)
            dve.wait_ge(s_ident, 2)
            dve.tensor_copy(rep8[:, :].rearrange("p (b t) -> p b t", b=DB),
                            ident[0:DS, 0:DS].unsqueeze(1).broadcast_to([DS, DB, DS])).then_inc(s_dve0, 1)
            for g, w in enumerate(POOL_WINDOWS):
                dve.tensor_scalar(recip16[:, g, :], count_i[:, :], float(w), None, ALU.min).then_inc(s_dve0, 1)
            dve.wait_ge(s_dve0, 1 + BT)
            dve.reciprocal(recip16[:, :, :], recip16[:, :, :]).then_inc(s_dve0, 1)
            dve.memset(rstd_t[:, :], 1.0)
            for i, s_ in enumerate((gated, y_out, ss_add, z_out)):
                for j in range(2):
                    dve.memset(ss_sum[:, 2 * i + j:2 * i + j + 1], 0.0).then_inc(s_, 1)

            with dve.Fori(0, DEPTH) as l:
                link = Link(l)
                dve.wait_ge(s_gains, 1)
                dve.tensor_copy(gain[:, :], gains[:, bass.ds(l * NGAIN, NGAIN)]).then_inc(s_gain, 1)
                dve.wait_ge(s_gain, 2 * l + 1)
                for s in (0, 2):
                    g = gain[:, G_POST[s]:G_POST[s] + KD]
                    ins = dve.tensor_scalar(g, g, 0.5, None, ALU.mult)
                ins.then_inc(s_gain, 1)
                dve.wait_ge(s_gain, 2 * l + 2)
                q0 = l * SLOT_USES
                pre_norm_ffn(l, 0)
                ffn(l, 0, q0 + Q_FFN1)
                post_norm(l, 0)
                pre_norm(l, 1)

                dve.memset(row_reset[:, :], 1.0)
                dve.memset(gate_q[:, :], 0.0)
                dve.memset(qm[:, :, :], 0.0)
                dve.memset(state[:, :, :], 0.0).then_inc(st_zero, 1)
                dve.memset(s_vt[:, DV:VE], 1.0)
                dve.memset(vt[:, :, DV], 1.0).then_inc(vt_ones, 1)
                link(dve.memset(mprev[:, :], 0.0))
                dve.memset(row_reset[:, 0:SEQ:P], 0.0)
                link(dve.memset(row_reset[:, SEQ:T:DS], 0.0))
                dve.wait_ge(mm[0], l * SLOT_USES + Q_MIX + 2)
                dve.wait_ge(mm[1], l * SLOT_USES + Q_MIX + 2)
                dve.wait_ge(s_bias, 32 * (l + 1))
                dve.tensor_scalar(halves(row_i[:, :]), pair(0)[0:HEADS], i_bias, None, ALU.add)
                dve.tensor_scalar(halves(row_f[:, :]), pair(1)[0:HEADS], f_bias, None, ALU.add).then_inc(row_in, 1)
                dve.wait_ge(row_sp, l + 1)
                link(dve.scalar_tensor_tensor(out=row_lf[:, :], in0=row_f[:, :], scalar=0.0, in1=row_softplus[:, :],
                                              op0=ALU.min, op1=ALU.subtract))
                link(dve.tensor_tensor_scan(row_b[:, :], row_reset[:, :], row_lf[:, :], 0.0, ALU.mult, ALU.add))
                dve.tensor_tensor(gate_q[0:HEADS, :], row_i[:, :], row_b[:, :], ALU.subtract)
                dve.tensor_copy(row_lf2[:, :], row_lf[:, :])
                dve.tensor_copy(row_i2[:, :], row_i[:, :])
                dve.wait_ge(s_m0, 16 * (l + 1))
                link(dve.tensor_tensor(m0t[:, :], row_lf[:, SEQ:T:DS], m0[:, :], ALU.add))
                dve.tensor_tensor(row_i2[:, SEQ:T:DS], row_i[:, SEQ:T:DS], m0t[:, :], ALU.max)
                link(dve.memset(row_lf2[:, SEQ:T:DS], NEG))
                link(dve.tensor_tensor_scan(row_m[:, :], row_lf2[:, :], row_i2[:, :], 0.0, ALU.add, ALU.max))
                dve.tensor_copy(mprev[:, 1:NC], row_m[:, P - 1:SEQ - 1:P])
                dve.tensor_copy(mprev[:, NC:NC + DB], m0[:, :])
                link(dve.tensor_tensor(row_bm[:, :], row_b[:, :], row_m[:, :], ALU.subtract))
                dve.tensor_tensor(dlast[:, 0:NC], row_bm[:, P - 1:SEQ:P], mprev[:, 0:NC], ALU.add)
                dve.tensor_tensor(dlast[:, NC:NC + DB], row_bm[:, SEQ + DS - 1:T:DS], mprev[:, NC:NC + DB],
                                  ALU.add).then_inc(row_decay, 1)
                pv = lambda t_, r0=0: t_[r0:r0 + HEADS, 0:SEQ].rearrange("h (c n) -> h c n", n=P)
                sv = lambda t_, r0=0: t_[r0:r0 + HEADS, SEQ:T].rearrange("h (b n) -> h b n", n=DS)
                bp = lambda t_: t_.unsqueeze(2).broadcast_to([HEADS, NC, P])
                bs = lambda t_: t_.unsqueeze(2).broadcast_to([HEADS, DB, DS])
                dve.tensor_tensor(pv(gate_q, 32), pv(row_bm), bp(mprev[:, 0:NC]), ALU.add)
                dve.tensor_tensor(sv(gate_q, 32), sv(row_bm), bs(mprev[:, NC:NC + DB]), ALU.add)
                dve.tensor_scalar(gate_q[64:64 + HEADS, :], row_m[:, :], -1.0, None, ALU.mult)
                dve.tensor_tensor(pv(gate_q, 96), pv(gate_q), bp(row_bm[:, P - 1:SEQ:P]), ALU.add)
                dve.tensor_tensor(sv(gate_q, 96), sv(gate_q), bs(row_bm[:, SEQ + DS - 1:T:DS]), ALU.add).then_inc(row_done, 1)
                dve.wait_ge(decay_ps, l + 1)
                dve.tensor_copy(decay[:, :, :], ps[:, 6, 0:HEADS * (NC + DB)].rearrange("p (h c) -> p h c", h=HEADS))\
                    .then_inc(decay_sb, 1)

                dve.wait_ge(n0_ps, l + 1)
                dve.tensor_copy(n0T[:, :, :], ps[:, 2, 0:HEADS * DB].rearrange("p (h b) -> p h b", h=HEADS))
                link(dve.tensor_copy(decay8[:, :], ps[0:DB, 3, 0:HEADS]))
                n3 = n0[:, :].rearrange("b (h k) -> b h k", h=HEADS)
                dve.tensor_tensor(n3, n3, decay8[:, :].unsqueeze(2).broadcast_to([DB, HEADS, DK]), ALU.mult)\
                    .then_inc(n0_sb, 1)

                def head_norm(num_, sum_ready, ss, den_, rec, var, floor, var_s, std_s, count, out_s):
                    den = num_[:, :, DV]
                    n, heads = den.shape
                    link(dve.scalar_tensor_tensor(out=den_, in0=den, scalar=-1.0, in1=den, op0=ALU.mult, op1=ALU.max))
                    link(dve.tensor_tensor(den_, den_, floor, ALU.max))
                    link(dve.reciprocal(rec, den_))
                    dve.wait_ge(sum_ready, count)
                    link(dve.tensor_tensor(var, ss, rec, ALU.mult))
                    link(dve.tensor_tensor(var, var, rec, ALU.mult))
                    dve.tensor_scalar(var, var, 1.0 / DV, EPS, ALU.mult, ALU.add).then_inc(var_s, 1)
                    dve.wait_ge(std_s, count)
                    link(dve.reciprocal(var, var))
                    link(dve.tensor_tensor(var, var, rec, ALU.mult))
                    dve.tensor_tensor(num_[:, :, 0:DV], num_[:, :, 0:DV],
                                      var.unsqueeze(2).broadcast_to([n, heads, DV]), ALU.mult).then_inc(out_s, 1)

                s_inter = tok_exp[0:NS, NC, 0:HEADS]
                s_win = tok_exp[0:NS, NC, 64:64 + HEADS]
                for ch in range(NC):
                    h = ch
                    t0, n = ch * P, P
                    cc = l * NC + ch
                    hs = l * HEADS + h
                    inter, w_in = tok_exp[:, ch, 0:HEADS], tok_exp[:, ch, 64:64 + HEADS]
                    dve.wait_ge(s_in_ps, hs + 1)
                    if ch == 0:
                        dve.wait_ge(tok_sb, l + 1)
                    link(dve.scalar_tensor_tensor(out=s_kw[:, :], in0=ps[0:NS, 3, 0:DK], scalar=QK_SCALE,
                                                  in1=s_win[:, h:h + 1].broadcast_to([NS, DK]), op0=ALU.mult, op1=ALU.mult))
                    dve.tensor_tensor(kwm[:, :, :], s_kw[:, :].unsqueeze(1).broadcast_to([NS, DB, DK]),
                                      block01[:, :].unsqueeze(2).broadcast_to([NS, DB, DK]), ALU.mult)
                    qsrc = z[:, Z_Q + h, SEQ:T].rearrange("p (b t) -> p b t", b=DB)
                    for b in range(DB):
                        dve.tensor_copy(qm[:, b, b * DS:(b + 1) * DS], qsrc[:, b, :])
                    dve.wait_ge(s_act, hs + 1)
                    dve.scalar_tensor_tensor(out=s_wt[:, :], in0=ps[0:NS, 3, DK:DK + NS], scalar=QK_SCALE, in1=s_dt[:, :],
                                             op0=ALU.mult, op1=ALU.mult).then_inc(s_dve, 1)
                    dve.wait_ge(vk_ps, cc + 1)
                    dve.scalar_tensor_tensor(out=kw[:, :, :], in0=ps[:, 6, :].rearrange("p (h k) -> p h k", h=HEADS),
                                             scalar=QK_SCALE, in1=w_in.unsqueeze(2).broadcast_to([n, HEADS, DK]),
                                             op0=ALU.mult, op1=ALU.mult).then_inc(kw_sb, 1)

                    def c0_decay(vh):
                        dve.wait_ge(c0T_ps, hs * VH + vh + 1)
                        cv = c0[:, vh, :, :]
                        return dve.tensor_tensor(cv, cv, decay[:, h, NC:NC + DB].unsqueeze(2).broadcast_to([P, DB, DK]),
                                                 ALU.mult)

                    c0_decay(0)
                    dve.wait_ge(qk_ps, cc + 1)
                    dve.wait_ge(dt_sb, cc + 1)
                    dve.scalar_tensor_tensor(out=wt[:, :, :], in0=ps[:, 4, :].rearrange("p (h t) -> p h t", h=HEADS),
                                             scalar=QK_SCALE, in1=dt_[:, :, :], op0=ALU.mult, op1=ALU.mult).then_inc(wt_sb, 1)
                    link(c0_decay(1))

                    def two_heads(r):
                        dve.wait_ge(num_ps, l * 2 * NC + 2 * ch + r + 1)
                        hr = slice(2 * r, 2 * r + 2)
                        link(dve.tensor_tensor(num[:, hr, :], ps[:, 6:8, 0:VE],
                                               inter[:, hr].unsqueeze(2).broadcast_to([n, 2, VE]), ALU.mult))
                        dve.tensor_tensor(num[:, hr, :], num[:, hr, :], ps[:, 4:6, 0:VE], ALU.add).then_inc(num_sb, 1)

                    two_heads(0)
                    dve.wait_ge(s_num_ps, hs + 1)
                    link(dve.tensor_scalar(s_num[:, :], ps[0:NS, 3, 0:VE], s_inter[:, h:h + 1], None, ALU.mult))
                    dve.wait_ge(n0_sb, l + 1)
                    dve.tensor_tensor(n0[:, h * DK:(h + 1) * DK], n0[:, h * DK:(h + 1) * DK], ps[0:DB, 2, 384:384 + DK],
                                      ALU.add)
                    dve.tensor_tensor(s_num[:, :], s_num[:, :], ps[0:NS, 2, 0:VE], ALU.add).then_inc(s_num_sb, 1)
                    two_heads(1)
                    dve.wait_ge(s_num_sb, hs + 1)
                    head_norm(s_num[:, :].unsqueeze(1), s_ss_s, s_ss[:, :], s_den[:, :], s_rec[:, :], s_var[:, :],
                              tok_exp[0:NS, NC, 32 + h:33 + h], s_var_s, s_std_s, hs + 1, s_h)
                    dve.wait_ge(num_sb, l * 2 * NC + 2 * ch + 2)
                    head_norm(num[:, :, :], hss_s, hss[:, :], hden[:, :], hrec[:, :], hvar[:, :],
                              tok_exp[:, ch, 32:32 + HEADS], hvar_s, hstd_s, cc + 1, hc_sb)

                    def c0_add(vh):
                        dve.wait_ge(cu_ps, hs * VH + vh + 1)
                        cv = c0[:, vh, :, :]
                        dve.tensor_tensor(cv, cv, ps[:, 2:4, :].rearrange("p b (c k) -> p (b c) k", k=DK),
                                          ALU.add).then_inc(cu_sb, 1)

                    c0_add(0)
                    dve.wait_ge(st_ps, l * NC + ch + 1)
                    link(dve.tensor_tensor(state[:, :, :], state[:, :, :],
                                           decay[:, :, ch:ch + 1].broadcast_to([P, HEADS, VE]), ALU.mult))
                    dve.tensor_tensor(state[:, :, :], state[:, :, :], ps[:, 4:8, 0:VE], ALU.add).then_inc(st_sb, 1)
                    c0_add(1)

                dve.memset(ln_rstd, 1.0)
                for ch in range(NC + 1):
                    _, n = tokens(ch)
                    dve.wait_ge(av_sb, l * (NC + 1) + ch + 1)
                    link(dve.bn_stats(ln_stats[0:n, ch, :], vn[0:n, ch, :]), True)
                    link(dve.bn_aggr(ln_mv[0:n, ch, :], ln_stats[0:n, ch, :]))
                    ins = dve.tensor_scalar(ln_rstd[0:n, ch:ch + 1], ln_mv[0:n, ch, 1:2], EPS, None, ALU.add)
                ins.then_inc(ln_var, 1)

                def branch_c(t0, t1):
                    for t in range(t0, t1 + 1):
                        if t < t1:
                            g = G_HEAD + t
                            dve.scalar_tensor_tensor(out=z[:, Z_O + t, :], in0=z[:, Z_VAL + t, :], scalar=gain[:, g:g + 1],
                                                     in1=z[:, Z_O + t, :], op0=ALU.mult, op1=ALU.mult).then_inc(c_sb, 1)
                        if t > t0:
                            dve.wait_ge(c_hi_s, l * CT_ + t)
                            dve.tensor_tensor(c_lo[:, t - 1, :], z[:, Z_O + t - 1, :], c_hi[:, t - 1, :].bitcast(F32),
                                              ALU.subtract).then_inc(c_lo_s, 1)

                dve.wait_ge(o_sig, 2 * l + 1)
                dve.wait_ge(ws_ps, l + 1)
                m3 = mask_p[:, :].unsqueeze(1).broadcast_to([P, AT, P])
                dve.scalar_tensor_tensor(out=wsT[:, :, :], in0=m3, scalar=-0.5,
                                         in1=ps[:, 6, :].rearrange("p (g t) -> p g t", g=AT),
                                         op0=ALU.is_ge, op1=ALU.mult).then_inc(wsT_s, 1)
                branch_c(0, CHUNK_O)
                dve.wait_ge(ln_std, l + 1)
                link(dve.reciprocal(ln_rstd, ln_rstd))

                def layer_norm(chunks):
                    for ch in chunks:
                        _, n = tokens(ch)
                        v_ = vn[0:n, ch, :]
                        link(dve.tensor_scalar(v_, v_, ln_mv[0:n, ch, 0:1], ln_rstd[0:n, ch:ch + 1], ALU.subtract, ALU.mult))
                        link(dve.tensor_tensor(v_, v_, ln_gb[0:n, 0, :], ALU.mult))
                        dve.tensor_tensor(v_, v_, ln_gb[0:n, 1, :], ALU.add).then_inc(vn_sb, 1)

                layer_norm(range(3))
                dve.wait_ge(o_sig, 2 * l + 2)
                dve.wait_ge(wss_ps, l + 1)
                for g in range(AT):
                    rep = ps[0:NS, 6, g * DS:(g + 1) * DS].unsqueeze(1).broadcast_to([NS, DB, DS])
                    dve.scalar_tensor_tensor(out=ws_s[:, g, :].rearrange("p (b t) -> p b t", b=DB),
                                             in0=mask_s[:, :].rearrange("p (b t) -> p b t", b=DB), scalar=-0.5, in1=rep,
                                             op0=ALU.is_ge, op1=ALU.mult)
                branch_c(CHUNK_O, CT_)
                layer_norm(range(3, NC + 1))
                dve.wait_ge(u_gelu, l + 1)

                def gate_a(ch):
                    t0, n = tokens(ch)
                    dve.wait_ge(mix_ps, l * (NC + 1) + ch + 1)
                    dst = z[:, Z_U:Z_U + AT, t0:t0 + n]
                    dve.tensor_tensor(dst, dst, ps[:, 4 + ch % 2, 0:AT * n].rearrange("p (g t) -> p g t", g=AT),
                                      ALU.mult).then_inc(a_sb, 1)

                def pool_b(g):
                    w = POOL_WINDOWS[g]
                    gg = l * BT + g
                    dve.wait_ge(seg_sb, gg + 1)
                    src, step, first, bufs = seg, 1, 0, (win_a, win_b)
                    for j in range(g + 1):
                        dst = bufs[j % 2]
                        first += step
                        link(dve.tensor_tensor(dst[:, first:WID], src[:, first:WID], src[:, first - step:WID - step], ALU.add))
                        src, step = dst, 2 * step
                    if g:
                        dve.wait_ge(pmix_ps, gg)
                    dve.scalar_tensor_tensor(out=pooled[:, 16:SEQ], in0=src[:, BUF + 16:BUF + SEQ], scalar=1.0 / w,
                                             in1=seg[:, BUF + 16:BUF + SEQ], op0=ALU.mult, op1=ALU.subtract)
                    sview = lambda t_: t_[:, BUF + SEQ:WID].rearrange("p (b r) -> p b r", b=DB)[:, :, BUF:BUF + DS]
                    dve.scalar_tensor_tensor(out=pooled[:, SEQ:T].rearrange("p (b t) -> p b t", b=DB), in0=sview(src),
                                             scalar=1.0 / w, in1=sview(seg), op0=ALU.mult, op1=ALU.subtract)
                    link(dve.tensor_tensor(pooled[:, 0:16], src[:, BUF:BUF + 16], recip16[:, g, :], ALU.mult))
                    ins = dve.tensor_tensor(pooled[:, 0:16], pooled[:, 0:16], seg[:, BUF:BUF + 16], ALU.subtract)
                    ins.then_inc(pooled_s, 1)

                def scale_b(g):
                    dve.wait_ge(pmix_ps, l * BT + g + 1)
                    dve.tensor_scalar(halves(z[:, Z_B + g, :]), pair(3), gain[:, G_POOL + g:G_POOL + g + 1], None,
                                      ALU.mult).then_inc(b_sb, 1)

                gate_a(0)
                gate_a(1)
                for m in range(KD):
                    if m == 1:
                        gate_a(4)
                        for vh in range(VH):
                            dve.wait_ge(c0_done[vh], 16 * HEADS * (l + 1))
                        link(dve.memset(seg[:, 0:BUF], 0.0))
                        pool_b(0)
                    if 2 <= m < 2 + BT:
                        scale_b(m - 2)
                        if m < 1 + BT:
                            pool_b(m - 1)
                    dve.wait_ge(sig_s, l * 3 * KD + m + 1)
                    dve.wait_ge(mm[1], l * SLOT_USES + Q_GATE + m + 2)
                    dve.tensor_tensor(halves(z[:, Z_O + m, :]), halves(gate_act[m % 2][:, :]), pair(1), ALU.mult)\
                        .then_inc(gated, 1)
                    if m == 0:
                        gate_a(2)
                        gate_a(3)
                    if m == KD - 2:
                        dve.wait_ge(a_hi_s, l + 1)
                        dve.tensor_tensor(a_lo[:, :, :], z[:, Z_U:Z_U + AT, :], a_hi[:, :, :].bitcast(F32), ALU.subtract)\
                            .then_inc(a_lo_s, 1)
                        dve.wait_ge(a_lo_s, l + 1)
                        dve.wait_ge(b_hi_s, l + 1)
                        dve.tensor_tensor(b_lo[:, :, :], z[:, Z_B:Z_B + BT, :], b_hi[:, :, :].bitcast(F32), ALU.subtract)\
                            .then_inc(b_lo_s, 1)

                for half, m_lo in enumerate((merged_lo0, merged_lo1)):
                    apart(dve)
                    with dve.Fori(0, 2) as i:
                        for m2 in range(2):
                            m = 4 * half + 2 * i + m2
                            for br in range(2):
                                n = 2 * m2 + br
                                dve.wait_ge(sig_s, l * 3 * KD + KD + 8 * half + 4 * i + n + 1)
                                dst = prod[m2] if br else sq[m2]
                                dve.tensor_tensor(halves(dst[:, :]), halves(gate_act[n % 2][:, :]), pair(2 * (n % 2) + 1),
                                                  ALU.mult).then_inc(gated, 1)
                                dve.wait_ge(gated, l * PAIRS + G_MIX + KD + 8 * half + 4 * i + n + 3)
                                if br == 0:
                                    c_m = z[:, bass.ds(Z_O + m, 1), :].rearrange("p a n -> p (a n)")
                                    dve.tensor_tensor(sq[m2][:, :], sq[m2][:, :], c_m, ALU.add).then_inc(merge1, 1)
                                else:
                                    dve.wait_ge(merge1, l * KD + m + 1)
                                    dve.tensor_tensor(sq[m2][:, :], sq[m2][:, :], prod[m2][:, :], ALU.add).then_inc(merged_s, 1)
                            dve.wait_ge(merged_hi_s, l * KD + m + 1)
                            hi_t = merged_hi[:, bass.ds(m, 1), :].bitcast(F32)
                            dve.tensor_tensor(m_lo[:, bass.ds(2 * i + m2, 1), :].rearrange("p a n -> p (a n)"),
                                              sq[m2][:, :], hi_t.rearrange("p a n -> p (a n)"), ALU.subtract)\
                                .then_inc(merged_lo_s, 1)
                out_tiles(l, 1)
                post_norm(l, 1)
                pre_norm_ffn(l, 2)
                ffn(l, 1, q0 + Q_FFN2)
                post_norm(l, 2)
                assert link.n == DVE_STEPS, link.n

            for ch in range(NC + 1):
                _, n = tokens(ch)
                dve.wait_ge(xo_ps, ch + 1)
                dve.tensor_copy(x_in[0:n, ch, D // 2:D], ps[0:n, 2 * Y_PAIR[ch] + 1, :]).then_inc(xo_sb_d, 1)


def kernel(**inputs):
    import numpy as _np
    import concourse.bacc as _bacc
    from concourse import mybir as _mybir
    from concourse.bass_utils import run_bass_kernel_spmd as _run

    nc = _bacc.Bacc("TRN2", target_bir_lowering=False, num_devices=1)
    arrays, args = {}, {}
    for name, value in inputs.items():
        v = _np.ascontiguousarray(value)
        arrays[f"in_{name}"] = v
        args[name] = nc.dram_tensor(f"in_{name}", v.shape, _mybir.dt.from_np(v.dtype), kind="ExternalInput").ap()
    x_p, x_s, pool, c, n, m = (inputs[k].shape for k in (
        "x_prompt", "x_sample", "state_pool", "state_mlstm_C", "state_mlstm_n", "state_mlstm_m"))
    a_width = inputs["gmlp_ln_g"].shape[1]
    depth = c[0]
    shapes = {
        "y_prompt": x_p, "y_sample": x_s,
        "pool_prompt": (depth, 1, *pool[2:]), "C_prompt": (depth, 1, *c[2:]), "n_prompt": (depth, 1, *n[2:]),
        "m_prompt": (depth, 1, *m[2:]),
        "pool_sample": pool, "C_sample": c, "n_sample": n, "m_sample": m,
        "gmlp_v_sample": (depth, *x_s[:2], a_width),
    }
    outs = {k: nc.dram_tensor(f"out_{k}", s, _mybir.dt.float32, kind="ExternalOutput").ap() for k, s in shapes.items()}
    trunk_program(nc, args, outs)
    r = _run(nc, [arrays], core_ids=[0])
    return tuple(r.results[0][f"out_{k}"] for k in shapes)
```
